# Optimizing a Trainium2 kernel written in Bass

```python
import math
import jax
import jax.numpy as jnp
from jax import lax
import numpy as np
import jax, jax.numpy as jnp

D_MODEL = 2048
BATCH = 1
SEQ = 256
DEPTH = 1

D_MIX = D_MODEL
D_POOL = D_MIX // 2
POOL_WINDOWS = (2, 4, 8, 16)
N_POOL_GROUPS = len(POOL_WINDOWS)
POOL_GROUP = D_POOL // N_POOL_GROUPS
D_ATTN = D_MIX - D_POOL
HEAD_DIM = 128
N_HEADS = D_ATTN // HEAD_DIM
IDX_HEADS = 16
IDX_DIM = 64
TOPK_MAX = 256
Q_BLOCK = 128
D_FF = 5632
CONV_WIDTH = 3
EPS = 1e-6

D_IN = D_POOL + 3 * D_ATTN + IDX_HEADS * IDX_DIM + IDX_DIM + IDX_HEADS


def rmsnorm(x, g):
    xf = x.astype(jnp.float32)
    y = xf * lax.rsqrt(jnp.mean(xf * xf, axis=-1, keepdims=True) + EPS)
    return (y * g.astype(jnp.float32)).astype(x.dtype)

def pool_mixer(u, pool_w, pool_scale):
    B, S, C = u.shape
    uf = u.astype(jnp.float32)
    csum = jnp.concatenate([jnp.zeros((B, 1, C), jnp.float32), jnp.cumsum(uf, axis=1)], axis=1)
    t = jnp.arange(S)
    outs = []
    for gi, w in enumerate(POOL_WINDOWS):
        lo = jnp.maximum(t + 1 - w, 0)
        cnt = (t + 1 - lo).astype(jnp.float32)[None, :, None]
        c_g = csum[:, :, gi * POOL_GROUP:(gi + 1) * POOL_GROUP]
        mean = (c_g[:, 1:] - c_g[:, lo]) / cnt
        outs.append(mean - uf[:, :, gi * POOL_GROUP:(gi + 1) * POOL_GROUP])
    d = jnp.stack(outs, axis=2).astype(u.dtype)
    y = jnp.einsum('bsgc,gcd->bsgd', d, pool_w).reshape(B, S, C)
    return y * pool_scale

def dsa_attention(q, k, v, q_idx, k_idx, w_idx):
    B, S, H, Dh = q.shape
    topk = min(TOPK_MAX, S // 4)
    n_blocks = S // Q_BLOCK
    key_pos = jnp.arange(S)
    scale = Dh ** -0.5
    neg = jnp.finfo(jnp.float32).min

    def one_block(blk):
        start = blk * Q_BLOCK
        qb = lax.dynamic_slice_in_dim(q, start, Q_BLOCK, axis=1)
        qib = lax.dynamic_slice_in_dim(q_idx, start, Q_BLOCK, axis=1)
        wb = lax.dynamic_slice_in_dim(w_idx, start, Q_BLOCK, axis=1)
        q_pos = start + jnp.arange(Q_BLOCK)
        rel = jax.nn.relu(jnp.einsum('bthd,bsd->bths', qib.astype(jnp.float32), k_idx.astype(jnp.float32)))
        iscore = jnp.einsum('bths,bth->bts', rel, wb.astype(jnp.float32))
        causal = key_pos[None, :] <= q_pos[:, None]
        iscore = jnp.where(causal[None], iscore, neg)
        _, sel = lax.top_k(iscore, topk)
        valid = sel <= q_pos[None, :, None]
        k_sel = jax.vmap(lambda kb, ib: kb[ib])(k, sel)
        v_sel = jax.vmap(lambda vb, ib: vb[ib])(v, sel)
        s = jnp.einsum('bthd,btjhd->bhtj', qb, k_sel).astype(jnp.float32) * scale
        s = jnp.where(valid[:, None], s, neg)
        p = jax.nn.softmax(s, axis=-1).astype(v.dtype)
        return jnp.einsum('bhtj,btjhd->bthd', p, v_sel)

    out = lax.map(one_block, jnp.arange(n_blocks, dtype=jnp.int32))
    return jnp.transpose(out, (1, 0, 2, 3, 4)).reshape(B, S, H * Dh)

def conv_ffn(h, w_up, conv_w, conv_b, w_down):
    B, S, _ = h.shape
    up = h @ w_up
    up_p = jnp.pad(up, ((0, 0), (CONV_WIDTH - 1, 0), (0, 0)))
    c = conv_b + sum(conv_w[j] * up_p[:, j:j + S] for j in range(CONV_WIDTH))
    gate, val = jnp.split(c, 2, axis=-1)
    return (jax.nn.silu(gate) * val) @ w_down

def first_inputs(seed: int = 0) -> dict:
    key = jax.random.key(seed)
    ks = jax.random.split(key, 14)
    f32 = jnp.float32
    nrm = lambda k, shape, s: jax.random.normal(k, shape, f32) * s
    return {
        "x": nrm(ks[0], (BATCH, SEQ, D_MODEL), 1.0),
        "attn_norm_g": 1.0 + nrm(ks[1], (D_MODEL,), 0.02),
        "w_in": nrm(ks[2], (D_MODEL, D_IN), D_MODEL ** -0.5),
        "pool_w": nrm(ks[3], (N_POOL_GROUPS, POOL_GROUP, POOL_GROUP), POOL_GROUP ** -0.5),
        "pool_scale": 1.0 + nrm(ks[4], (D_POOL,), 0.02),
        "q_norm_g": 1.0 + nrm(ks[5], (HEAD_DIM,), 0.02),
        "k_norm_g": 1.0 + nrm(ks[6], (HEAD_DIM,), 0.02),
        "w_out": nrm(ks[7], (D_MIX, D_MODEL), D_MIX ** -0.5),
        "ffn_norm_g": 1.0 + nrm(ks[8], (D_MODEL,), 0.02),
        "w_up": nrm(ks[9], (D_MODEL, 2 * D_FF), D_MODEL ** -0.5),
        "conv_w": nrm(ks[10], (CONV_WIDTH, 2 * D_FF), CONV_WIDTH ** -0.5),
        "conv_b": nrm(ks[11], (2 * D_FF,), 0.01),
        "w_down": nrm(ks[12], (D_FF, D_MODEL), D_FF ** -0.5),
    }

def first_block(x, attn_norm_g, w_in, pool_w, pool_scale, q_norm_g, k_norm_g, w_out,
              ffn_norm_g, w_up, conv_w, conv_b, w_down):
    B, S, _ = x.shape
    for _layer in range(DEPTH):
        h = rmsnorm(x, attn_norm_g)
        z = h @ w_in
        o = 0
        u_pool = z[..., o:o + D_POOL]; o += D_POOL
        q = z[..., o:o + D_ATTN].reshape(B, S, N_HEADS, HEAD_DIM); o += D_ATTN
        k = z[..., o:o + D_ATTN].reshape(B, S, N_HEADS, HEAD_DIM); o += D_ATTN
        v = z[..., o:o + D_ATTN].reshape(B, S, N_HEADS, HEAD_DIM); o += D_ATTN
        q_idx = z[..., o:o + IDX_HEADS * IDX_DIM].reshape(B, S, IDX_HEADS, IDX_DIM); o += IDX_HEADS * IDX_DIM
        k_idx = z[..., o:o + IDX_DIM]; o += IDX_DIM
        w_idx = z[..., o:o + IDX_HEADS] * (IDX_HEADS ** -0.5) * (IDX_DIM ** -0.5)
        q = rmsnorm(q, q_norm_g)
        k = rmsnorm(k, k_norm_g)
        y_pool = pool_mixer(u_pool, pool_w, pool_scale)
        y_attn = dsa_attention(q, k, v, q_idx, k_idx, w_idx)
        x = x + jnp.concatenate([y_pool, y_attn], axis=-1) @ w_out
        x = x + conv_ffn(rmsnorm(x, ffn_norm_g), w_up, conv_w, conv_b, w_down)
    return x


DEPTH_2 = 2

N_MIXERS = 2
N_FOX_LAYERS = (DEPTH_2 + 1) // 2
N_RET_LAYERS = DEPTH_2 // 2

FOX_HEAD_DIM = 128
FOX_HEADS = D_MODEL // FOX_HEAD_DIM
FOX_WIDTH = FOX_HEADS * FOX_HEAD_DIM
FOX_BLOCK = 128
FOX_IN_COLS = 4 * FOX_WIDTH + FOX_HEADS

RET_QK_DIM = 256
RET_HEADS = D_MODEL // RET_QK_DIM
RET_V_DIM = 2 * RET_QK_DIM
RET_QK_WIDTH = RET_HEADS * RET_QK_DIM
RET_V_WIDTH = RET_HEADS * RET_V_DIM
RET_CHUNK = 128
RET_IN_COLS = 2 * RET_QK_WIDTH + 2 * RET_V_WIDTH
ROPE_BASE = 10000.0

LN_EPS = 1e-5
GN_EPS = 1e-6
QK_EPS = 1e-6
DEEPNORM_ALPHA = (2.0 * DEPTH_2) ** 0.25
DEEPNORM_BETA = (8.0 * DEPTH_2) ** -0.25


def layer_norm(x, g, b):
    xf = x.astype(jnp.float32)
    mu = jnp.mean(xf, axis=-1, keepdims=True)
    var = jnp.mean(jnp.square(xf - mu), axis=-1, keepdims=True)
    y = (xf - mu) * lax.rsqrt(var + LN_EPS) * g.astype(jnp.float32) + b.astype(jnp.float32)
    return y.astype(x.dtype)

def rms_norm(x, g):
    xf = x.astype(jnp.float32)
    y = xf * lax.rsqrt(jnp.mean(jnp.square(xf), axis=-1, keepdims=True) + QK_EPS) * g.astype(jnp.float32)
    return y.astype(x.dtype)

def group_norm_heads(x):
    mu = jnp.mean(x, axis=-1, keepdims=True)
    var = jnp.mean(jnp.square(x - mu), axis=-1, keepdims=True)
    return (x - mu) * lax.rsqrt(var + GN_EPS)

def rotary(t):
    S, d = t.shape[1], t.shape[-1]
    inv_freq = ROPE_BASE ** (-jnp.arange(0, d, 2, dtype=jnp.float32) / d)
    ang = jnp.arange(S, dtype=jnp.float32)[:, None] * inv_freq[None, :]
    cos = jnp.cos(ang)[None, :, None, :]
    sin = jnp.sin(ang)[None, :, None, :]
    t1, t2 = t[..., : d // 2], t[..., d // 2:]
    return jnp.concatenate([t1 * cos - t2 * sin, t1 * sin + t2 * cos], axis=-1)

def fox_branch(x, w_in, b_f, q_gain, k_gain, w_out):
    B, S, _ = x.shape
    proj = jnp.einsum('bsd,de->bse', x, w_in)
    q, k, v, gate, f_logit = jnp.split(
        proj, [FOX_WIDTH, 2 * FOX_WIDTH, 3 * FOX_WIDTH, 4 * FOX_WIDTH], axis=-1)

    def heads(t):
        return t.reshape(B, S, FOX_HEADS, FOX_HEAD_DIM).transpose(0, 2, 1, 3)

    q = rms_norm(heads(q), q_gain)
    k = rms_norm(heads(k), k_gain)
    v = heads(v)
    log_f = jax.nn.log_sigmoid((f_logit + b_f).astype(jnp.float32))
    c = jnp.cumsum(log_f, axis=1).transpose(0, 2, 1)

    n_blocks = S // FOX_BLOCK
    q_blocks = q.reshape(B, FOX_HEADS, n_blocks, FOX_BLOCK, FOX_HEAD_DIM).transpose(2, 0, 1, 3, 4)
    c_blocks = c.reshape(B, FOX_HEADS, n_blocks, FOX_BLOCK).transpose(2, 0, 1, 3)
    key_pos = jnp.arange(S)
    scale = FOX_HEAD_DIM ** -0.5

    def attend_block(args):
        qb, cb, blk = args
        s = jnp.einsum('bhqd,bhkd->bhqk', qb, k).astype(jnp.float32) * scale
        s = s + cb[..., :, None] - c[..., None, :]
        q_pos = blk * FOX_BLOCK + jnp.arange(FOX_BLOCK)
        s = jnp.where(key_pos[None, :] <= q_pos[:, None], s, -jnp.inf)
        p = jax.nn.softmax(s, axis=-1).astype(v.dtype)
        return jnp.einsum('bhqk,bhkd->bhqd', p, v)

    o = lax.map(attend_block, (q_blocks, c_blocks, jnp.arange(n_blocks)))
    o = o.transpose(1, 0, 3, 2, 4).reshape(B, S, FOX_WIDTH)
    y = o * jax.nn.silu(gate)
    return jnp.einsum('bse,ed->bsd', y, w_out)

def retention_branch(x, w_in, w_out):
    B, S, _ = x.shape
    proj = jnp.einsum('bsd,de->bse', x, w_in)
    q, k, v, gate = jnp.split(
        proj, [RET_QK_WIDTH, 2 * RET_QK_WIDTH, 2 * RET_QK_WIDTH + RET_V_WIDTH], axis=-1)
    q = rotary(q.reshape(B, S, RET_HEADS, RET_QK_DIM).astype(jnp.float32))
    k = rotary(k.reshape(B, S, RET_HEADS, RET_QK_DIM).astype(jnp.float32)) * (RET_QK_DIM ** -0.5)
    v = v.reshape(B, S, RET_HEADS, RET_V_DIM).astype(jnp.float32)

    log_gamma = jnp.log1p(-jnp.exp2(-5.0 - jnp.arange(RET_HEADS, dtype=jnp.float32)))
    pos = jnp.arange(RET_CHUNK, dtype=jnp.float32)
    diff = pos[:, None] - pos[None, :]
    intra_decay = jnp.where(diff >= 0,
                            jnp.exp(jnp.maximum(diff, 0.0)[None] * log_gamma[:, None, None]),
                            0.0)
    query_decay = jnp.exp((pos[None, :] + 1.0) * log_gamma[:, None])
    key_decay = jnp.exp((RET_CHUNK - 1.0 - pos[None, :]) * log_gamma[:, None])
    chunk_decay = jnp.exp(RET_CHUNK * log_gamma)

    n_chunks = S // RET_CHUNK

    def chunks(t):
        return t.reshape(B, n_chunks, RET_CHUNK, RET_HEADS, t.shape[-1]).transpose(1, 0, 3, 2, 4)

    def step(R, inp):
        qc, kc, vc = inp
        inner = jnp.einsum('bhqd,bhkd->bhqk', qc, kc) * intra_decay[None]
        o = (jnp.einsum('bhqk,bhkv->bhqv', inner, vc)
             + jnp.einsum('bhqd,bhdv->bhqv', qc, R) * query_decay[None, :, :, None])
        R = (R * chunk_decay[None, :, None, None]
             + jnp.einsum('bhkd,bhkv->bhdv', kc * key_decay[None, :, :, None], vc))
        return R, o

    R0 = jnp.zeros((B, RET_HEADS, RET_QK_DIM, RET_V_DIM), jnp.float32)
    _, o = lax.scan(step, R0, (chunks(q), chunks(k), chunks(v)))
    o = o.transpose(1, 0, 3, 2, 4)
    o = group_norm_heads(o).reshape(B, S, RET_V_WIDTH).astype(gate.dtype)
    y = o * jax.nn.silu(gate)
    return jnp.einsum('bse,ed->bsd', y, w_out)

def second_inputs(seed: int = 0) -> dict:
    key = jax.random.key(seed)
    ks = jax.random.split(key, 10)
    std_in = D_MODEL ** -0.5
    fox_col_scale = jnp.ones((FOX_IN_COLS,), jnp.float32).at[2 * FOX_WIDTH:3 * FOX_WIDTH].set(DEEPNORM_BETA)
    ret_col_scale = jnp.ones((RET_IN_COLS,), jnp.float32).at[
        2 * RET_QK_WIDTH:2 * RET_QK_WIDTH + RET_V_WIDTH].set(DEEPNORM_BETA)
    x = jax.random.normal(ks[0], (BATCH, SEQ, D_MODEL), jnp.float32)
    fox_w_in = jax.random.normal(ks[1], (N_FOX_LAYERS, D_MODEL, FOX_IN_COLS), jnp.float32) * std_in * fox_col_scale
    fox_b_f = 3.0 + 0.5 * jax.random.normal(ks[2], (N_FOX_LAYERS, FOX_HEADS), jnp.float32)
    fox_q_gain = 1.0 + 0.02 * jax.random.normal(ks[3], (N_FOX_LAYERS, FOX_HEAD_DIM), jnp.float32)
    fox_k_gain = 1.0 + 0.02 * jax.random.normal(ks[4], (N_FOX_LAYERS, FOX_HEAD_DIM), jnp.float32)
    fox_w_out = (jax.random.normal(ks[5], (N_FOX_LAYERS, FOX_WIDTH, D_MODEL), jnp.float32)
                 * (FOX_WIDTH ** -0.5) * DEEPNORM_BETA)
    ret_w_in = jax.random.normal(ks[6], (N_RET_LAYERS, D_MODEL, RET_IN_COLS), jnp.float32) * std_in * ret_col_scale
    ret_w_out = (jax.random.normal(ks[7], (N_RET_LAYERS, RET_V_WIDTH, D_MODEL), jnp.float32)
                 * (RET_V_WIDTH ** -0.5) * DEEPNORM_BETA)
    ln_gain = 1.0 + 0.02 * jax.random.normal(ks[8], (DEPTH_2, D_MODEL), jnp.float32)
    ln_bias = 0.02 * jax.random.normal(ks[9], (DEPTH_2, D_MODEL), jnp.float32)
    return {"x": x, "fox_w_in": fox_w_in, "fox_b_f": fox_b_f, "fox_q_gain": fox_q_gain,
            "fox_k_gain": fox_k_gain, "fox_w_out": fox_w_out, "ret_w_in": ret_w_in,
            "ret_w_out": ret_w_out, "ln_gain": ln_gain, "ln_bias": ln_bias}

def second_block(x, fox_w_in, fox_b_f, fox_q_gain, fox_k_gain, fox_w_out, ret_w_in, ret_w_out,
              ln_gain, ln_bias):
    h = x
    for i in range(DEPTH_2):
        j = i // N_MIXERS
        if i % N_MIXERS == 0:
            y = fox_branch(h, fox_w_in[j], fox_b_f[j], fox_q_gain[j], fox_k_gain[j], fox_w_out[j])
        else:
            y = retention_branch(h, ret_w_in[j], ret_w_out[j])
        h = layer_norm(DEEPNORM_ALPHA * h + y, ln_gain[i], ln_bias[i])
    return h


def setup_inputs(seed=0):
    out = dict(first_inputs(seed))
    for name, value in second_inputs(seed + 1).items():
        if name != "x":
            out[name + "_2"] = value
    return out


def reference(
    x, attn_norm_g, w_in, pool_w, pool_scale, q_norm_g, k_norm_g, w_out, ffn_norm_g, w_up,
    conv_w, conv_b, w_down, fox_w_in_2, fox_b_f_2, fox_q_gain_2, fox_k_gain_2, fox_w_out_2,
    ret_w_in_2, ret_w_out_2, ln_gain_2, ln_bias_2,
):
    x = first_block(
        x, attn_norm_g, w_in, pool_w, pool_scale, q_norm_g, k_norm_g, w_out, ffn_norm_g, w_up,
        conv_w, conv_b, w_down,
    )
    return second_block(
        x, fox_w_in_2, fox_b_f_2, fox_q_gain_2, fox_k_gain_2, fox_w_out_2, ret_w_in_2,
        ret_w_out_2, ln_gain_2, ln_bias_2,
    )


_drawn_inputs = setup_inputs


def setup_inputs(seed=0):
    import zlib

    import numpy as np

    out = dict(_drawn_inputs(seed))
    spreads = {}
    factors = {'pool_scale': 4.675,
     'q_norm_g': 8.0,
     'k_norm_g': 8.0,
     'ffn_norm_g': 4.061,
     'conv_b': 8.0,
     'fox_b_f_2': 3.858,
     'fox_q_gain_2': 8.0,
     'fox_k_gain_2': 8.0}
    for name, (base, spread) in spreads.items():
        noise = np.random.default_rng([zlib.crc32(name.encode()), seed]).standard_normal(out[name].shape)
        drawn = base * np.exp(spread * noise) if base else spread * noise
        out[name] = jnp.asarray(drawn.astype(out[name].dtype))
    for name, factor in factors.items():
        out[name] = (out[name] * factor).astype(out[name].dtype)
    return out
```

```python
import numpy as np
import concourse.bass as bass
from concourse import mybir
from contextlib import ExitStack

F32 = mybir.dt.float32
F32R = mybir.dt.float32r
ALU = mybir.AluOpType
ACT = mybir.ActivationFunctionType
AX = mybir.AxisListType.X

P = 128
S = 256
TOK = S // P
D = 2048
KT = D // P
COL = 512
KC = 2
CH = KT // KC
NOUT = D // COL
HD = 128
EPS = 1e-6
LN_EPS = 1e-5
GN_EPS = 1e-6
NEG = -1e30
TAKEN = -3e38

D_POOL = 1024
POOL_W = (2, 4, 8, 16)
IDX_HEADS, IDX_DIM = 16, 64
TOPK = 64
ATT_HEADS = 8
D_IN = 5200
C_Q, C_K, C_V, C_QI, C_KI = 1024, 2048, 3072, 4096, 5120
NARROW = IDX_DIM + IDX_HEADS
NARROW_K = 8
D_FF = 5632
PAIRS = D_FF // COL
FOX_HEADS = 16
GROUP = 4
FOX_GROUPS = FOX_HEADS // GROUP
RET_HEADS, RET_QK, RET_V = 8, 256, 512
RET_PAIR = 2
RET_GROUPS = RET_HEADS // RET_PAIR
ALPHA = (2.0 * 2) ** 0.25

RAW = 4
SPLIT = 4
LEAD = SPLIT - 1

L1_CHUNKS = 16 + 2 + 16 + 24 + 16 + 24 + 8 + 8
L1_BLOCKS = 2 + 1 + 2 + 3 + 8 + 3 + 4 + 4
FFN_IN, FFN_OUT = 2 * CH, NOUT * 2
FOX_IN, FOX_OUT = 4 * CH, NOUT * 2
RET_IN, RET_OUT = 6 * CH, NOUT * 4
FFN_0 = L1_CHUNKS
FOX_0 = FFN_0 + PAIRS * (FFN_IN + FFN_OUT)
RET_0 = FOX_0 + 1 + FOX_GROUPS * (FOX_IN + FOX_OUT)
TOTAL = RET_0 + RET_GROUPS * (RET_IN + RET_OUT)
FFN_B = L1_BLOCKS
FOX_B = FFN_B + PAIRS * 6
RET_B = FOX_B + 1 + FOX_GROUPS * 8


class Count:

    def __init__(self, base, per=0, i=None):
        self.base, self.per, self.i = base, per, i

    def at(self, k=0, times=1):
        v = (self.base + k) * times
        return v if self.i is None else self.i * (self.per * times) + v

    def plus(self, k):
        return Count(self.base + k, self.per, self.i)

    def over(self, n):
        return Count(self.base // n, self.per // n, self.i)

    def some(self):
        return self.i is not None or self.base > 0


def constants():
    s = np.arange(P)[:, None]
    t = np.arange(P)[None, :]
    tri = (s <= t).astype(np.float32)
    pen = np.zeros((P, 3 * P), np.float32)
    upper = np.where(np.arange(P)[None, :] <= np.arange(P)[:, None], 0.0, NEG).astype(np.float32)
    pen[:, 0:P] = upper
    pen[:, 2 * P:3 * P] = upper
    pool = np.zeros((len(POOL_W), S, S), np.float32)
    for g, w in enumerate(POOL_W):
        for q in range(S):
            lo = max(q + 1 - w, 0)
            pool[g, lo:q + 1, q] = 1.0 / (q + 1 - lo)
            pool[g, q, q] -= 1.0
    packed = np.concatenate([pool[:, 0:P, :], pool[:, P:S, P:S]], axis=2).transpose(1, 0, 2)
    inv = 10000.0 ** (-np.arange(0, RET_QK, 2, dtype=np.float32) / RET_QK)
    ang = (np.arange(S, dtype=np.float32)[:, None] * inv.astype(np.float32)[None, :]).astype(np.float32)
    rot = np.stack([np.cos(ang), np.sin(ang)]).astype(np.float32)
    rot = rot.reshape(2, TOK, P, P).transpose(2, 0, 1, 3)
    lg = np.log1p(-np.exp2(-5.0 - np.arange(RET_HEADS, dtype=np.float64)))
    diff = (np.arange(S)[None, :] - np.arange(S)[:, None]).astype(np.float64)
    dec = np.where(diff >= 0, np.exp(np.maximum(diff, 0)[None] * lg[:, None, None]), 0.0) * RET_QK ** -0.5
    dec = np.concatenate([dec[:, 0:P, :], dec[:, P:S, P:S]], axis=2).transpose(1, 0, 2)
    return {
        "ident": np.eye(P, dtype=np.float32),
        "causal": pen,
        "upto": np.concatenate([tri, np.ones((P, P), np.float32)], axis=1),
        "poolband": np.ascontiguousarray(packed.reshape(P, -1), dtype=np.float32),
        "rotary": np.ascontiguousarray(rot.reshape(P, -1), dtype=np.float32),
        "decay": np.ascontiguousarray(dec.reshape(P, -1), dtype=np.float32),
    }


def mixers_kernel(nc, x, attn_norm_g, w_in, pool_w, pool_scale, q_norm_g, k_norm_g, w_out,
                  ffn_norm_g, w_up, conv_w, conv_b, w_down, fox_w_in, fox_b_f, fox_q_gain,
                  fox_k_gain, fox_w_out, ret_w_in, ret_w_out, ln_gain, ln_bias,
                  ident_d, causal_d, upto_d, poolband_d, rotary_d, decay_d, out):
    ctx = ExitStack()
    with ctx:
        def sb(name, shape, dt=F32):
            return ctx.enter_context(nc.sbuf_tensor(name, shape, dt))

        def sem(name):
            return ctx.enter_context(nc.semaphore(name))

        raw = sb("raw", [P, RAW, KC * COL])
        w_hi = sb("w_hi", [P, SPLIT, KC * COL], F32R)
        w_lo = sb("w_lo", [P, SPLIT, KC * COL], F32R)
        x_hi = sb("x_hi", [P, KT, S], F32R)
        x_lo = sb("x_lo", [P, KT, S], F32R)
        y_hi = sb("y_hi", [P, 8, S], F32R)
        y_lo = sb("y_lo", [P, 8, S], F32R)
        res = sb("res", [P, TOK, D])
        z = sb("z", [P, 6, TOK, COL])
        xn = z[:, 0:4, :, :].rearrange("p b t c -> p (b t c)").rearrange("p (t d) -> p t d", t=TOK)
        qk = sb("qk", [P, TOK, 8, HD])
        tmp = sb("tmp", [P, 4 * COL])
        qT = sb("qT", [P, 2, S])
        kT = sb("kT", [P, 2, S])
        s_sb = sb("s_sb", [P, 3 * P])
        heads = sb("heads", [P, 2 * COL])
        y_sb = heads[:].rearrange("p (t c) -> p t c", t=TOK)
        y_att = heads[:, 0:S].rearrange("p (t c) -> p t c", t=TOK)
        p_sb = heads[:, S:S + 3 * P]
        pT = heads[:, S + 3 * P:S + 6 * P]
        pen = sb("pen", [P, 3 * P])
        top8 = sb("top8", [P, 2, 8])
        w_idx = sb("w_idx", [P, TOK, IDX_HEADS])
        ident = sb("ident_sb", [P, P])
        causal = sb("causal_sb", [P, 3 * P])
        upto = sb("upto_sb", [P, 2 * P])
        rot = sb("rot", [P, 2, TOK, P])
        cols = sb("cols", [P, 4, P])
        gains = sb("gains", [P, 64])
        small = sb("small", [P, 4])
        pconst = sb("pconst", [P, 4])
        ssq = sb("ssq", [P, 16])
        rstd = sb("rstd", [P, 16])
        nmax = sb("nmax", [P, TOK])
        sums = sb("sums", [P, TOK])
        rinv = sb("rinv", [P, TOK])
        bfb = sb("bfb", [P, FOX_HEADS])
        c_nat = sb("c_nat", [P, TOK * FOX_HEADS])
        cT = qT[0:FOX_HEADS, 1, :]
        ckT = kT[0:FOX_HEADS, 1, :]
        minus = sb("minus", [FOX_HEADS, P])
        stats = sb("stats", [P, TOK, 4, 6])
        mv = sb("mv", [P, TOK, 2])
        rows = z[:, 4, :, :].rearrange("p t c -> p (t c)")[:, 0:4 * P].rearrange("p (r c) -> p r c", r=4)
        kdup = z[:, 5, :, :].rearrange("p t c -> p (t c)")[:, 0:2 * P].rearrange("p (t c) -> p t c", t=TOK)
        fz = z[:, 5, :, :].rearrange("p t c -> p (t c)")[:, 256:256 + 4 * TOK * FOX_HEADS]\
            .rearrange("p (a t c) -> p a t c", a=4, t=TOK)
        table = sb("table", [P, RET_HEADS * 3 * P])
        band = table[:, 0:4 * 3 * P]
        rel = table[:, 12 * P:18 * P].rearrange("p (b c) -> p b c", b=2)
        isc = table[:, 18 * P:21 * P]
        kiT = table[:, 21 * P:23 * P]
        arena = sb("arena", [P, 6144])

        def part(at, *shape):
            n = int(np.prod(shape))
            names = "abc"[:len(shape)]
            kw = dict(zip(names, shape))
            return arena[:, at:at + n].rearrange(f"p ({' '.join(names)}) -> p {' '.join(names)}", **kw)

        qiT, poolT, pw = part(0, 8, S), part(2048, 8, S), part(4096, 8, 256)
        up = part(0, 2, 2, S + 2)
        cg, cg2, cg3 = part(1032, 2, 2, S), part(2056, 2, 2, S), part(3080, 2, 2, S)
        th, act_t, act_r = part(4104, 2, S), part(4616, 2, S), part(5128, 2, S)
        gbc = part(0, 2, D)
        rp = arena[:, 4096:6144]

        acc = [[ctx.enter_context(nc.psum_tensor(f"acc{b}{t}", [P, COL], F32)) for t in range(TOK)]
               for b in range(2)]
        M = [ctx.enter_context(nc.psum_tensor(f"mix{b}", [P, COL], F32)) for b in range(4)]

        G_ATT, G_FFN, G_POOL, G_Q, G_K, G_FQ, G_FK = 0, 16, 32, 40, 41, 42, 43

        raw_full = [sem(f"raw_full{k}") for k in range(RAW)]
        hi_done, lo_done = sem("hi_done"), sem("lo_done")
        used = sem("used")
        drained = [sem("drained0"), sem("drained1")]
        x_full, c_full = sem("x_full"), sem("c_full")
        b_full = sem("b_full")
        xn_ready = sem("xn_ready")
        ssq_done = sem("ssq_done")
        xt_mm, xt_hi, xt_lo = sem("xt_mm"), sem("xt_hi"), sem("xt_lo")
        vec_mm, vec_sb = sem("vec_mm"), sem("vec_sb")
        dve = sem("dve_chain")
        dve_n = [0]
        idx_mm, idx_sb = sem("idx_mm"), sem("idx_sb")
        rel_mm, rel_sb, rel_add = sem("rel_mm"), sem("rel_sb"), sem("rel_add")
        pen_ready = sem("pen_ready")
        pd_mm, pd_sb, py_mm, py_hi, py_lo = (sem(n) for n in ("pd_mm", "pd_sb", "py_mm", "py_hi", "py_lo"))
        out_sem = sem("out_sem")
        f_abs, f_exp, f_log, f_lf, f_mm, f_sb = (sem(n) for n in (
            "f_abs", "f_exp", "f_log", "f_lf", "f_mm", "f_sb"))
        scaled = sem("res_scaled")
        want, got, added, pc = sem("power_want"), sem("power_got"), sem("power_added"), sem("power_const")
        W_RET = 4 + FOX_GROUPS + 1

        class Att:

            def __init__(self, p):
                self.normed = sem(p + "normed")
                self.gated = sem(p + "gated")
                self.tanh = sem(p + "tanh")
                self.chain = sem(p + "chain")
                self.qk_mm, self.qk_sb = sem(p + "qk_mm"), sem(p + "qk_sb")
                self.ck = sem(p + "ck")
                self.s_mm, self.maxed, self.exped = sem(p + "s_mm"), sem(p + "maxed"), sem(p + "exped")
                self.p_mm, self.p_sb = sem(p + "p_mm"), sem(p + "p_sb")
                self.o_mm, self.y_sb = sem(p + "o_mm"), sem(p + "y_sb")
                self.y_mm, self.y_hi, self.y_lo = sem(p + "y_mm"), sem(p + "y_hi"), sem(p + "y_lo")

        att, fox = Att("att_"), Att("fox_")
        r_rot, r_gated, r_tanh = sem("r_rot"), sem("r_gated"), sem("r_tanh")
        r_chain, r_rot_chain, fox_norm = sem("r_chain"), sem("r_rot_chain"), sem("fox_norm")
        dec_full, ln_full = sem("dec_full"), sem("ln_full")
        r_qk_mm, r_qk_sb, r_s_mm, r_st, r_o_mm = (sem("r_" + n) for n in ("qk_mm", "qk_sb", "s_mm", "st", "o_mm"))
        r_t, r_y, r_y_mm, r_hi, r_lo = (sem("r_" + n) for n in ("t", "y", "y_mm", "hi", "lo"))
        u_mm, u_aff, u_c1, u_conv, u_tanh, u_r, u_act, u_hi, u_lo = (sem("u_" + n) for n in (
            "mm", "aff", "c1", "conv", "tanh", "r", "act", "hi", "lo"))

        def tiles(w):
            return w.rearrange("(k p) c -> p k c", p=P)

        w_in_v, w_out_v, w_up_v, w_down_v = tiles(w_in), tiles(w_out), tiles(w_up), tiles(w_down)
        fox_in_v, fox_out_v = tiles(fox_w_in[0]), tiles(fox_w_out[0])
        ret_in_v, ret_out_v = tiles(ret_w_in[0]), tiles(ret_w_out[0])

        def block_out(eng, blk):
            eng.wait_ge(drained[blk.base % 2], blk.plus(2).over(2).at())

        def all_out(eng, blk):
            eng.wait_ge(drained[0], blk.plus(1).over(2).at())
            eng.wait_ge(drained[1], blk.over(2).at())

        block = ctx.enter_context(nc.Block())

        @block.sync
        def _(sp):
            def chunk(g, src, kk=KC, n=COL):
                if g.base >= RAW or g.i is not None:
                    sp.wait_ge(lo_done, g.at(1 - RAW))
                slot = g.base % RAW
                sp.dma_start(raw[:, slot, 0:kk * n].rearrange("p (k c) -> p k c", k=kk), src)\
                    .then_inc(raw_full[slot], 16)

            def in_block(g, w_v, c0, n=COL, kk=KC):
                for c in range(KT // kk):
                    chunk(g.plus(c), w_v[:, c * kk:(c + 1) * kk, bass.ds(c0, n)], kk, n)
                return g.plus(KT // kk)

            def out_blocks(g, w_v, k0, kt):
                for n in range(NOUT):
                    for c in range(kt // KC):
                        chunk(g.plus(n * (kt // KC) + c),
                              w_v[:, bass.ds(k0 + c * KC, KC), n * COL:(n + 1) * COL])
                return g.plus(NOUT * kt // KC)

            sp.dma_start(res[:, 0, :], x[0, 0:P, :]).then_inc(x_full, 16)
            sp.dma_start(res[:, 1, :], x[0, P:S, :]).then_inc(x_full, 16)
            g = Count(0)
            g = in_block(g, w_in_v, C_QI)
            g = in_block(g, w_in_v, C_QI + COL)
            g = in_block(g, w_in_v, C_KI, NARROW, NARROW_K)
            g = in_block(g, w_in_v, 0)
            g = in_block(g, w_in_v, COL)
            for c in (C_Q, C_K, C_V):
                g = in_block(g, w_in_v, c)
            g = out_blocks(g, w_out_v, 0, 4)
            g = out_blocks(g, w_out_v, 4, 4)
            for c in (C_Q, C_K, C_V):
                g = in_block(g, w_in_v, c + COL)
            g = out_blocks(g, w_out_v, 8, 4)
            g = out_blocks(g, w_out_v, 12, 4)
            assert g.base == FFN_0

            def ffn_in(g, i):
                g = in_block(g, w_up_v, i * COL)
                return in_block(g, w_up_v, i * COL + D_FF)

            per = FFN_IN + FFN_OUT
            ffn_in(g, 0)
            with sp.Fori(1, PAIRS) as i:
                g = ffn_in(Count(FFN_0 + FFN_IN - per, per, i), i)
                out_blocks(g, w_down_v, i * 4 - 4, 4)
            out_blocks(Count(FOX_0 - FFN_OUT), w_down_v, 4 * PAIRS - 4, 4)

            g = in_block(Count(FOX_0), fox_in_v, 0)
            g = in_block(g, fox_in_v, 4 * D, FOX_HEADS, KT)
            for b in range(1, 4):
                g = in_block(g, fox_in_v, b * D)
            per = FOX_IN + FOX_OUT
            with sp.Fori(1, FOX_GROUPS) as i:
                g = Count(FOX_0 + 1 + FOX_IN - per, per, i)
                for b in range(4):
                    g = in_block(g, fox_in_v, i * COL + b * D)
                out_blocks(g, fox_out_v, i * 4 - 4, 4)
            out_blocks(Count(RET_0 - FOX_OUT), fox_out_v, 4 * FOX_GROUPS - 4, 4)

            def ret_in(g, i):
                g = in_block(g, ret_in_v, i * COL)
                g = in_block(g, ret_in_v, i * COL + D)
                for b in range(4):
                    g = in_block(g, ret_in_v, i * (2 * COL) + 2 * D + (b // 2) * 2 * D + (b % 2) * COL)
                return g

            per = RET_IN + RET_OUT
            ret_in(Count(RET_0), 0)
            with sp.Fori(1, RET_GROUPS) as i:
                g = ret_in(Count(RET_0 + RET_IN - per, per, i), i)
                out_blocks(g, ret_out_v, i * 8 - 8, 8)
            out_blocks(Count(TOTAL - RET_OUT), ret_out_v, 8 * RET_GROUPS - 8, 8)

            sp.wait_ge(xn_ready, 5)
            for t in range(TOK):
                sp.dma_start(out[0, t * P:(t + 1) * P, :], res[:, t, :]).then_inc(out_sem, 16)
            sp.wait_ge(out_sem, 16 * TOK)

        @block.gpsimd
        def _(pool):
            def load(dst, src, s):
                pool.dma_start(dst, src).then_inc(s, 16)

            def power(k, o, i_, eps):
                pool.wait_ge(want, k.at(1))
                n = i_.shape[1]
                c = 0 if eps == EPS else 1
                nc.gpsimd.tensor_tensor(o, i_, pconst[:, c:c + 1].to_broadcast([P, n]), ALU.add).then_inc(added, 1)
                pool.wait_ge(added, k.at(1))
                nc.gpsimd.tensor_tensor(o, o, pconst[:, 2:3].to_broadcast([P, n]), ALU.pow).then_inc(got, 1)

            def rows_power(k):
                power(Count(k), rstd[:, 0:TOK], ssq[:, 0:TOK], EPS)

            def heads_power(k):
                power(k, rstd[:], ssq[:], EPS)

            def var_power(k, eps):
                power(k, rstd[:, 0:TOK], mv[:, :, 1], eps)

            nc.gpsimd.memset(pconst[:, 0:1], EPS)
            nc.gpsimd.memset(pconst[:, 1:2], LN_EPS)
            nc.gpsimd.memset(pconst[:, 2:3], -0.5).then_inc(pc, 1)
            pool.wait_ge(pc, 1)
            rows_power(0)
            pool.wait_ge(vec_sb, 1)
            for j in range(3):
                load(rows[0:2 * D_FF // P, j, :], conv_w[j].rearrange("(j p) -> j p", p=P), b_full)
            load(rows[0:2 * D_FF // P, 3, :], conv_b.rearrange("(j p) -> j p", p=P), b_full)
            pool.wait_ge(py_lo, 8)
            load(table[:], decay_d, dec_full)
            heads_power(Count(1))
            heads_power(Count(2))
            rows_power(3)
            pool.wait_ge(xn_ready, 3)
            load(gbc[:, 0, :], ln_gain[0:1, :].to_broadcast([P, D]), ln_full)
            load(gbc[:, 1, :], ln_bias[0:1, :].to_broadcast([P, D]), ln_full)
            heads_power(Count(4))
            with pool.Fori(1, FOX_GROUPS) as i:
                heads_power(Count(4, 1, i))
            var_power(Count(W_RET - 1), LN_EPS)
            pool.wait_ge(xn_ready, 4)
            load(gbc[:, 0, :], ln_gain[1:2, :].to_broadcast([P, D]), ln_full)
            load(gbc[:, 1, :], ln_bias[1:2, :].to_broadcast([P, D]), ln_full)
            with pool.Fori(1, RET_GROUPS) as i:
                for h in range(RET_PAIR):
                    var_power(Count(W_RET - 2 + h, 2, i), GN_EPS)
            for h in range(RET_PAIR):
                var_power(Count(W_RET + RET_HEADS - 2 + h), GN_EPS)
            var_power(Count(W_RET + RET_HEADS), LN_EPS)

        @block.tensor
        def _(pe):
            def mm(o, l, r, start, stop):
                return nc.tensor.matmul(o, l, r, start=start, stop=stop)

            def chunk(g, b, lhs_hi, lhs_lo, k0, first, last, kk=KC, n=COL):
                pe.wait_ge(lo_done, g.at(1))
                slot = g.base % SPLIT
                for k in range(kk):
                    wh = w_hi[:, slot, k * n:(k + 1) * n]
                    wl = w_lo[:, slot, k * n:(k + 1) * n]
                    for t in range(TOK):
                        xh = lhs_hi[:, k0 + k, t * P:(t + 1) * P]
                        xl = lhs_lo[:, k0 + k, t * P:(t + 1) * P]
                        o = acc[b][t][:, 0:n]
                        mm(o, xh, wh, first and k == 0, False)
                        mm(o, xh, wl, False, False)
                        done = mm(o, xl, wh, False, last and k == kk - 1)
                done.then_inc(used, 1)

            def in_block(g, blk, step, slot, n=COL, kk=KC, build=None, hook=True):
                par = blk.base % 2
                if blk.plus(-1).some():
                    pe.wait_ge(drained[par], blk.over(2).at())
                for c in range(KT // kk):
                    if build is not None:
                        pe.wait_ge(xt_lo, 8 * build + c + 1)
                    chunk(g.plus(c), par, x_hi, x_lo, c * kk, c == 0, c == KT // kk - 1, kk, n)
                    if build is not None and c + 4 < 8:
                        xt(build, c + 4)
                    step(slot + c)

            def out_blocks(g, blk, y0, kt, step, slot):
                for nb in range(NOUT):
                    par = (blk.base + nb) % 2
                    pe.wait_ge(drained[par], blk.plus(nb).over(2).at())
                    for c in range(kt // KC):
                        chunk(g.plus(nb * (kt // KC) + c), par, y_hi, y_lo, y0 + c * KC,
                              c == 0, c == kt // KC - 1)
                        step(slot + nb * (kt // KC) + c)

            def xt(phase, j):
                if j >= 4:
                    pe.wait_ge(xt_lo, 8 * phase + j - 3)
                src = res[:] if phase >= 2 else xn
                for k in range(2):
                    for t in range(TOK):
                        c = k * S + t * P
                        done = nc.tensor.transpose(M[j % 4][:, c:c + P],
                                                   src[:, t, (2 * j + k) * P:(2 * j + k + 1) * P], ident[:])
                done.then_inc(xt_mm, 1)

            def xt_start(phase):
                pe.wait_ge(xn_ready, phase + 1)
                for j in range(4):
                    xt(phase, j)

            none = lambda s: None

            def att_step(A, what, n, h, group, forget, blk0):
                if what == "T":
                    if h == 0:
                        all_out(pe, blk0)
                    pe.wait_ge(A.normed, group.at(1))
                    if n.some():
                        pe.wait_ge(A.qk_sb, n.at())
                    for a in range(2):
                        for t in range(TOK):
                            c = a * S + t * P
                            done = nc.tensor.transpose(M[0][:, c:c + P], qk[:, t, a * GROUP + h, :], ident[:])
                    done.then_inc(A.qk_mm, 1)
                elif what == "S":
                    pe.wait_ge(A.qk_sb, n.at(1))
                    if n.some():
                        pe.wait_ge(A.y_lo, n.at())
                    if forget:
                        pe.wait_ge(A.ck, n.at(1))
                    for t in range(TOK):
                        o = M[1][:, t * P:(1 + 2 * t) * P]
                        keys = (t + 1) * P
                        done = mm(o, qT[:, 0, t * P:(t + 1) * P], kT[:, 0, 0:keys], True, not forget)
                        if forget:
                            done = mm(o, minus[:], ckT[:, 0:keys], False, True)
                    done.then_inc(A.s_mm, 1)
                elif what == "PT":
                    pe.wait_ge(A.exped, n.at(1))
                    if n.some():
                        pe.wait_ge(A.p_sb, n.at())
                    for c in range(3):
                        done = nc.tensor.transpose(M[2][:, c * P:(c + 1) * P], p_sb[:, c * P:(c + 1) * P], ident[:])
                    done.then_inc(A.p_mm, 1)
                elif what == "V":
                    pe.wait_ge(A.p_sb, n.at(1))
                    if n.some():
                        pe.wait_ge(A.y_sb, n.at())
                    v = z[:, 2, :, h * HD:(h + 1) * HD]
                    mm(M[3][:, 0:P], pT[:, 0:P], v[:, 0, :], True, True)
                    mm(M[3][:, P:2 * P], pT[:, P:2 * P], v[:, 0, :], True, False)
                    mm(M[3][:, P:2 * P], pT[:, 2 * P:3 * P], v[:, 1, :], False, True).then_inc(A.o_mm, 1)
                elif what == "Y":
                    pe.wait_ge(A.y_sb, n.at(1))
                    for t in range(TOK):
                        done = nc.tensor.transpose(M[1][:, t * P:(t + 1) * P], y_att[:, t, :], ident[:])
                    done.then_inc(A.y_mm, 1)

            ATT_AT = {0: "T", 1: "S", 3: "PT", 4: "V", 5: "Y"}

            def att_slots(A, n, group, forget, blk0):
                def step(s):
                    h = s // 6
                    if h < GROUP and s % 6 in ATT_AT:
                        att_step(A, ATT_AT[s % 6], n.plus(h), h, group, forget, blk0)
                return step

            pe.wait_ge(c_full, 16 * 14)
            nc.tensor.transpose(M[0][:, 0:44], rows[0:44, 3, :], ident[0:44, 0:44]).then_inc(vec_mm, 1)
            pe.wait_ge(vec_sb, 1)

            xt_start(0)
            in_block(Count(0), Count(0), none, 0, build=0)
            in_block(Count(8), Count(1), none, 8)
            in_block(Count(16), Count(2), none, 16, NARROW, NARROW_K)

            def indexer(s):
                if s < 4:
                    if s == 0:
                        all_out(pe, Count(2))
                    for k in range(2):
                        for t in range(TOK):
                            f = (2 * s + k) * P
                            c = k * S + t * P
                            done = nc.tensor.transpose(
                                M[s][:, c:c + P], z[:, f // COL, t, f % COL:f % COL + P], ident[:])
                    done.then_inc(idx_mm, 1)
                elif s == 4:
                    block_out(pe, Count(2))
                    pe.wait_ge(idx_sb, 4)
                    for t in range(TOK):
                        done = nc.tensor.transpose(M[2][:, t * P:(t + 1) * P], kdup[:, t, :], ident[:])
                    done.then_inc(idx_mm, 1)
                elif s < 16:
                    for h in range(min(16, 2 * (s - 5)), min(16, 2 * (s - 5) + 2)):
                        if h == 0:
                            pe.wait_ge(idx_sb, 5)
                        else:
                            if h >= 2:
                                pe.wait_ge(rel_sb, h - 1)
                        half = slice(64 * (h % 2), 64 * (h % 2) + 64)
                        for t in range(TOK):
                            done = mm(M[h % 2][:, t * P:(1 + 2 * t) * P], qiT[half, h // 2, t * P:(t + 1) * P],
                                      kiT[half, 0:(t + 1) * P], True, True)
                        done.then_inc(rel_mm, 1)

            in_block(Count(18), Count(3), indexer, 0)
            in_block(Count(26), Count(4), indexer, 8)

            def pool_step(s):
                if s < 8:
                    b = s % 2
                    if s == 0:
                        all_out(pe, Count(5))
                    if s >= 2:
                        pe.wait_ge(pd_sb, s - 1)
                    else:
                        pe.wait_ge(rel_sb, 16)
                    grp = s // 2
                    u = z[:, 2 + s // 4, :, (s % 4) * P:(s % 4 + 1) * P]
                    c = grp * 3 * P
                    o = M[2 + b]
                    mm(o[:, 0:S], u[:, 0, :], band[:, c:c + S], True, False)
                    mm(o[:, P:S], u[:, 1, :], band[:, c + S:c + 3 * P], False, True).then_inc(pd_mm, 1)
                elif s < 16:
                    t = s - 8
                    grp = t // 2
                    pe.wait_ge(pd_sb, 8)
                    if t >= 2:
                        pe.wait_ge(py_lo, t - 1)
                    for k in range(2):
                        done = mm(M[t % 2][:, 0:S], pw[:, 2 * grp + k, (t % 2) * P:(t % 2 + 1) * P],
                                  poolT[:, 2 * grp + k, :], k == 0, k == 1)
                    done.then_inc(py_mm, 1)

            for b in range(3):
                in_block(Count(34 + 8 * b), Count(5 + b), pool_step, 8 * b)
            pe.wait_ge(py_lo, 8)
            out_blocks(Count(58), Count(8), 0, 4, none, 0)
            out_blocks(Count(66), Count(12), 4, 4, none, 0)
            step = att_slots(att, Count(0), Count(0), False, Count(8))
            for b in range(3):
                in_block(Count(74 + 8 * b), Count(16 + b), step, 8 * b)
            pe.wait_ge(att.y_lo, 4)
            out_blocks(Count(98), Count(19), 0, 4, none, 0)
            step = att_slots(att, Count(4), Count(1), False, Count(19))
            for s in range(24):
                step(s)
            pe.wait_ge(att.y_lo, 8)
            out_blocks(Count(106), Count(23), 4, 4, none, 0)

            pe.wait_ge(b_full, 16 * 4)
            n = 2 * D_FF // P
            for j in range(4):
                done = nc.tensor.transpose(M[0][:, j * P:j * P + n], rows[0:n, j, :], ident[0:n, 0:n])
            done.then_inc(vec_mm, 1)
            pe.wait_ge(vec_sb, 2)

            def ffn_slots(pair, blk0):
                def step(s):
                    if s % 2 == 0 and s < 8:
                        f = s // 2
                        n = Count(pair.base * 4 + f, pair.per * 4, pair.i)
                        if f == 0:
                            all_out(pe, blk0)
                        if pair.some():
                            pe.wait_ge(u_aff, pair.at(0, 4))
                        for a in range(2):
                            for t in range(TOK):
                                c = a * S + t * P
                                done = nc.tensor.transpose(M[f][:, c:c + P], z[:, a, t, f * P:(f + 1) * P], ident[:])
                        done.then_inc(u_mm, 1)
                return step

            xt_start(1)
            in_block(Count(FFN_0), Count(FFN_B), none, 0, build=1)
            in_block(Count(FFN_0 + 8), Count(FFN_B + 1), none, 8)
            per = FFN_IN + FFN_OUT
            with pe.Fori(1, PAIRS) as i:
                g = Count(FFN_0 + FFN_IN - per, per, i)
                blk = Count(FFN_B + 2 - 6, 6, i)
                step = ffn_slots(Count(-1, 1, i), blk)
                in_block(g, blk, step, 0)
                in_block(g.plus(8), blk.plus(1), step, 8)
                pe.wait_ge(u_lo, i * 4)
                out_blocks(g.plus(16), blk.plus(2), 0, 4, none, 0)
            step = ffn_slots(Count(PAIRS - 1), Count(FOX_B - 4))
            for s in range(16):
                step(s)
            pe.wait_ge(u_lo, 4 * PAIRS)
            out_blocks(Count(FOX_0 - FFN_OUT), Count(FOX_B - 4), 0, 4, none, 0)

            def forget(s):
                if s == 12:
                    pe.wait_ge(f_lf, 1)
                    pe.wait_ge(xt_lo, 24)
                    lf = fz[:, 3, :, :]
                    mm(M[0][:, 0:16], upto[:, 0:P], lf[:, 0, :], True, True)
                    mm(M[0][:, 16:32], upto[:, P:2 * P], lf[:, 0, :], True, False)
                    mm(M[0][:, 16:32], upto[:, 0:P], lf[:, 1, :], False, True)
                    mm(M[1][0:16, 0:S], lf[:, 0, :], upto[:, 0:2 * P], True, False)
                    mm(M[1][0:16, P:S], lf[:, 1, :], upto[:, 0:P], False, True).then_inc(f_mm, 1)

            xt_start(2)
            in_block(Count(FOX_0), Count(FOX_B), none, 0, build=2)
            in_block(Count(FOX_0 + 8), Count(FOX_B + 1), none, 8, FOX_HEADS, KT)
            for b in range(1, 4):
                in_block(Count(FOX_0 + 1 + 8 * b), Count(FOX_B + 1 + b), forget, 8 * b)
            per = FOX_IN + FOX_OUT
            with pe.Fori(1, FOX_GROUPS) as i:
                g = Count(FOX_0 + 1 + FOX_IN - per, per, i)
                blk = Count(FOX_B + 5 - 8, 8, i)
                step = att_slots(fox, Count(-4, 4, i), Count(-1, 1, i), True, blk)
                for b in range(4):
                    in_block(g.plus(8 * b), blk.plus(b), step, 8 * b)
                pe.wait_ge(fox.y_lo, i * 4)
                out_blocks(g.plus(32), blk.plus(4), 0, 4, none, 0)
            step = att_slots(fox, Count(12), Count(3), True, Count(RET_B - 4))
            for s in range(24):
                step(s)
            pe.wait_ge(fox.y_lo, 16)
            out_blocks(Count(RET_0 - FOX_OUT), Count(RET_B - 4), 0, 4, none, 0)

            def ret_step(what, n, h, group, blk0):
                if what == "T":
                    if h == 0:
                        all_out(pe, blk0)
                    pe.wait_ge(r_rot, group.at(1))
                    if n.some():
                        pe.wait_ge(r_y, n.at())
                    for a in range(2):
                        for dt in range(2):
                            for t in range(TOK):
                                c = dt * S + t * P
                                src = qk[:, t, 4 * a + 2 * h + dt, :]
                                done = nc.tensor.transpose(M[a][:, c:c + P], src, ident[:])
                    done.then_inc(r_qk_mm, 1)
                elif what == "S":
                    pe.wait_ge(r_qk_sb, n.at(1))
                    if n.some():
                        pe.wait_ge(r_lo, n.at())
                    for dt in range(2):
                        mm(M[2][:, 0:S], kT[:, dt, 0:P], qT[:, dt, :], dt == 0, dt == 1)
                    for dt in range(2):
                        done = mm(M[2][:, S:S + P], kT[:, dt, P:S], qT[:, dt, P:S], dt == 0, dt == 1)
                    done.then_inc(r_s_mm, 1)
                elif what == "O":
                    pe.wait_ge(r_st, n.at(1))
                    v = z[:, 2 + h, :, :]
                    mm(M[0][:], s_sb[:, 0:P], v[:, 0, :], True, True)
                    mm(M[1][:], s_sb[:, P:2 * P], v[:, 0, :], True, False)
                    mm(M[1][:], s_sb[:, 2 * P:3 * P], v[:, 1, :], False, True).then_inc(r_o_mm, 1)
                elif what == "Y":
                    pe.wait_ge(r_y, n.at(1))
                    for k in range(4):
                        for t in range(TOK):
                            c = (k % 2) * S + t * P
                            done = nc.tensor.transpose(M[2 + k // 2][:, c:c + P], y_sb[:, t, k * P:(k + 1) * P], ident[:])
                    done.then_inc(r_y_mm, 1)

            RET_AT = {0: "T", 2: "S", 4: "O", 7: "Y"}

            def ret_slots(n, group, blk0):
                def step(s):
                    h = s // 10
                    if h < RET_PAIR and s % 10 in RET_AT:
                        ret_step(RET_AT[s % 10], n.plus(h), h, group, blk0)
                return step

            xt_start(3)
            in_block(Count(RET_0), Count(RET_B), none, 0, build=3)
            for b in range(1, 6):
                in_block(Count(RET_0 + 8 * b), Count(RET_B + b), none, 8 * b)
            per = RET_IN + RET_OUT
            with pe.Fori(1, RET_GROUPS) as i:
                g = Count(RET_0 + RET_IN - per, per, i)
                blk = Count(RET_B + 6 - 10, 10, i)
                step = ret_slots(Count(-2, 2, i), Count(-1, 1, i), blk)
                for b in range(6):
                    in_block(g.plus(8 * b), blk.plus(b), step, 8 * b)
                pe.wait_ge(r_lo, i * 2)
                out_blocks(g.plus(48), blk.plus(6), 0, 8, none, 0)
            step = ret_slots(Count(RET_HEADS - 2), Count(RET_GROUPS - 1), Count(RET_B + 10 * RET_GROUPS - 4))
            for s in range(20):
                step(s)
            pe.wait_ge(r_lo, RET_HEADS)
            out_blocks(Count(TOTAL - RET_OUT), Count(RET_B + 10 * RET_GROUPS - 4), 0, 8, none, 0)

        @block.scalar
        def _(act):
            def a_(o, i_, f, **kw):
                return nc.scalar.activation(o, i_, f, **kw)

            def split(g, k):
                g = g.plus(k)
                if g.i is None and g.base >= TOTAL:
                    return
                act.wait_ge(raw_full[g.base % RAW], g.over(RAW).at(1, 16))
                if g.plus(1 - SPLIT).some():
                    act.wait_ge(used, g.at(1 - SPLIT))
                a_(w_hi[:, g.base % SPLIT, :], raw[:, g.base % RAW, :], ACT.Copy).then_inc(hi_done, 1)

            def drain(g, blk, zb, free=()):
                act.wait_ge(used, g.at())
                for s, v in free:
                    act.wait_ge(s, v)
                par = blk.base % 2
                for t in range(TOK):
                    done = a_(z[:, zb, t, :], acc[par][t][:], ACT.Copy)
                done.then_inc(drained[par], 1)

            def xt_out(phase, j):
                act.wait_ge(xt_mm, 8 * phase + j + 1)
                if phase >= 2:
                    a_(x_hi[:, 2 * j:2 * j + 2, :].rearrange("p k s -> p (k s)"), M[j % 4][:], ACT.Copy)\
                        .then_inc(xt_hi, 1)
                    return
                c = (G_ATT, G_FFN)[phase] + 2 * j
                for k in range(2):
                    done = a_(x_hi[:, 2 * j + k, :], M[j % 4][:, k * S:(k + 1) * S], ACT.Copy,
                              scale=gains[:, c + k:c + k + 1])
                done.then_inc(xt_hi, 1)

            def first_block(phase, g, step):
                for j in range(4):
                    xt_out(phase, j)
                for s in range(CH):
                    split(g, s + LEAD)
                    if s + 4 < 8:
                        xt_out(phase, s + 4)
                    step(s)

            def squares(phase):
                for t in range(TOK):
                    done = a_(xn[:, t, :], res[:, t, :], ACT.Square, accum_out=ssq[:, t:t + 1])
                done.then_inc(ssq_done, 1)

            def slots(g, n, step, s0=0):
                for s in range(s0, s0 + n):
                    split(g, s - s0 + LEAD)
                    step(s)

            none = lambda s: None

            def att_step(A, what, n, gq, gk):
                if what == "E":
                    act.wait_ge(A.qk_mm, n.at(1))
                    if n.some():
                        act.wait_ge(A.s_mm, n.at())
                    a_(qT[:, 0, :], M[0][:, 0:S], ACT.Copy, scale=gains[:, gq:gq + 1])
                    a_(kT[:, 0, :], M[0][:, S:2 * S], ACT.Copy, scale=gains[:, gk:gk + 1]).then_inc(A.qk_sb, 1)
                elif what == "P":
                    act.wait_ge(A.maxed, n.at(1))
                    if n.some():
                        act.wait_ge(A.p_mm, n.at())
                        act.wait_ge(A.y_sb, n.at())
                    for t in range(TOK):
                        c = slice(t * P, (1 + 2 * t) * P)
                        done = a_(p_sb[:, c], s_sb[:, c], ACT.Exp, bias=nmax[:, t:t + 1], accum_out=sums[:, t:t + 1])
                    done.then_inc(A.exped, 1)
                elif what == "C":
                    act.wait_ge(A.p_mm, n.at(1))
                    if n.some():
                        act.wait_ge(A.o_mm, n.at())
                    a_(pT, M[2][:, 0:3 * P], ACT.Copy).then_inc(A.p_sb, 1)

            def att_slots(A, n, gq, gk, y0, half):
                def step(s):
                    h = s // 6
                    if h >= GROUP:
                        return
                    m = n.plus(h)
                    if s % 6 in (0, 2, 3):
                        att_step(A, {0: "E", 2: "P", 3: "C"}[s % 6], m, gq, gk)
                    elif s % 6 == 5:
                        act.wait_ge(A.y_mm, m.at(1))
                        a_(y_hi[:, y0 + h, :], M[1][:, 0:S], ACT.Copy, scale=half).then_inc(A.y_hi, 1)
                return step

            def load(dst, src):
                act.dma_start(dst, src).then_inc(c_full, 16)

            load(rows[0:16, 3, :], attn_norm_g.rearrange("(j p) -> j p", p=P))
            load(rows[16:32, 3, :], ffn_norm_g.rearrange("(j p) -> j p", p=P))
            load(rows[32:40, 3, :], pool_scale.rearrange("(j p) -> j p", p=P))
            load(rows[40:41, 3, :], q_norm_g.rearrange("(j p) -> j p", p=P))
            load(rows[41:42, 3, :], k_norm_g.rearrange("(j p) -> j p", p=P))
            load(rows[42:43, 3, :], fox_q_gain)
            load(rows[43:44, 3, :], fox_k_gain)
            load(ident[:], ident_d)
            load(causal[:], causal_d)
            load(upto[:], upto_d)
            load(band, poolband_d)
            load(pw, pool_w.rearrange("g (t p) d -> p (g t) d", p=P))
            load(rot[:].rearrange("p a t c -> p (a t c)"), rotary_d)
            load(bfb[:], fox_b_f.to_broadcast([P, FOX_HEADS]))
            for k in range(LEAD):
                split(Count(0), k)
            act.wait_ge(x_full, 32)
            squares(0)
            act.wait_ge(vec_mm, 1)
            a_(gains[:, 0:44], M[0][:, 0:44], ACT.Copy).then_inc(vec_sb, 1)
            act.wait_ge(vec_sb, 1)

            first_block(0, Count(0), none)
            drain(Count(8), Count(0), 0)
            slots(Count(8), 8, none)
            drain(Count(16), Count(1), 1)
            slots(Count(16), 2, none)
            act.wait_ge(used, 18)
            for t in range(TOK):
                a_(kdup[:, t, 0:64], acc[0][t][:, 0:64], ACT.Copy)
                a_(kdup[:, t, 64:128], acc[0][t][:, 0:64], ACT.Copy)
                done = a_(w_idx[:, t, :], acc[0][t][:, 64:80], ACT.Copy, scale=float(IDX_HEADS * IDX_DIM) ** -0.5)
            done.then_inc(drained[0], 1)

            def indexer(s):
                if s < 4:
                    act.wait_ge(idx_mm, s + 1)
                    a_(qiT[:, 2 * s:2 * s + 2, :].rearrange("p k s -> p (k s)"), M[s][:], ACT.Copy).then_inc(idx_sb, 1)
                elif s == 4:
                    act.wait_ge(idx_mm, 5)
                    a_(kiT, M[2][:, 0:S], ACT.Copy).then_inc(idx_sb, 1)
                else:
                    for h in range(min(16, 2 * (s - 5)), min(16, 2 * (s - 5) + 2)):
                        act.wait_ge(rel_mm, h + 1)
                        if h >= 2:
                            act.wait_ge(rel_add, h - 1)
                        a_(rel[:, h % 2, :], M[h % 2][:, 0:3 * P], ACT.Relu).then_inc(rel_sb, 1)

            slots(Count(18), 8, indexer)
            drain(Count(26), Count(3), 2)
            slots(Count(26), 8, indexer, 8)
            drain(Count(34), Count(4), 3)

            def pool_step(s):
                if s < 8:
                    act.wait_ge(pd_mm, s + 1)
                    a_(poolT[:, s, :], M[2 + s % 2][:, 0:S], ACT.Copy).then_inc(pd_sb, 1)
                elif s < 16:
                    t = s - 8
                    act.wait_ge(py_mm, t + 1)
                    a_(y_hi[:, t, :], M[t % 2][:, 0:S], ACT.Copy, scale=gains[:, G_POOL + t:G_POOL + t + 1])\
                        .then_inc(py_hi, 1)

            slots(Count(34), 8, pool_step)
            drain(Count(42), Count(5), 0, [(idx_mm, 4)])
            slots(Count(42), 8, pool_step, 8)
            drain(Count(50), Count(6), 1)
            slots(Count(50), 8, pool_step, 16)
            drain(Count(58), Count(7), 2, [(pd_mm, 8)])
            slots(Count(58), 16, none)
            step = att_slots(att, Count(0), G_Q, G_K, 0, 1.0)
            slots(Count(74), 8, step)
            drain(Count(82), Count(16), 0, [(att.normed, 1)])
            slots(Count(82), 8, step, 8)
            drain(Count(90), Count(17), 1)
            slots(Count(90), 8, step, 16)
            drain(Count(98), Count(18), 2, [(att.o_mm, 4)])
            slots(Count(98), 8, none)
            step = att_slots(att, Count(4), G_Q, G_K, 4, 1.0)
            for s in range(24):
                step(s)
            slots(Count(106), 8, none)

            act.wait_ge(vec_mm, 2)
            a_(cols[:].rearrange("p a c -> p (a c)"), M[0][:], ACT.Copy).then_inc(vec_sb, 1)
            act.wait_ge(vec_sb, 2)
            all_out(act, Count(FFN_B))
            squares(1)

            def ffn_slots(pair):
                def tile(f):
                    return Count(pair.base * 4 + f, pair.per * 4, pair.i)

                def tap(a, f, j):
                    c = pair.at(0, 4) + (a * D_FF // P + f)
                    return cols[:, j, bass.ds(c, 1)]

                def step(s):
                    if s % 2 == 1 and s < 9:
                        f = s // 2
                        n, b = tile(f), f % 2
                        act.wait_ge(u_conv, n.at(1))
                        a_(th[:, b, :], cg3[:, b, 0, :], ACT.Tanh, scale=0.5).then_inc(u_tanh, 1)
                    if s % 2 == 0 and 0 < s < 10:
                        f = s // 2 - 1
                        n, b = tile(f), f % 2
                        act.wait_ge(u_act, n.at(1))
                        a_(y_hi[:, f, :], act_t[:, b, :], ACT.Copy).then_inc(u_hi, 1)
                    if s % 2 == 0 and s < 8:
                        f = s // 2
                        n, b = tile(f), f % 2
                        act.wait_ge(u_mm, n.at(1))
                        if n.plus(-1).some():
                            act.wait_ge(u_act, n.at(-1 if f else 0))
                        p2 = M[f][:].rearrange("p (a s) -> p a s", a=2)
                        a_(up[:, b, :, 2:S + 2], p2, ACT.Copy)
                        for a in range(2):
                            done = a_(cg[:, b, a, :], M[f][:, a * S:(a + 1) * S], ACT.Identity,
                                      scale=tap(a, f, 2), bias=tap(a, f, 3))
                        done.then_inc(u_aff, 1)
                return step

            g = Count(FFN_0)
            first_block(1, g, none)
            drain(g.plus(8), Count(FFN_B), 0)
            slots(g.plus(8), 8, none)
            drain(g.plus(16), Count(FFN_B + 1), 1)
            per = FFN_IN + FFN_OUT
            with act.Fori(1, PAIRS) as i:
                g = Count(FFN_0 + FFN_IN - per, per, i)
                blk = Count(FFN_B + 2 - 6, 6, i)
                step = ffn_slots(Count(-1, 1, i))
                slots(g, 8, step)
                drain(g.plus(8), blk, 0, [(u_mm, i * 4)])
                slots(g.plus(8), 8, step, 8)
                drain(g.plus(16), blk.plus(1), 1)
                slots(g.plus(16), 8, none)
            step = ffn_slots(Count(PAIRS - 1))
            for s in range(16):
                step(s)
            slots(Count(FOX_0 - FFN_OUT), 8, none)

            g = Count(FOX_0)
            first_block(2, g, none)
            drain(g.plus(8), Count(FOX_B), 0)

            def forget(s):
                if s == 9:
                    block_out(act, Count(FOX_B + 1))
                    a_(fz[:, 1, :, :], fz[:, 0, :, :], ACT.Abs).then_inc(f_abs, 1)
                    act.wait_ge(f_abs, 1)
                    a_(fz[:, 1, :, :], fz[:, 1, :, :], ACT.Exp, scale=-1.0).then_inc(f_exp, 1)
                    act.wait_ge(f_exp, 1)
                    a_(fz[:, 2, :, :], fz[:, 1, :, :], ACT.Ln, bias=1.0).then_inc(f_log, 1)

            def tanh_gate(gated, zb, t_sem, n, blk):
                block_out(act, blk)
                if n.some():
                    act.wait_ge(gated, n.at())
                a_(tmp[:, 0:TOK * COL], z[:, zb, :, :].rearrange("p t c -> p (t c)"), ACT.Tanh, scale=0.5)\
                    .then_inc(t_sem, 1)

            slots(g.plus(8), 1, none)
            for b in range(1, 4):
                slots(g.plus(1 + 8 * b), 8, forget, 8 * b)
                drain(g.plus(9 + 8 * b), Count(FOX_B + 1 + b), b)
            tanh_gate(fox.gated, 3, fox.tanh, Count(0), Count(FOX_B + 4))
            per = FOX_IN + FOX_OUT
            with act.Fori(1, FOX_GROUPS) as i:
                g = Count(FOX_0 + 1 + FOX_IN - per, per, i)
                blk = Count(FOX_B + 5 - 8, 8, i)
                step = att_slots(fox, Count(-4, 4, i), G_FQ, G_FK, 0, 0.5)
                slots(g, 8, step)
                drain(g.plus(8), blk, 0, [(fox.normed, i)])
                slots(g.plus(8), 8, step, 8)
                drain(g.plus(16), blk.plus(1), 1)
                slots(g.plus(16), 8, step, 16)
                drain(g.plus(24), blk.plus(2), 2, [(fox.o_mm, i * 4)])
                slots(g.plus(24), 8, none)
                drain(g.plus(32), blk.plus(3), 3, [(fox.y_sb, i * 4)])
                tanh_gate(fox.gated, 3, fox.tanh, Count(0, 1, i), blk.plus(3))
                slots(g.plus(32), 8, none)
            step = att_slots(fox, Count(12), G_FQ, G_FK, 0, 0.5)
            for s in range(24):
                step(s)
            slots(Count(RET_0 - FOX_OUT), 8, none)

            def ret_slots(n):
                def step(s):
                    h = s // 10
                    if h >= RET_PAIR:
                        return
                    m = n.plus(h)
                    if s % 10 == 0:
                        act.wait_ge(r_qk_mm, m.at(1))
                        if m.some():
                            act.wait_ge(r_s_mm, m.at())
                        a_(qT[:].rearrange("p k s -> p (k s)"), M[0][:], ACT.Copy)
                        a_(kT[:].rearrange("p k s -> p (k s)"), M[1][:], ACT.Copy).then_inc(r_qk_sb, 1)
                    elif s % 10 == 6:
                        act.wait_ge(r_t, m.at(1))
                        if m.some():
                            act.wait_ge(r_y_mm, m.at())
                        for t in range(TOK):
                            done = a_(y_sb[:, t, :], tmp[:, (2 + t) * COL:(3 + t) * COL], ACT.Copy, scale=rstd[:, t:t + 1])
                        done.then_inc(r_y, 1)
                    elif s % 10 == 7:
                        act.wait_ge(r_y_mm, m.at(1))
                        for k in range(2):
                            done = a_(y_hi[:, 4 * h + 2 * k:4 * h + 2 * k + 2, :].rearrange("p k s -> p (k s)"),
                                      M[2 + k][:], ACT.Copy, scale=0.5)
                        done.then_inc(r_hi, 1)
                return step

            def ret_group(g, blk, step, free):
                for b in range(6):
                    slots(g.plus(8 * b), 8, step, 8 * b)
                    drain(g.plus(8 * b + 8), blk.plus(b), b, free.get(b, ()))
                    if b >= 4:
                        tanh_gate(r_gated, b, r_tanh, tg.plus(b - 4), blk.plus(b))

            g = Count(RET_0)
            first_block(3, g, none)
            drain(g.plus(8), Count(RET_B), 0)
            for b in range(1, 6):
                slots(g.plus(8 * b), 8, none, 8 * b)
                drain(g.plus(8 * b + 8), Count(RET_B + b), b)
                if b >= 4:
                    tanh_gate(r_gated, b, r_tanh, Count(b - 4), Count(RET_B + b))
            per = RET_IN + RET_OUT
            with act.Fori(1, RET_GROUPS) as i:
                g = Count(RET_0 + RET_IN - per, per, i)
                blk = Count(RET_B + 6 - 10, 10, i)
                tg = Count(0, 2, i)
                ret_group(g, blk, ret_slots(Count(-2, 2, i)),
                          {0: [(r_rot, i)], 2: [(r_o_mm, i * 2 - 1)], 3: [(r_o_mm, i * 2)], 4: [(r_t, i * 2)]})
                slots(g.plus(48), 16, none)
            step = ret_slots(Count(RET_HEADS - 2))
            for s in range(20):
                step(s)
            slots(Count(TOTAL - RET_OUT), 16, none)

        @block.vector
        def _(v):
            V = nc.vector

            def link(ins):
                dve_n[0] += 1
                ins.then_inc(dve, 1)
                v.wait_ge(dve, dve_n[0])

            class Chain:

                def __init__(self, s, n, per):
                    self.s, self.n, self.per, self.k = s, n, per, 0

                def link(self, ins):
                    self.k += 1
                    ins.then_inc(self.s, 1)
                    v.wait_ge(self.s, self.n.at(0, self.per) + self.k)

            def split(g, k):
                g = g.plus(k)
                if g.i is None and g.base >= TOTAL:
                    return
                v.wait_ge(hi_done, g.at(1))
                a = g.base % SPLIT
                V.tensor_tensor(w_lo[:, a, :], raw[:, g.base % RAW, :], w_hi[:, a, :], ALU.subtract)\
                    .then_inc(lo_done, 1)

            def add_out(g, blk, nb):
                par = blk.base % 2
                v.wait_ge(used, g.at())
                v.wait_ge(drained[par], blk.over(2).at())
                v.wait_ge(drained[1 - par], blk.plus(1).over(2).at())
                for t in range(TOK):
                    c = slice(nb * COL, (nb + 1) * COL)
                    done = V.tensor_tensor(res[:, t, c], acc[par][t][:], res[:, t, c], ALU.add)
                done.then_inc(drained[par], 1)

            def out_slots(g, blk, kt, step=lambda s: None, s0=0):
                for nb in range(NOUT):
                    for c in range(kt // KC):
                        s = nb * (kt // KC) + c
                        split(g, s + LEAD)
                        step(s0 + s)
                    add_out(g.plus((nb + 1) * (kt // KC)), blk.plus(nb), nb)

            def xt_out(phase, j):
                v.wait_ge(xt_hi, 8 * phase + j + 1)
                xl = x_lo[:, 2 * j:2 * j + 2, :]
                xh = x_hi[:, 2 * j:2 * j + 2, :]
                if phase >= 2:
                    V.tensor_tensor(xl.rearrange("p k s -> p (k s)"), M[j % 4][:],
                                    xh.rearrange("p k s -> p (k s)"), ALU.subtract).then_inc(xt_lo, 1)
                    return
                c = (G_ATT, G_FFN)[phase] + 2 * j
                for k in range(2):
                    done = V.scalar_tensor_tensor(xl[:, k, :], M[j % 4][:, k * S:(k + 1) * S],
                                                  gains[:, c + k:c + k + 1], xh[:, k, :], ALU.mult, ALU.subtract)
                done.then_inc(xt_lo, 1)

            def first_block(phase, g):
                for j in range(4):
                    xt_out(phase, j)
                for s in range(CH):
                    split(g, s + LEAD)
                    if s + 4 < 8:
                        xt_out(phase, s + 4)

            def slots(g, n, step=lambda s: None, s0=0):
                for s in range(s0, s0 + n):
                    split(g, s - s0 + LEAD)
                    step(s)

            def power(k, ins):
                ins.then_inc(want, 1)
                v.wait_ge(got, k.at(1))

            def rms_rows(phase):
                v.wait_ge(ssq_done, phase + 1)
                power(Count((0, 3)[phase]), V.tensor_scalar(ssq[:, 0:TOK], ssq[:, 0:TOK], 1.0 / D, None, ALU.mult))
                for t in range(TOK):
                    done = V.tensor_scalar(xn[:, t, :], res[:, t, :], rstd[:, t:t + 1], None, ALU.mult)
                done.then_inc(xn_ready, 1)

            def layer_norm(which):
                all_out(v, Count((RET_B, RET_B + 10 * RET_GROUPS)[which]))
                for t in range(TOK):
                    for q in range(4):
                        done = V.bn_stats(stats[:, t, q, :], res[:, t, q * COL:(q + 1) * COL])
                link(done)
                for t in range(TOK):
                    done = V.bn_aggr(mv[:, t, :], stats[:, t, :, :].rearrange("p a b -> p (a b)"))
                power(Count((W_RET - 1, W_RET + RET_HEADS)[which]), done)
                for t in range(TOK):
                    done = V.tensor_scalar(res[:, t, :], res[:, t, :], mv[:, t, 0:1], rstd[:, t:t + 1],
                                           ALU.subtract, ALU.mult)
                link(done)
                v.wait_ge(ln_full, 32 * (which + 1))
                for t in range(TOK):
                    done = V.tensor_tensor(res[:, t, :], res[:, t, :], gbc[:, 0, :], ALU.mult)
                link(done)
                for t in range(TOK):
                    done = V.tensor_tensor(res[:, t, :], res[:, t, :], gbc[:, 1, :], ALU.add)
                done.then_inc(xn_ready, 1)

            def norm_qk(A, ch, part, zr, k):
                t = part % 2
                q = z[:, 0:2, t, :]
                if part < 2:
                    if part == 0:
                        block_out(v, zr)
                    sq = tmp[:, 2 * COL:4 * COL]
                    ch.link(V.tensor_tensor(sq.rearrange("p (b c) -> p b c", b=2), q, q, ALU.mult))
                    done = V.tensor_reduce(ssq[:, 8 * t:8 * t + 8], sq.rearrange("p (h c) -> p h c", c=HD), AX, ALU.add)
                    ch.link(done)
                    if part == 1:
                        V.tensor_scalar(ssq[:], ssq[:], 1.0 / HD, None, ALU.mult).then_inc(want, 1)
                else:
                    if part == 2:
                        v.wait_ge(got, k.at(1))
                    done = V.tensor_tensor(qk[:, t, :, :].rearrange("p (b h) c -> p b h c", b=2),
                                           q.rearrange("p b (h c) -> p b h c", c=HD),
                                           rstd[:, 8 * t:8 * t + 8].rearrange("p (b h c) -> p b h c", b=2, c=1)
                                           .to_broadcast([P, 2, GROUP, HD]), ALU.mult)
                    if part == 3:
                        done.then_inc(A.normed, 1)

            NORM_LINKS = 4

            def att_slots(A, n, y0, forget, head0, mask):
                def step(s):
                    h = s // 6
                    if h >= GROUP:
                        return
                    m = n.plus(h)
                    if s % 6 == 0 and forget:
                        if m.some():
                            v.wait_ge(A.s_mm, m.at())
                        V.tensor_scalar(ckT, cT, ident[0:FOX_HEADS, bass.ds(head0 + h, 1)], None, ALU.mult)\
                            .then_inc(A.ck, 1)
                    elif s % 6 == 1:
                        v.wait_ge(A.s_mm, m.at(1))
                        if m.some():
                            v.wait_ge(A.exped, m.at())
                        for t in range(TOK):
                            c = slice(t * P, (1 + 2 * t) * P)
                            if forget:
                                sc = c_nat[:, bass.ds(head0 + (t * FOX_HEADS + h), 1)]
                                done = V.scalar_tensor_tensor(s_sb[:, c], M[1][:, c], sc, mask[:, c], ALU.add, ALU.add)
                            else:
                                done = V.scalar_tensor_tensor(s_sb[:, c], M[1][:, c], HD ** -0.5, mask[:, c], ALU.mult, ALU.add)
                        ch = Chain(A.chain, m, 2)
                        ch.link(done)
                        for t in range(TOK):
                            done = V.reduce_max(nmax[:, t:t + 1], s_sb[:, t * P:(1 + 2 * t) * P], AX, negate=True)
                        done.then_inc(A.maxed, 1)
                    elif s % 6 == 4:
                        v.wait_ge(A.o_mm, m.at(1))
                        if m.some():
                            v.wait_ge(A.y_mm, m.at())
                        ch = Chain(A.chain, m, 2)
                        ch.k = 1
                        ch.link(V.reciprocal(rinv[:], sums[:]))
                        for t in range(TOK):
                            o = M[3][:, t * P:(t + 1) * P]
                            if forget:
                                done = V.scalar_tensor_tensor(y_att[:, t, :], o, rinv[:, t:t + 1],
                                                              z[:, 3, t, h * HD:(h + 1) * HD], ALU.mult, ALU.mult)
                            else:
                                done = V.tensor_scalar(y_att[:, t, :], o, rinv[:, t:t + 1], None, ALU.mult)
                        done.then_inc(A.y_sb, 1)
                    elif s % 6 == 5:
                        v.wait_ge(A.y_hi, m.at(1))
                        V.scalar_tensor_tensor(y_lo[:, y0 + h, :], M[1][:, 0:S], 0.5 if forget else 1.0,
                                               y_hi[:, y0 + h, :], ALU.mult, ALU.subtract).then_inc(A.y_lo, 1)
                return step

            V.memset(minus[:], -1.0)
            V.memset(isc, 0.0)
            link(V.memset(small[:], 0.0))
            for k in range(LEAD):
                split(Count(0), k)
            v.wait_ge(x_full, 32)
            rms_rows(0)
            v.wait_ge(vec_sb, 1)
            link(V.tensor_scalar(gains[:, G_FQ:G_FQ + 1], gains[:, G_FQ:G_FQ + 1], HD ** -0.5, None, ALU.mult))

            first_block(0, Count(0))
            slots(Count(8), 10)

            def indexer(s):
                if s < 5:
                    return
                if s == 5:
                    block_out(v, Count(2))
                for h in range(min(16, 2 * (s - 5)), min(16, 2 * (s - 5) + 2)):
                    v.wait_ge(rel_sb, h + 1)
                    if h > 0:
                        v.wait_ge(rel_add, h)
                    for t in range(TOK):
                        c = slice(t * P, (1 + 2 * t) * P)
                        done = V.scalar_tensor_tensor(isc[:, c], rel[:, h % 2, c], w_idx[:, t, h:h + 1], isc[:, c],
                                                      ALU.mult, ALU.add)
                    done.then_inc(rel_add, 1)

            slots(Count(18), 16, indexer)

            def topk(s):
                if s == 0:
                    v.wait_ge(rel_add, 16)
                    link(V.tensor_tensor(isc, isc, causal[:], ALU.add))
                if s < 8:
                    for t in range(TOK):
                        c = slice(t * P, (1 + 2 * t) * P)
                        done = V.max(top8[:, t, :], isc[:, c])
                    link(done)
                    for t in range(TOK):
                        c = slice(t * P, (1 + 2 * t) * P)
                        done = V.match_replace(isc[:, c], top8[:, t, :], isc[:, c], TAKEN)
                    link(done)
                if s == 8:
                    link(V.tensor_scalar(pen[:], isc, TAKEN * 0.9, NEG, ALU.is_gt, ALU.mult))
                    link(V.tensor_tensor(pen[:], pen[:], causal[:], ALU.min))

            def pool_step(s):
                topk(s)
                if 8 <= s < 16:
                    t = s - 8
                    v.wait_ge(py_hi, t + 1)
                    V.scalar_tensor_tensor(y_lo[:, t, :], M[t % 2][:, 0:S], gains[:, G_POOL + t:G_POOL + t + 1],
                                           y_hi[:, t, :], ALU.mult, ALU.subtract).then_inc(py_lo, 1)

            slots(Count(34), 24, pool_step)
            link_now = link

            class Straight:
                link = staticmethod(link_now)

            def norm_step(A, ch, zr, s0, k):
                def step(s):
                    if s0 <= s < s0 + 4:
                        norm_qk(A, ch, s - s0, zr, k)
                return step

            out_slots(Count(58), Count(8), 4, norm_step(att, Straight, Count(6), 0, Count(1)))
            out_slots(Count(66), Count(12), 4)
            slots(Count(74), 24, att_slots(att, Count(0), 0, False, 0, pen))
            out_slots(Count(98), Count(19), 4, norm_step(att, Straight, Count(17), 0, Count(2)))
            step = att_slots(att, Count(4), 4, False, 0, pen)
            for s in range(24):
                step(s)
            out_slots(Count(106), Count(23), 4)

            rms_rows(1)
            v.wait_ge(used, FFN_0)
            link(V.memset(up[:, :, :, 0:2], 0.0))
            g = Count(FFN_0)
            first_block(1, g)
            slots(g.plus(8), 8)

            def ffn_slots(pair):
                def tile(f):
                    return Count(pair.base * 4 + f, pair.per * 4, pair.i)

                def tap(a, f, j):
                    c = pair.at(0, 4) + (a * D_FF // P + f)
                    return cols[:, j, bass.ds(c, 1)]

                def step(s):
                    if s % 2 == 0 and 0 < s < 10:
                        f = s // 2 - 1
                        n, b = tile(f), f % 2
                        v.wait_ge(u_hi, n.at(1))
                        V.tensor_tensor(y_lo[:, f, :], act_t[:, b, :], y_hi[:, f, :], ALU.subtract).then_inc(u_lo, 1)
                    if s % 2 == 0 and s < 8:
                        f = s // 2
                        n, b = tile(f), f % 2
                        v.wait_ge(u_aff, n.at(1))
                        for a in range(2):
                            done = V.scalar_tensor_tensor(cg2[:, b, a, :], up[:, b, a, 1:S + 1], tap(a, f, 1),
                                                          cg[:, b, a, :], ALU.mult, ALU.add)
                        done.then_inc(u_c1, 1)
                        v.wait_ge(u_c1, n.at(1))
                        for a in range(2):
                            done = V.scalar_tensor_tensor(cg3[:, b, a, :], up[:, b, a, 0:S], tap(a, f, 0),
                                                          cg2[:, b, a, :], ALU.mult, ALU.add)
                        done.then_inc(u_conv, 1)
                    if s % 2 == 1 and s < 9:
                        f = s // 2
                        n, b = tile(f), f % 2
                        v.wait_ge(u_tanh, n.at(1))
                        if n.plus(-1).some():
                            v.wait_ge(u_hi, n.at(-1 if f else 0))
                        V.scalar_tensor_tensor(act_r[:, b, :], th[:, b, :], 1.0, cg3[:, b, 0, :], ALU.add, ALU.mult)\
                            .then_inc(u_r, 1)
                        v.wait_ge(u_r, n.at(1))
                        V.scalar_tensor_tensor(act_t[:, b, :], act_r[:, b, :], 0.5, cg3[:, b, 1, :], ALU.mult, ALU.mult)\
                            .then_inc(u_act, 1)
                return step

            per = FFN_IN + FFN_OUT
            with v.Fori(1, PAIRS) as i:
                g = Count(FFN_0 + FFN_IN - per, per, i)
                slots(g, 16, ffn_slots(Count(-1, 1, i)))
                out_slots(g.plus(16), Count(FFN_B + 4 - 6, 6, i), 4)
            step = ffn_slots(Count(PAIRS - 1))
            for s in range(16):
                step(s)
            out_slots(Count(FOX_0 - FFN_OUT), Count(FOX_B - 4), 4)

            V.memset(small[:, 0:1], 0.0).then_inc(xn_ready, 1)
            g = Count(FOX_0)
            first_block(2, g)
            v.wait_ge(xt_mm, 24)
            for t in range(TOK):
                done = V.tensor_scalar(res[:, t, :], res[:, t, :], ALPHA, None, ALU.mult)
            done.then_inc(scaled, 1)
            v.wait_ge(scaled, 1)
            slots(g.plus(8), 1)
            v.wait_ge(used, FOX_0 + 9)
            v.wait_ge(c_full, 16 * 14)
            par = (FOX_B + 1) % 2
            for t in range(TOK):
                done = V.tensor_tensor(fz[:, 0, t, :], acc[par][t][:, 0:FOX_HEADS], bfb[:], ALU.add)
            done.then_inc(drained[par], 1)
            v.wait_ge(drained[par], (FOX_B + 1) // 2 + 1)

            def forget(s):
                if s == 10:
                    v.wait_ge(f_log, 1)
                    V.scalar_tensor_tensor(fz[:, 3, :, :], fz[:, 0, :, :], 0.0, fz[:, 2, :, :], ALU.min, ALU.subtract)\
                        .then_inc(f_lf, 1)
                if s == 12:
                    v.wait_ge(f_mm, 1)
                    V.tensor_copy(c_nat[:], M[0][:, 0:TOK * FOX_HEADS])
                    V.tensor_copy(cT, M[1][0:FOX_HEADS, 0:S]).then_inc(f_sb, 1)
                    v.wait_ge(f_sb, 1)

            def norm_gate(A, group, zr):
                ch = Chain(fox_norm, group, NORM_LINKS)

                def step(s):
                    if 24 <= s < 28:
                        norm_qk(A, ch, s - 24, zr, group.plus(4))
                return step

            ng = norm_gate(fox, Count(0), Count(FOX_B + 2))
            slots(g.plus(9), 24, lambda s: (forget(s + 8), ng(s + 8)))

            def gate(t_sem, g_sem, zb, n):
                v.wait_ge(t_sem, n)
                t = z[:, zb, :, :].rearrange("p t c -> p (t c)")
                V.scalar_tensor_tensor(t, tmp[:, 0:TOK * COL], 1.0, t, ALU.add, ALU.mult).then_inc(g_sem, 1)
                v.wait_ge(g_sem, n)

            gate(fox.tanh, fox.gated, 3, 1)
            per = FOX_IN + FOX_OUT
            with v.Fori(1, FOX_GROUPS) as i:
                g = Count(FOX_0 + 1 + FOX_IN - per, per, i)
                st = att_slots(fox, Count(-4, 4, i), 0, True, i * 4 - 4, causal)
                ng = norm_gate(fox, Count(0, 1, i), Count(FOX_B + 6 - 8, 8, i))
                slots(g, 32, lambda s: (st(s), ng(s)))
                gate(fox.tanh, fox.gated, 3, i + 1)
                out_slots(g.plus(32), Count(FOX_B + 9 - 8, 8, i), 4)
            st = att_slots(fox, Count(12), 0, True, 12, causal)
            for s in range(24):
                st(s)
            out_slots(Count(RET_0 - FOX_OUT), Count(RET_B - 4), 4)
            layer_norm(0)

            def rotate(group, zr):
                ch = Chain(r_rot_chain, group, 3)

                def step(s):
                    if not 24 <= s < 26:
                        return
                    t = s - 24
                    if t == 0:
                        block_out(v, zr)
                    m = rp.rearrange("p (x a h c) -> p x a h c", x=4, a=2, h=2)
                    for a in range(2):
                        src = z[:, a, t, :].rearrange("p (h f c) -> p h f c", h=2, f=2)
                        cos = rot[:, 0, t:t + 1, :].to_broadcast([P, 2, P])
                        sin = rot[:, 1, t:t + 1, :].to_broadcast([P, 2, P])
                        V.tensor_tensor(m[:, 0, a], src[:, :, 0, :], cos, ALU.mult)
                        V.tensor_tensor(m[:, 1, a], src[:, :, 1, :], sin, ALU.mult)
                        V.tensor_tensor(m[:, 2, a], src[:, :, 0, :], sin, ALU.mult)
                        done = V.tensor_tensor(m[:, 3, a], src[:, :, 1, :], cos, ALU.mult)
                    ch.link(done)
                    for a in range(2):
                        dst = qk[:, t, 4 * a:4 * a + 4, :].rearrange("p (h f) c -> p h f c", h=2)
                        V.tensor_tensor(dst[:, :, 0, :], m[:, 0, a], m[:, 1, a], ALU.subtract)
                        done = V.tensor_tensor(dst[:, :, 1, :], m[:, 2, a], m[:, 3, a], ALU.add)
                    if t == 0:
                        ch.link(done)
                    else:
                        done.then_inc(r_rot, 1)
                        v.wait_ge(r_rot, group.at(1))
                return step

            def ret_slots(n, head0):
                def step(s):
                    h = s // 10
                    if h >= RET_PAIR:
                        return
                    m = n.plus(h)
                    if s % 10 == 2:
                        v.wait_ge(r_s_mm, m.at(1))
                        if m.some():
                            v.wait_ge(r_o_mm, m.at())
                        V.tensor_tensor(s_sb[:], M[2][:, 0:3 * P], table[:, bass.ds((head0 + h) * (3 * P), 3 * P)], ALU.mult)\
                            .then_inc(r_st, 1)
                    elif s % 10 == 4:
                        v.wait_ge(r_o_mm, m.at(1))
                        if m.some():
                            v.wait_ge(r_y, m.at())
                        ch = Chain(r_chain, m, 1)
                        for t in range(TOK):
                            done = V.bn_stats(stats[:, t, 0, :], M[t][:])
                        ch.link(done)
                        V.memset(small[:, 3:4], 0.0)
                        for t in range(TOK):
                            done = V.bn_aggr(mv[:, t, :], stats[:, t, 0, :])
                        power(m.plus(W_RET), done)
                        for t in range(TOK):
                            done = V.scalar_tensor_tensor(tmp[:, (2 + t) * COL:(3 + t) * COL], M[t][:], mv[:, t, 0:1],
                                                          z[:, 4 + h, t, :], ALU.subtract, ALU.mult)
                        done.then_inc(r_t, 1)
                    elif s % 10 == 7:
                        v.wait_ge(r_hi, m.at(1))
                        for k in range(2):
                            t = 4 * h + 2 * k
                            done = V.scalar_tensor_tensor(y_lo[:, t:t + 2, :].rearrange("p k s -> p (k s)"), M[2 + k][:], 0.5,
                                                          y_hi[:, t:t + 2, :].rearrange("p k s -> p (k s)"),
                                                          ALU.mult, ALU.subtract)
                        done.then_inc(r_lo, 1)
                return step

            v.wait_ge(dec_full, 16)
            g = Count(RET_0)
            first_block(3, g)
            v.wait_ge(xt_mm, 32)
            for t in range(TOK):
                done = V.tensor_scalar(res[:, t, :], res[:, t, :], ALPHA, None, ALU.mult)
            done.then_inc(scaled, 1)
            v.wait_ge(scaled, 2)
            st = rotate(Count(0), Count(RET_B + 1))
            slots(g.plus(8), 32, st, 8)
            gate(r_tanh, r_gated, 4, 1)
            slots(g.plus(40), 8, st, 40)
            gate(r_tanh, r_gated, 5, 2)
            per = RET_IN + RET_OUT
            with v.Fori(1, RET_GROUPS) as i:
                g = Count(RET_0 + RET_IN - per, per, i)
                st = ret_slots(Count(-2, 2, i), i * 2 - 2)
                ro = rotate(Count(0, 1, i), Count(RET_B + 7 - 10, 10, i))
                slots(g, 40, lambda s: (st(s), ro(s)))
                gate(r_tanh, r_gated, 4, i * 2 + 1)
                slots(g.plus(40), 8, st, 40)
                gate(r_tanh, r_gated, 5, i * 2 + 2)
                out_slots(g.plus(48), Count(RET_B + 12 - 10, 10, i), 8)
            st = ret_slots(Count(RET_HEADS - 2), RET_HEADS - 2)
            for s in range(20):
                st(s)
            out_slots(Count(TOTAL - RET_OUT), Count(RET_B + 10 * RET_GROUPS - 4), 8)
            layer_norm(1)


NAMES = ["x", "attn_norm_g", "w_in", "pool_w", "pool_scale", "q_norm_g", "k_norm_g", "w_out",
         "ffn_norm_g", "w_up", "conv_w", "conv_b", "w_down", "fox_w_in_2", "fox_b_f_2", "fox_q_gain_2",
         "fox_k_gain_2", "fox_w_out_2", "ret_w_in_2", "ret_w_out_2", "ln_gain_2", "ln_bias_2"]


def kernel(**inputs):
    import concourse.bacc as bacc
    from concourse.bass_utils import run_bass_kernel_spmd

    nc = bacc.Bacc("TRN2", target_bir_lowering=False, num_devices=1)
    arrays, args = {}, []
    for name in NAMES:
        arrays[f"in_{name}"] = np.ascontiguousarray(inputs[name])
    arrays.update({f"const_{k}": a for k, a in constants().items()})
    for name, a in arrays.items():
        args.append(nc.dram_tensor(name, a.shape, mybir.dt.from_np(a.dtype), kind="ExternalInput").ap())
    args.append(nc.dram_tensor("y", (1, S, D), F32, kind="ExternalOutput").ap())
    mixers_kernel(nc, *args)
    r = run_bass_kernel_spmd(nc, [arrays], core_ids=[0])
    return r.results[0]["y"]
```

```python
import numpy as np
import concourse.bass as bass
from concourse import mybir
from contextlib import ExitStack

F32 = mybir.dt.float32
F32R = mybir.dt.float32r
ALU = mybir.AluOpType
ACT = mybir.ActivationFunctionType
AX = mybir.AxisListType.X

P = 128
S = 256
TOK = S // P
D = 2048
KT = D // P
COL = 512
KC = 2
CH = KT // KC
NOUT = D // COL
HD = 128
EPS = 1e-6
LN_EPS = 1e-5
GN_EPS = 1e-6
NEG = -1e30
TAKEN = -3e38

D_POOL = 1024
POOL_W = (2, 4, 8, 16)
IDX_HEADS, IDX_DIM = 16, 64
TOPK = 64
ATT_HEADS = 8
D_IN = 5200
C_Q, C_K, C_V, C_QI, C_KI = 1024, 2048, 3072, 4096, 5120
NARROW = IDX_DIM + IDX_HEADS
NARROW_K = 8
D_FF = 5632
PAIRS = D_FF // COL
FOX_HEADS = 16
GROUP = 4
FOX_GROUPS = FOX_HEADS // GROUP
RET_HEADS, RET_QK, RET_V = 8, 256, 512
RET_PAIR = 2
RET_GROUPS = RET_HEADS // RET_PAIR
ALPHA = (2.0 * 2) ** 0.25

RAW = 4
SPLIT = 4
LEAD = SPLIT - 1
STRIDE, TAIL_STRIDE = 5, 3
TAIL = 3 * TAIL_STRIDE + 6
HALF_AT = 9
RET_STRIDE, RET_TAIL_STRIDE = 10, 8

L1_CHUNKS = 16 + 2 + 16 + 24 + 16 + 24 + 8 + 8
L1_BLOCKS = 2 + 1 + 2 + 3 + 8 + 3 + 4 + 8
FFN_IN, FFN_OUT = 2 * CH, NOUT * 2
FOX_IN, FOX_OUT = 4 * CH, NOUT * 2
RET_IN, RET_OUT = 6 * CH, NOUT * 4
FFN_0 = L1_CHUNKS
FOX_0 = FFN_0 + PAIRS * (FFN_IN + FFN_OUT)
RET_0 = FOX_0 + 1 + FOX_GROUPS * (FOX_IN + FOX_OUT)
TOTAL = RET_0 + RET_GROUPS * (RET_IN + RET_OUT)
FFN_B = L1_BLOCKS
FOX_B = FFN_B + PAIRS * 6
RET_B = FOX_B + 1 + FOX_GROUPS * 8 + 4


class Count:

    def __init__(self, base, per=0, i=None):
        self.base, self.per, self.i = base, per, i

    def at(self, k=0, times=1):
        v = (self.base + k) * times
        return v if self.i is None else self.i * (self.per * times) + v

    def plus(self, k):
        return Count(self.base + k, self.per, self.i)

    def over(self, n):
        return Count(self.base // n, self.per // n, self.i)

    def some(self):
        return self.i is not None or self.base > 0


def constants():
    pen = np.zeros((P, 3 * P), np.float32)
    upper = np.where(np.arange(P)[None, :] <= np.arange(P)[:, None], 0.0, NEG).astype(np.float32)
    pen[:, 0:P] = upper
    pen[:, 2 * P:3 * P] = upper
    pool = np.zeros((len(POOL_W), S, S), np.float32)
    for g, w in enumerate(POOL_W):
        for q in range(S):
            lo = max(q + 1 - w, 0)
            pool[g, lo:q + 1, q] = 1.0 / (q + 1 - lo)
            pool[g, q, q] -= 1.0
    packed = np.concatenate([pool[:, 0:P, :], pool[:, P:S, P:S]], axis=2).transpose(1, 0, 2)
    inv = 10000.0 ** (-np.arange(0, RET_QK, 2, dtype=np.float32) / RET_QK)
    ang = (np.arange(S, dtype=np.float32)[:, None] * inv.astype(np.float32)[None, :]).astype(np.float32)
    rot = np.stack([np.cos(ang), np.sin(ang)]).astype(np.float32)
    rot = rot.reshape(2, TOK, P, P).transpose(2, 0, 1, 3)
    lg = np.log1p(-np.exp2(-5.0 - np.arange(RET_HEADS, dtype=np.float64)))
    diff = (np.arange(S)[None, :] - np.arange(S)[:, None]).astype(np.float64)
    dec = np.where(diff >= 0, np.exp(np.maximum(diff, 0)[None] * lg[:, None, None]), 0.0) * RET_QK ** -0.5
    dec = np.concatenate([dec[:, 0:P, :], dec[:, P:S, P:S]], axis=2).transpose(1, 0, 2)
    return {
        "ident": np.eye(P, dtype=np.float32),
        "causal": pen,
        "poolband": np.ascontiguousarray(packed.reshape(P, -1), dtype=np.float32),
        "rotary": np.ascontiguousarray(rot.reshape(P, -1), dtype=np.float32),
        "decay": np.ascontiguousarray(dec.reshape(P, -1), dtype=np.float32),
    }


def mixers_kernel(nc, x, attn_norm_g, w_in, pool_w, pool_scale, q_norm_g, k_norm_g, w_out,
                  ffn_norm_g, w_up, conv_w, conv_b, w_down, fox_w_in, fox_b_f, fox_q_gain,
                  fox_k_gain, fox_w_out, ret_w_in, ret_w_out, ln_gain, ln_bias,
                  ident_d, causal_d, poolband_d, rotary_d, decay_d, out):
    ctx = ExitStack()
    with ctx:
        def sb(name, shape, dt=F32):
            return ctx.enter_context(nc.sbuf_tensor(name, shape, dt))

        def sem(name):
            return ctx.enter_context(nc.semaphore(name))

        raw = sb("raw", [P, RAW, KC * COL])
        w_hi = sb("w_hi", [P, SPLIT, KC * COL], F32R)
        w_lo = sb("w_lo", [P, SPLIT, KC * COL], F32R)
        x_hi = sb("x_hi", [P, KT, S], F32R)
        x_lo = sb("x_lo", [P, KT, S], F32R)
        y_hi = sb("y_hi", [P, 8, S], F32R)
        y_lo = sb("y_lo", [P, 8, S], F32R)
        res = sb("res", [P, TOK, D])
        z = sb("z", [P, 6, TOK, COL])
        squares_out = z[:, 0:4, :, :].rearrange("p b t c -> p (b t c)").rearrange("p (t d) -> p t d", t=TOK)
        qk = sb("qk", [P, TOK, 8, HD])
        tmp = sb("tmp", [P, 4 * COL])
        qT = sb("qT", [P, 2, S])
        kT = sb("kT", [P, 2, S])
        s_sb = sb("s_sb", [P, 3 * P])
        heads = sb("heads", [P, 2 * COL])
        y_sb = heads[:].rearrange("p (t c) -> p t c", t=TOK)
        y_att = heads[:, 0:S].rearrange("p (t c) -> p t c", t=TOK)
        p_sb = heads[:, S:S + 3 * P]
        pT = heads[:, S + 3 * P:S + 6 * P]
        pen = sb("pen", [P, 3 * P])
        top8 = sb("top8", [P, 2, 8])
        w_idx = sb("w_idx", [P, TOK, IDX_HEADS])
        ident = sb("ident_sb", [P, P])
        causal = sb("causal_sb", [P, 3 * P])
        ones = sb("ones", [P, P])
        rot = sb("rot", [P, 2, TOK, P])
        cols = sb("cols", [P, 4, P])
        gains = sb("gains", [P, 80])
        small = sb("small", [P, 4])
        pconst = sb("pconst", [P, 4])
        ssq = sb("ssq", [P, 16])
        rstd = sb("rstd", [P, 16])
        nmax = sb("nmax", [P, TOK])
        sums = sb("sums", [P, TOK])
        rinv = sb("rinv", [P, TOK])
        rs = sb("rs", [P, TOK])
        bfc = sb("bfc", [FOX_HEADS, 1])
        tq = heads[:].rearrange("p (b c) -> p b c", b=2)
        c_nat = sb("c_nat", [P, TOK * FOX_HEADS])
        cT = qT[0:FOX_HEADS, 1, :]
        ckT = kT[0:FOX_HEADS, 1, :]
        minus = sb("minus", [FOX_HEADS, P])
        stats = sb("stats", [P, TOK, 4, 6])
        mv = sb("mv", [P, TOK, 2])
        spare = z[:, 4:6, :, :].rearrange("p b t c -> p (b t c)")
        rows = spare[:, 0:4 * P].rearrange("p (r c) -> p r c", r=4)
        kwT, wT, diag, rbc = (spare[:, (2 + k) * S:(3 + k) * S] for k in range(4))
        fT = spare[0:FOX_HEADS, 0:5 * S].rearrange("p (a s) -> p a s", a=5)
        table = sb("table", [P, RET_HEADS * 3 * P])
        band = table[:, 0:4 * 3 * P]
        rel = table[:, 12 * P:18 * P].rearrange("p (b c) -> p b c", b=2)
        isc = table[:, 18 * P:21 * P]
        kiT = table[:, 21 * P:23 * P]
        arena = sb("arena", [P, 6144])

        def part(at, *shape):
            n = int(np.prod(shape))
            names = "abc"[:len(shape)]
            kw = dict(zip(names, shape))
            return arena[:, at:at + n].rearrange(f"p ({' '.join(names)}) -> p {' '.join(names)}", **kw)

        qiT, poolT, pw = part(0, 8, S), part(2048, 8, S), part(4096, 8, 256)
        up = part(0, 2, 2, S + 2)
        cg, cg2, cg3 = part(1032, 2, 2, S), part(2056, 2, 2, S), part(3080, 2, 2, S)
        th, act_t, act_r = part(4104, 2, S), part(4616, 2, S), part(5128, 2, S)
        gbc = part(0, 2, D)
        rp = arena[:, 4096:6144]

        acc = [[ctx.enter_context(nc.psum_tensor(f"acc{b}{t}", [P, COL], F32)) for t in range(TOK)]
               for b in range(2)]
        M = [ctx.enter_context(nc.psum_tensor(f"mix{b}", [P, COL], F32)) for b in range(4)]

        G_ATT, G_FFN, G_POOL, G_Q, G_K, G_FQ, G_FK, G_LG, G_LB = 0, 16, 32, 40, 41, 42, 43, 44, 60

        raw_full = [sem(f"raw_full{k}") for k in range(RAW)]
        hi_done, lo_done = sem("hi_done"), sem("lo_done")
        used = sem("used")
        drained = [sem("drained0"), sem("drained1")]
        x_full, c_full = sem("x_full"), sem("c_full")
        v_full, b_full = sem("v_full"), sem("b_full")
        xn_ready = sem("xn_ready")
        ssq_done = sem("ssq_done")
        xt_mm, xt_hi, xt_lo = sem("xt_mm"), sem("xt_hi"), sem("xt_lo")
        vec_mm, vec_sb = sem("vec_mm"), sem("vec_sb")
        dve = sem("dve_chain")
        dve_n = [0]
        idx_mm, idx_sb = sem("idx_mm"), sem("idx_sb")
        rel_mm, rel_sb, rel_add = sem("rel_mm"), sem("rel_sb"), sem("rel_add")
        d_full, rbc_mm, rbc_sb, ki_part, ki_full, w_full = (sem(n) for n in (
            "diag_full", "rbc_mm", "rbc_sb", "ki_part", "ki_full", "w_full"))
        xt_aff, ln_used = sem("xt_aff"), sem("ln_used")
        c_ready, out_ready = sem("c_ready"), [sem(f"out_ready{t}") for t in range(TOK)]
        pd_mm, pd_sb, py_mm, py_hi, py_lo = (sem(n) for n in ("pd_mm", "pd_sb", "py_mm", "py_hi", "py_lo"))
        out_sem = sem("out_sem")
        f_abs, f_exp, f_log, f_lf, f_mm, f_sb = (sem(n) for n in (
            "f_abs", "f_exp", "f_log", "f_lf", "f_mm", "f_sb"))
        want, got, added, pc = sem("power_want"), sem("power_got"), sem("power_added"), sem("power_const")
        W_RET = 4 + FOX_GROUPS + 1

        class Att:

            def __init__(self, p):
                self.normed = sem(p + "normed")
                self.gated = sem(p + "gated")
                self.tanh = sem(p + "tanh")
                self.chain = sem(p + "chain")
                self.qk_mm, self.qk_sb = sem(p + "qk_mm"), sem(p + "qk_sb")
                self.ck = sem(p + "ck")
                self.s_mm, self.maxed, self.exped = sem(p + "s_mm"), sem(p + "maxed"), sem(p + "exped")
                self.p_mm, self.p_sb = sem(p + "p_mm"), sem(p + "p_sb")
                self.o_mm, self.y_sb = sem(p + "o_mm"), sem(p + "y_sb")
                self.y_mm, self.y_hi, self.y_lo = sem(p + "y_mm"), sem(p + "y_hi"), sem(p + "y_lo")

        att, fox = Att("att_"), Att("fox_")
        r_rot, r_gated, r_tanh = sem("r_rot"), sem("r_gated"), sem("r_tanh")
        r_chain, r_rot_chain, fox_norm = sem("r_chain"), sem("r_rot_chain"), sem("fox_norm")
        dec_full, ln_full = sem("dec_full"), sem("ln_full")
        r_qk_mm, r_qk_sb, r_s_mm, r_st, r_o_mm = (sem("r_" + n) for n in ("qk_mm", "qk_sb", "s_mm", "st", "o_mm"))
        r_t, r_y, r_y_mm, r_hi, r_lo = (sem("r_" + n) for n in ("t", "y", "y_mm", "hi", "lo"))
        u_mm, u_aff, u_c1, u_conv, u_tanh, u_r, u_act, u_hi, u_lo = (sem("u_" + n) for n in (
            "mm", "aff", "c1", "conv", "tanh", "r", "act", "hi", "lo"))

        def tiles(w):
            return w.rearrange("(k p) c -> p k c", p=P)

        w_in_v, w_out_v, w_up_v, w_down_v = tiles(w_in), tiles(w_out), tiles(w_up), tiles(w_down)
        fox_in_v, fox_out_v = tiles(fox_w_in[0]), tiles(fox_w_out[0])
        ret_in_v, ret_out_v = tiles(ret_w_in[0]), tiles(ret_w_out[0])

        def block_out(eng, blk):
            eng.wait_ge(drained[blk.base % 2], blk.plus(2).over(2).at())

        def all_out(eng, blk):
            eng.wait_ge(drained[0], blk.plus(1).over(2).at())
            eng.wait_ge(drained[1], blk.over(2).at())

        block = ctx.enter_context(nc.Block())

        @block.sync
        def _(sp):
            def chunk(g, src, kk=KC, n=COL):
                if g.base >= RAW or g.i is not None:
                    sp.wait_ge(lo_done, g.at(1 - RAW))
                slot = g.base % RAW
                sp.dma_start(raw[:, slot, 0:kk * n].rearrange("p (k c) -> p k c", k=kk), src)\
                    .then_inc(raw_full[slot], 16)

            def in_block(g, w_v, c0, n=COL, kk=KC):
                for c in range(KT // kk):
                    chunk(g.plus(c), w_v[:, c * kk:(c + 1) * kk, bass.ds(c0, n)], kk, n)
                return g.plus(KT // kk)

            def out_blocks(g, w_v, k0, kt):
                for n in range(NOUT):
                    for c in range(kt // KC):
                        chunk(g.plus(n * (kt // KC) + c),
                              w_v[:, bass.ds(k0 + c * KC, KC), n * COL:(n + 1) * COL])
                return g.plus(NOUT * kt // KC)

            sp.dma_start(res[:, 0, :], x[0, 0:P, :]).then_inc(x_full, 16)
            sp.dma_start(res[:, 1, :], x[0, P:S, :]).then_inc(x_full, 16)
            g = Count(0)
            g = in_block(g, w_in_v, C_QI)
            g = in_block(g, w_in_v, C_QI + COL)
            g = in_block(g, w_in_v, C_KI, NARROW, NARROW_K)
            g = in_block(g, w_in_v, 0)
            g = in_block(g, w_in_v, COL)
            for c in (C_Q, C_K, C_V):
                g = in_block(g, w_in_v, c)
            g = out_blocks(g, w_out_v, 0, 4)
            g = out_blocks(g, w_out_v, 4, 4)
            for c in (C_Q, C_K, C_V):
                g = in_block(g, w_in_v, c + COL)
            g = out_blocks(g, w_out_v, 8, 4)
            g = out_blocks(g, w_out_v, 12, 2)
            g = out_blocks(g, w_out_v, 14, 2)
            assert g.base == FFN_0

            def ffn_in(g, i):
                g = in_block(g, w_up_v, i * COL)
                return in_block(g, w_up_v, i * COL + D_FF)

            per = FFN_IN + FFN_OUT
            ffn_in(g, 0)
            with sp.Fori(1, PAIRS) as i:
                g = ffn_in(Count(FFN_0 + FFN_IN - per, per, i), i)
                out_blocks(g, w_down_v, i * 4 - 4, 4)
            out_blocks(Count(FOX_0 - FFN_OUT), w_down_v, 4 * PAIRS - 4, 4)

            g = in_block(Count(FOX_0), fox_in_v, 0)
            g = in_block(g, fox_in_v, 4 * D, FOX_HEADS, KT)
            for b in range(1, 4):
                g = in_block(g, fox_in_v, b * D)
            per = FOX_IN + FOX_OUT
            with sp.Fori(1, FOX_GROUPS) as i:
                g = Count(FOX_0 + 1 + FOX_IN - per, per, i)
                for b in range(4):
                    g = in_block(g, fox_in_v, i * COL + b * D)
                out_blocks(g, fox_out_v, i * 4 - 4, 4)
            for half in range(2):
                out_blocks(Count(RET_0 - FOX_OUT + 4 * half), fox_out_v, 4 * FOX_GROUPS - 4 + 2 * half, 2)

            def ret_in(g, i):
                g = in_block(g, ret_in_v, i * COL)
                g = in_block(g, ret_in_v, i * COL + D)
                for b in range(4):
                    g = in_block(g, ret_in_v, i * (2 * COL) + 2 * D + (b // 2) * 2 * D + (b % 2) * COL)
                return g

            per = RET_IN + RET_OUT
            ret_in(Count(RET_0), 0)
            with sp.Fori(1, RET_GROUPS) as i:
                g = ret_in(Count(RET_0 + RET_IN - per, per, i), i)
                out_blocks(g, ret_out_v, i * 8 - 8, 8)
            out_blocks(Count(TOTAL - RET_OUT), ret_out_v, 8 * RET_GROUPS - 8, 8)

            for t in range(TOK):
                sp.wait_ge(out_ready[t], 1)
                sp.dma_start(out[0, t * P:(t + 1) * P, :], res[:, t, :]).then_inc(out_sem, 16)
            sp.wait_ge(out_sem, 16 * TOK)

        @block.gpsimd
        def _(pool):
            def load(dst, src, s):
                pool.dma_start(dst, src).then_inc(s, 16)

            def power(k, o, i_, eps):
                pool.wait_ge(want, k.at(1))
                n = i_.shape[1]
                c = 0 if eps == EPS else 1
                nc.gpsimd.tensor_tensor(o, i_, pconst[:, c:c + 1].to_broadcast([P, n]), ALU.add).then_inc(added, 1)
                pool.wait_ge(added, k.at(1))
                nc.gpsimd.tensor_tensor(o, o, pconst[:, 2:3].to_broadcast([P, n]), ALU.pow).then_inc(got, 1)

            def rows_power(k):
                power(Count(k), rs[:], ssq[:, 0:TOK], EPS)

            def heads_power(k):
                power(k, rstd[:], ssq[:], EPS)

            def var_power(k, eps):
                power(k, rstd[:, 0:TOK], mv[:, :, 1], eps)

            nc.gpsimd.memset(pconst[:, 0:1], EPS)
            nc.gpsimd.memset(pconst[:, 1:2], LN_EPS)
            nc.gpsimd.memset(pconst[:, 2:3], -0.5).then_inc(pc, 1)
            pool.wait_ge(pc, 1)
            rows_power(0)
            load(causal[:], causal_d, c_full)
            load(band, poolband_d, c_full)
            load(pw, pool_w.rearrange("g (t p) d -> p (g t) d", p=P), c_full)
            load(rot[:].rearrange("p a t c -> p (a t c)"), rotary_d, c_full)
            load(bfc[:], fox_b_f.rearrange("a h -> h a"), c_full)
            pool.wait_ge(vec_sb, 1)
            for j in range(3):
                load(rows[0:2 * D_FF // P, j, :], conv_w[j].rearrange("(j p) -> j p", p=P), b_full)
            load(rows[0:2 * D_FF // P, 3, :], conv_b.rearrange("(j p) -> j p", p=P), b_full)
            pool.wait_ge(drained[0], 2)
            load(wT[0:IDX_HEADS, :], kwT[64:64 + IDX_HEADS, :], w_full)
            pool.wait_ge(ki_part, 1)
            load(kiT[64:128, :], kiT[0:64, :], ki_full)
            pool.wait_ge(py_lo, 8)
            load(table[:], decay_d, dec_full)
            heads_power(Count(1))
            heads_power(Count(2))
            rows_power(3)
            all_out(pool, Count(FOX_B))
            load(gbc[:, 0, :], ln_gain[0:1, :].to_broadcast([P, D]), ln_full)
            load(gbc[:, 1, :], ln_bias[0:1, :].to_broadcast([P, D]), ln_full)
            heads_power(Count(4))
            with pool.Fori(1, FOX_GROUPS) as i:
                heads_power(Count(4, 1, i))
            var_power(Count(W_RET - 1), LN_EPS)
            pool.wait_ge(ln_used, 1)
            load(gbc[:, 0, :], ln_gain[1:2, :].to_broadcast([P, D]), ln_full)
            load(gbc[:, 1, :], ln_bias[1:2, :].to_broadcast([P, D]), ln_full)
            with pool.Fori(1, RET_GROUPS) as i:
                for h in range(RET_PAIR):
                    var_power(Count(W_RET - 2 + h, 2, i), GN_EPS)
            for h in range(RET_PAIR):
                var_power(Count(W_RET + RET_HEADS - 2 + h), GN_EPS)
            var_power(Count(W_RET + RET_HEADS), LN_EPS)

        @block.tensor
        def _(pe):
            def mm(o, l, r, start, stop):
                return nc.tensor.matmul(o, l, r, start=start, stop=stop)

            def chunk(g, b, lhs_hi, lhs_lo, k0, first, last, kk=KC, n=COL):
                pe.wait_ge(lo_done, g.at(1))
                slot = g.base % SPLIT
                for k in range(kk):
                    wh = w_hi[:, slot, k * n:(k + 1) * n]
                    wl = w_lo[:, slot, k * n:(k + 1) * n]
                    for t in range(TOK):
                        xh = lhs_hi[:, k0 + k, t * P:(t + 1) * P]
                        xl = lhs_lo[:, k0 + k, t * P:(t + 1) * P]
                        o = acc[b][t][:, 0:n]
                        mm(o, xh, wh, first and k == 0, False)
                        mm(o, xh, wl, False, False)
                        done = mm(o, xl, wh, False, last and k == kk - 1)
                done.then_inc(used, 1)

            def in_block(g, blk, step, slot, n=COL, kk=KC, build=None, hook=True):
                par = blk.base % 2
                if blk.plus(-1).some():
                    pe.wait_ge(drained[par], blk.over(2).at())
                for c in range(KT // kk):
                    if build is not None:
                        pe.wait_ge(xt_lo, 8 * build + c + 1)
                    chunk(g.plus(c), par, x_hi, x_lo, c * kk, c == 0, c == KT // kk - 1, kk, n)
                    if build is not None and c + 4 < 8:
                        xt(build, c + 4)
                    step(slot + c)

            def out_slot(g, blk, y0, kt, s, y=(y_hi, y_lo)):
                per = kt // KC
                nb, c = s // per, s % per
                par = (blk.base + nb) % 2
                if c == 0:
                    pe.wait_ge(drained[par], blk.plus(nb).over(2).at())
                chunk(g.plus(s), par, *y, y0 + c * KC, c == 0, c == per - 1)

            def out_blocks(g, blk, y0, kt, step, slot, y=(y_hi, y_lo)):
                for s in range(NOUT * kt // KC):
                    out_slot(g, blk, y0, kt, s, y)
                    step(slot + s)

            def xt(phase, j):
                if j >= 4:
                    pe.wait_ge(xt_lo, 8 * phase + j - 3)
                for k in range(2):
                    for t in range(TOK):
                        c = k * S + t * P
                        done = nc.tensor.transpose(M[j % 4][:, c:c + P],
                                                   res[:, t, (2 * j + k) * P:(2 * j + k + 1) * P], ident[:])
                done.then_inc(xt_mm, 1)

            def xt_start(phase):
                for j in range(4):
                    xt(phase, j)

            def narrow_block(g, blk, n, kk):
                par = blk.base % 2
                all_out(pe, blk)
                o = acc[par][0][:, 0:S]
                for c in range(KT // kk):
                    pe.wait_ge(lo_done, g.at(c + 1))
                    slot = (g.base + c) % SPLIT
                    for k in range(kk):
                        wh, wl = w_hi[:, slot, k * n:k * n + P], w_lo[:, slot, k * n:k * n + P]
                        t = c * kk + k
                        mm(o, wh, x_hi[:, t, :], t == 0, False)
                        mm(o, wl, x_hi[:, t, :], False, False)
                        done = mm(o, wh, x_lo[:, t, :], False, t == KT - 1)
                    done.then_inc(used, 1)

            none = lambda s: None

            def att_step(A, what, n, h, group, forget, blk0):
                if what == "T":
                    if h == 0:
                        all_out(pe, blk0)
                    pe.wait_ge(A.normed, group.at(1))
                    if n.some():
                        pe.wait_ge(A.qk_sb, n.at())
                    for a in range(2):
                        for t in range(TOK):
                            c = a * S + t * P
                            done = nc.tensor.transpose(M[0][:, c:c + P], qk[:, t, a * GROUP + h, :], ident[:])
                    done.then_inc(A.qk_mm, 1)
                elif what == "S":
                    pe.wait_ge(A.qk_sb, n.at(1))
                    if n.some():
                        pe.wait_ge(A.maxed, n.at())
                    if forget:
                        pe.wait_ge(A.ck, n.at(1))
                    for t in range(TOK):
                        o = M[1][:, t * P:(1 + 2 * t) * P]
                        keys = (t + 1) * P
                        done = mm(o, qT[:, 0, t * P:(t + 1) * P], kT[:, 0, 0:keys], True, not forget)
                        if forget:
                            done = mm(o, minus[:], ckT[:, 0:keys], False, True)
                    done.then_inc(A.s_mm, 1)
                elif what == "PT":
                    pe.wait_ge(A.exped, n.at(1))
                    if n.some():
                        pe.wait_ge(A.p_sb, n.at())
                    for c in range(3):
                        done = nc.tensor.transpose(M[2][:, c * P:(c + 1) * P], p_sb[:, c * P:(c + 1) * P], ident[:])
                    done.then_inc(A.p_mm, 1)
                elif what == "V":
                    pe.wait_ge(A.p_sb, n.at(1))
                    if n.some():
                        pe.wait_ge(A.y_lo, n.at())
                    v = z[:, 2, :, h * HD:(h + 1) * HD]
                    mm(M[3][:, 0:P], pT[:, 0:P], v[:, 0, :], True, True)
                    mm(M[3][:, P:2 * P], pT[:, P:2 * P], v[:, 0, :], True, False)
                    mm(M[3][:, P:2 * P], pT[:, 2 * P:3 * P], v[:, 1, :], False, True).then_inc(A.o_mm, 1)
                elif what == "Y":
                    pe.wait_ge(A.y_sb, n.at(1))
                    for t in range(TOK):
                        done = nc.tensor.transpose(M[3][:, t * P:(t + 1) * P], y_att[:, t, :], ident[:])
                    done.then_inc(A.y_mm, 1)

            ATT_AT = {0: "T", 1: "S", 3: "PT", 4: "V", 5: "Y"}

            def att_slots(A, n, group, forget, blk0, stride=STRIDE):
                def step(s):
                    for h in range(GROUP):
                        if s - stride * h in ATT_AT:
                            att_step(A, ATT_AT[s - stride * h], n.plus(h), h, group, forget, blk0)
                return step

            def att_tail(g, blk, y0, step, y0_last, lo):
                for s in range(TAIL):
                    if s < 8:
                        out_slot(g, blk, y0, 4, s)
                    elif HALF_AT <= s < HALF_AT + 4:
                        if s == HALF_AT:
                            pe.wait_ge(lo[0], lo[1] - 2)
                        out_slot(g.plus(8), blk.plus(4), y0_last, 2, s - HALF_AT)
                    step(s)
                pe.wait_ge(*lo)
                out_blocks(g.plus(12), blk.plus(8), y0_last + 2, 2, none, 0)

            pe.wait_ge(v_full, 16 * 10)
            nc.tensor.transpose(M[0][:, 0:76], rows[0:76, 3, :], ident[0:76, 0:76]).then_inc(vec_mm, 1)
            pe.wait_ge(vec_sb, 1)

            def spread(s):
                if s == 10:
                    pe.wait_ge(d_full, 1)
                    pe.wait_ge(xt_lo, 8)
                    mm(M[0][:, 0:S], ones[:], diag, True, True).then_inc(rbc_mm, 1)

            pe.wait_ge(x_full, 32)
            xt_start(0)
            in_block(Count(0), Count(0), none, 0, build=0)
            in_block(Count(8), Count(1), spread, 8)
            narrow_block(Count(16), Count(2), NARROW, NARROW_K)

            def indexer(s):
                if s < 4:
                    if s == 0:
                        all_out(pe, Count(2))
                        pe.wait_ge(rbc_sb, 1)
                    for k in range(2):
                        for t in range(TOK):
                            f = (2 * s + k) * P
                            c = k * S + t * P
                            done = nc.tensor.transpose(
                                M[s][:, c:c + P], z[:, f // COL, t, f % COL:f % COL + P], ident[:])
                    done.then_inc(idx_mm, 1)
                elif s == 4:
                    pe.wait_ge(w_full, 16)
                    pe.wait_ge(idx_sb, 4)
                    for t in range(TOK):
                        done = nc.tensor.transpose(M[2][:, t * 16:(t + 1) * 16], wT[0:IDX_HEADS, t * P:(t + 1) * P],
                                                   ident[0:IDX_HEADS, 0:IDX_HEADS])
                    done.then_inc(idx_mm, 1)
                elif s < 16:
                    for h in range(min(16, 2 * (s - 5)), min(16, 2 * (s - 5) + 2)):
                        if h == 0:
                            pe.wait_ge(ki_full, 16)
                        else:
                            if h >= 2:
                                pe.wait_ge(rel_sb, h - 1)
                        half = slice(64 * (h % 2), 64 * (h % 2) + 64)
                        for t in range(TOK):
                            done = mm(M[h % 2][:, t * P:(1 + 2 * t) * P], qiT[half, h // 2, t * P:(t + 1) * P],
                                      kiT[half, 0:(t + 1) * P], True, True)
                        done.then_inc(rel_mm, 1)

            in_block(Count(18), Count(3), indexer, 0)
            in_block(Count(26), Count(4), indexer, 8)

            def pool_step(s):
                if s < 8:
                    b = s % 2
                    if s == 0:
                        all_out(pe, Count(5))
                        pe.wait_ge(c_full, 16 * 5)
                    if s >= 2:
                        pe.wait_ge(pd_sb, s - 1)
                    else:
                        pe.wait_ge(rel_sb, 16)
                    grp = s // 2
                    u = z[:, 2 + s // 4, :, (s % 4) * P:(s % 4 + 1) * P]
                    c = grp * 3 * P
                    o = M[2 + b]
                    mm(o[:, 0:S], u[:, 0, :], band[:, c:c + S], True, False)
                    mm(o[:, P:S], u[:, 1, :], band[:, c + S:c + 3 * P], False, True).then_inc(pd_mm, 1)
                elif s < 16:
                    t = s - 8
                    grp = t // 2
                    pe.wait_ge(pd_sb, 8)
                    if t >= 2:
                        pe.wait_ge(py_lo, t - 1)
                    for k in range(2):
                        done = mm(M[t % 2][:, 0:S], pw[:, 2 * grp + k, (t % 2) * P:(t % 2 + 1) * P],
                                  poolT[:, 2 * grp + k, :], k == 0, k == 1)
                    done.then_inc(py_mm, 1)

            for b in range(3):
                in_block(Count(34 + 8 * b), Count(5 + b), pool_step, 8 * b)
            pe.wait_ge(py_lo, 8)
            out_blocks(Count(58), Count(8), 0, 4, none, 0)
            out_blocks(Count(66), Count(12), 4, 4, none, 0)
            step = att_slots(att, Count(0), Count(0), False, Count(8))
            for b in range(3):
                in_block(Count(74 + 8 * b), Count(16 + b), step, 8 * b)
            pe.wait_ge(att.y_lo, 4)
            step = att_slots(att, Count(4), Count(1), False, Count(19), TAIL_STRIDE)
            att_tail(Count(98), Count(19), 0, step, 4, (att.y_lo, 8))

            pe.wait_ge(b_full, 16 * 4)
            n = 2 * D_FF // P
            for j in range(4):
                done = nc.tensor.transpose(M[0][:, j * P:j * P + n], rows[0:n, j, :], ident[0:n, 0:n])
            done.then_inc(vec_mm, 1)
            pe.wait_ge(vec_sb, 2)

            def ffn_slots(pair, blk0):
                def step(s):
                    if s % 2 == 0 and s < 8:
                        f = s // 2
                        n = Count(pair.base * 4 + f, pair.per * 4, pair.i)
                        if f == 0:
                            all_out(pe, blk0)
                        if pair.some():
                            pe.wait_ge(u_aff, pair.at(0, 4))
                        for a in range(2):
                            for t in range(TOK):
                                c = a * S + t * P
                                done = nc.tensor.transpose(M[f][:, c:c + P], z[:, a, t, f * P:(f + 1) * P], ident[:])
                        done.then_inc(u_mm, 1)
                return step

            all_out(pe, Count(FFN_B))
            xt_start(1)
            in_block(Count(FFN_0), Count(FFN_B), none, 0, build=1)
            in_block(Count(FFN_0 + 8), Count(FFN_B + 1), none, 8)
            per = FFN_IN + FFN_OUT
            def ffn_pair(i, last):
                g = Count(FFN_0 + FFN_IN - per, per, i) if not last else Count(FOX_0 - 2 * FFN_OUT - FFN_IN)
                blk = Count(FFN_B + 2 - 6, 6, i) if not last else Count(FOX_B - 10)
                pair = Count(-1, 1, i) if not last else Count(PAIRS - 2)
                step = ffn_slots(pair, blk)
                in_block(g, blk, step, 0)
                in_block(g.plus(8), blk.plus(1), step, 8)
                pe.wait_ge(u_lo, pair.at(1, 4))
                out_blocks(g.plus(16), blk.plus(2), 0, 4,
                           ffn_slots(Count(PAIRS - 1), blk.plus(2)) if last else none, 0)

            with pe.Fori(1, PAIRS - 1) as i:
                ffn_pair(i, False)
            ffn_pair(None, True)
            pe.wait_ge(u_lo, 4 * PAIRS)
            out_blocks(Count(FOX_0 - FFN_OUT), Count(FOX_B - 4), 4, 4, none, 0)

            def forget(s):
                if s == 11:
                    pe.wait_ge(c_ready, 1)
                    pe.wait_ge(xt_lo, 24)
                    for t in range(TOK):
                        done = nc.tensor.transpose(M[0][:, t * 16:(t + 1) * 16], cT[:, t * P:(t + 1) * P],
                                                   ident[0:FOX_HEADS, 0:FOX_HEADS])
                    done.then_inc(f_mm, 1)

            all_out(pe, Count(FOX_B))
            xt_start(2)
            in_block(Count(FOX_0), Count(FOX_B), none, 0, build=2)
            narrow_block(Count(FOX_0 + 8), Count(FOX_B + 1), FOX_HEADS, KT)
            for b in range(1, 4):
                in_block(Count(FOX_0 + 1 + 8 * b), Count(FOX_B + 1 + b), forget, 8 * b)
            per = FOX_IN + FOX_OUT
            def fox_group(i):
                last = i is None
                g = Count(FOX_0 + 1 + FOX_IN - per, per, i) if not last else Count(RET_0 - 2 * FOX_OUT - FOX_IN)
                blk = Count(FOX_B + 5 - 8, 8, i) if not last else Count(RET_B - 16)
                group = Count(-1, 1, i) if not last else Count(FOX_GROUPS - 2)
                n = Count(-4, 4, i) if not last else Count(FOX_HEADS - 8)
                step = att_slots(fox, n, group, True, blk)
                for b in range(4):
                    in_block(g.plus(8 * b), blk.plus(b), step, 8 * b)
                pe.wait_ge(fox.y_lo, n.at(4))
                if not last:
                    out_blocks(g.plus(32), blk.plus(4), 0, 4, none, 0)
                    return
                step = att_slots(fox, Count(FOX_HEADS - 4), Count(FOX_GROUPS - 1), True, blk.plus(4), TAIL_STRIDE)
                att_tail(g.plus(32), blk.plus(4), 0, step, 4, (fox.y_lo, FOX_HEADS))

            with pe.Fori(1, FOX_GROUPS - 1) as i:
                fox_group(i)
            fox_group(None)

            def ret_step(what, n, h, group, blk0):
                if what == "T":
                    if h == 0:
                        all_out(pe, blk0)
                    pe.wait_ge(r_rot, group.at(1))
                    if n.some():
                        pe.wait_ge(r_y, n.at())
                    for a in range(2):
                        for dt in range(2):
                            for t in range(TOK):
                                c = dt * S + t * P
                                src = qk[:, t, 4 * a + 2 * h + dt, :]
                                done = nc.tensor.transpose(M[a][:, c:c + P], src, ident[:])
                    done.then_inc(r_qk_mm, 1)
                elif what == "S":
                    pe.wait_ge(r_qk_sb, n.at(1))
                    if n.some():
                        pe.wait_ge(r_lo, n.at())
                    for dt in range(2):
                        mm(M[2][:, 0:S], kT[:, dt, 0:P], qT[:, dt, :], dt == 0, dt == 1)
                    for dt in range(2):
                        done = mm(M[2][:, S:S + P], kT[:, dt, P:S], qT[:, dt, P:S], dt == 0, dt == 1)
                    done.then_inc(r_s_mm, 1)
                elif what == "O":
                    pe.wait_ge(r_st, n.at(1))
                    v = z[:, 2 + h, :, :]
                    mm(M[0][:], s_sb[:, 0:P], v[:, 0, :], True, True)
                    mm(M[1][:], s_sb[:, P:2 * P], v[:, 0, :], True, False)
                    mm(M[1][:], s_sb[:, 2 * P:3 * P], v[:, 1, :], False, True).then_inc(r_o_mm, 1)
                elif what == "Y":
                    pe.wait_ge(r_y, n.at(1))
                    for k in range(4):
                        for t in range(TOK):
                            c = (k % 2) * S + t * P
                            done = nc.tensor.transpose(M[2 + k // 2][:, c:c + P], y_sb[:, t, k * P:(k + 1) * P], ident[:])
                    done.then_inc(r_y_mm, 1)

            RET_AT = {0: "T", 2: "S", 4: "O", 7: "Y"}

            def ret_slots(n, group, blk0, stride=RET_STRIDE):
                def step(s):
                    for h in range(RET_PAIR):
                        if s - stride * h in RET_AT:
                            ret_step(RET_AT[s - stride * h], n.plus(h), h, group, blk0)
                return step

            pe.wait_ge(xn_ready, 1)
            xt_start(3)
            in_block(Count(RET_0), Count(RET_B), none, 0, build=3)
            for b in range(1, 6):
                in_block(Count(RET_0 + 8 * b), Count(RET_B + b), none, 8 * b)
            per = RET_IN + RET_OUT
            def ret_group(i):
                last = i is None
                g = Count(RET_0 + RET_IN - per, per, i) if not last else Count(TOTAL - 2 * RET_OUT - RET_IN)
                blk = Count(RET_B + 6 - 10, 10, i) if not last else Count(RET_B + 10 * RET_GROUPS - 14)
                group = Count(-1, 1, i) if not last else Count(RET_GROUPS - 2)
                n = Count(-2, 2, i) if not last else Count(RET_HEADS - 4)
                step = ret_slots(n, group, blk)
                for b in range(6):
                    in_block(g.plus(8 * b), blk.plus(b), step, 8 * b)
                pe.wait_ge(r_lo, n.at(2))
                step = none
                if last:
                    step = ret_slots(Count(RET_HEADS - 2), Count(RET_GROUPS - 1), blk.plus(6), RET_TAIL_STRIDE)
                out_blocks(g.plus(48), blk.plus(6), 0, 8, step, 0)

            with pe.Fori(1, RET_GROUPS - 1) as i:
                ret_group(i)
            ret_group(None)
            pe.wait_ge(r_lo, RET_HEADS)
            out_blocks(Count(TOTAL - RET_OUT), Count(RET_B + 10 * RET_GROUPS - 4), 0, 8, none, 0, (x_hi, x_lo))

        @block.scalar
        def _(act):
            def a_(o, i_, f, **kw):
                return nc.scalar.activation(o, i_, f, **kw)

            def split(g, k):
                g = g.plus(k)
                if g.i is None and g.base >= TOTAL:
                    return
                act.wait_ge(raw_full[g.base % RAW], g.over(RAW).at(1, 16))
                if g.plus(1 - SPLIT).some():
                    act.wait_ge(used, g.at(1 - SPLIT))
                a_(w_hi[:, g.base % SPLIT, :], raw[:, g.base % RAW, :], ACT.Copy).then_inc(hi_done, 1)

            def drain(g, blk, zb, free=(), rms=False):
                act.wait_ge(used, g.at())
                for s, v in free:
                    act.wait_ge(s, v)
                par = blk.base % 2
                for t in range(TOK):
                    done = a_(z[:, zb, t, :], acc[par][t][:], ACT.Copy, **({"scale": rs[:, t:t + 1]} if rms else {}))
                done.then_inc(drained[par], 1)

            def xt_out(phase, j):
                if phase == 3:
                    act.wait_ge(xt_aff, j + 1)
                    a_(x_hi[:, 2 * j:2 * j + 2, :].rearrange("p k s -> p (k s)"), tq[:, j % 2, :], ACT.Copy)\
                        .then_inc(xt_hi, 1)
                    return
                act.wait_ge(xt_mm, 8 * phase + j + 1)
                if phase == 2:
                    a_(x_hi[:, 2 * j:2 * j + 2, :].rearrange("p k s -> p (k s)"), M[j % 4][:], ACT.Copy)\
                        .then_inc(xt_hi, 1)
                    return
                c = (G_ATT, G_FFN)[phase] + 2 * j
                for k in range(2):
                    done = a_(x_hi[:, 2 * j + k, :], M[j % 4][:, k * S:(k + 1) * S], ACT.Copy,
                              scale=gains[:, c + k:c + k + 1])
                done.then_inc(xt_hi, 1)

            def first_block(phase, g):
                for j in range(4):
                    xt_out(phase, j)
                for s in range(CH):
                    split(g, s + LEAD)
                    if s + 4 < 8:
                        xt_out(phase, s + 4)
                    elif phase < 2 and s < 6:
                        t = s - 4
                        done = a_(squares_out[:, t, :], res[:, t, :], ACT.Square, accum_out=ssq[:, t:t + 1])
                        if t == TOK - 1:
                            done.then_inc(ssq_done, 1)

            def slots(g, n, step, s0=0):
                for s in range(s0, s0 + n):
                    split(g, s - s0 + LEAD)
                    step(s)

            none = lambda s: None

            def att_step(A, what, n, gq, gk):
                if what == "E":
                    act.wait_ge(A.qk_mm, n.at(1))
                    if n.some():
                        act.wait_ge(A.s_mm, n.at())
                    a_(qT[:, 0, :], M[0][:, 0:S], ACT.Copy, scale=gains[:, gq:gq + 1])
                    a_(kT[:, 0, :], M[0][:, S:2 * S], ACT.Copy, scale=gains[:, gk:gk + 1]).then_inc(A.qk_sb, 1)
                elif what == "P":
                    act.wait_ge(A.maxed, n.at(1))
                    if n.some():
                        act.wait_ge(A.p_mm, n.at())
                        act.wait_ge(A.y_sb, n.at())
                    for t in range(TOK):
                        c = slice(t * P, (1 + 2 * t) * P)
                        done = a_(p_sb[:, c], s_sb[:, c], ACT.Exp, bias=nmax[:, t:t + 1], accum_out=sums[:, t:t + 1])
                    done.then_inc(A.exped, 1)
                elif what == "C":
                    act.wait_ge(A.p_mm, n.at(1))
                    if n.some():
                        act.wait_ge(A.o_mm, n.at())
                    a_(pT, M[2][:, 0:3 * P], ACT.Copy).then_inc(A.p_sb, 1)

            def att_slots(A, n, gq, gk, y0, half, stride=STRIDE):
                def step(s):
                    for h in range(GROUP):
                        m, r = n.plus(h), s - stride * h
                        if r in (0, 2, 3):
                            att_step(A, {0: "E", 2: "P", 3: "C"}[r], m, gq, gk)
                        elif r == 5:
                            act.wait_ge(A.y_mm, m.at(1))
                            a_(y_hi[:, y0 + h, :], M[3][:, 0:S], ACT.Copy, scale=half).then_inc(A.y_hi, 1)
                return step

            def att_tail(g, step):
                for s in range(TAIL):
                    if s < 8:
                        split(g, s + LEAD)
                    elif HALF_AT <= s < HALF_AT + 4:
                        split(g, s - HALF_AT + 8 + LEAD)
                    step(s)
                slots(g.plus(12), 4, none)

            def load(dst, src):
                act.dma_start(dst, src).then_inc(v_full, 16)

            load(rows[0:16, 3, :], attn_norm_g.rearrange("(j p) -> j p", p=P))
            load(rows[16:32, 3, :], ffn_norm_g.rearrange("(j p) -> j p", p=P))
            load(rows[32:40, 3, :], pool_scale.rearrange("(j p) -> j p", p=P))
            load(rows[40:41, 3, :], q_norm_g.rearrange("(j p) -> j p", p=P))
            load(rows[41:42, 3, :], k_norm_g.rearrange("(j p) -> j p", p=P))
            load(rows[42:43, 3, :], fox_q_gain)
            load(rows[43:44, 3, :], fox_k_gain)
            load(rows[44:60, 3, :], ln_gain[0].rearrange("(j p) -> j p", p=P))
            load(rows[60:76, 3, :], ln_bias[0].rearrange("(j p) -> j p", p=P))
            load(ident[:], ident_d)
            act.wait_ge(vec_mm, 1)
            a_(gains[:, 0:76], M[0][:, 0:76], ACT.Copy).then_inc(vec_sb, 1)
            act.wait_ge(vec_sb, 1)
            for k in range(LEAD):
                split(Count(0), k)

            def spread(s):
                if s == 11:
                    act.wait_ge(rbc_mm, 1)
                    a_(rbc, M[0][:, 0:S], ACT.Copy).then_inc(rbc_sb, 1)

            first_block(0, Count(0))
            act.wait_ge(got, 1)
            drain(Count(8), Count(0), 0, rms=True)
            slots(Count(8), 8, spread, 8)
            drain(Count(16), Count(1), 1, rms=True)
            slots(Count(16), 2, none)
            act.wait_ge(used, 18)
            a_(kwT[0:NARROW, :], acc[0][0][0:NARROW, 0:S], ACT.Copy).then_inc(drained[0], 1)

            def indexer(s):
                if s < 4:
                    act.wait_ge(idx_mm, s + 1)
                    a_(qiT[:, 2 * s:2 * s + 2, :].rearrange("p k s -> p (k s)"), M[s][:], ACT.Copy).then_inc(idx_sb, 1)
                elif s > 4:
                    for h in range(min(16, 2 * (s - 5)), min(16, 2 * (s - 5) + 2)):
                        act.wait_ge(rel_mm, h + 1)
                        if h >= 2:
                            act.wait_ge(rel_add, h - 1)
                        a_(rel[:, h % 2, :], M[h % 2][:, 0:3 * P], ACT.Relu).then_inc(rel_sb, 1)

            slots(Count(18), 8, indexer)
            drain(Count(26), Count(3), 2, rms=True)
            slots(Count(26), 8, indexer, 8)
            drain(Count(34), Count(4), 3, rms=True)

            def pool_step(s):
                if s < 8:
                    act.wait_ge(pd_mm, s + 1)
                    a_(poolT[:, s, :], M[2 + s % 2][:, 0:S], ACT.Copy).then_inc(pd_sb, 1)
                elif s < 16:
                    t = s - 8
                    act.wait_ge(py_mm, t + 1)
                    a_(y_hi[:, t, :], M[t % 2][:, 0:S], ACT.Copy, scale=gains[:, G_POOL + t:G_POOL + t + 1])\
                        .then_inc(py_hi, 1)

            slots(Count(34), 8, pool_step)
            drain(Count(42), Count(5), 0, [(idx_mm, 4)], rms=True)
            slots(Count(42), 8, pool_step, 8)
            drain(Count(50), Count(6), 1, rms=True)
            slots(Count(50), 8, pool_step, 16)
            drain(Count(58), Count(7), 2, [(pd_mm, 8)], rms=True)
            slots(Count(58), 16, none)
            step = att_slots(att, Count(0), G_Q, G_K, 0, 1.0)
            slots(Count(74), 8, step)
            drain(Count(82), Count(16), 0, [(att.normed, 1)], rms=True)
            slots(Count(82), 8, step, 8)
            drain(Count(90), Count(17), 1, rms=True)
            slots(Count(90), 8, step, 16)
            drain(Count(98), Count(18), 2, [(att.o_mm, 4)], rms=True)
            att_tail(Count(98), att_slots(att, Count(4), G_Q, G_K, 4, 1.0, TAIL_STRIDE))

            act.wait_ge(vec_mm, 2)
            a_(cols[:].rearrange("p a c -> p (a c)"), M[0][:], ACT.Copy).then_inc(vec_sb, 1)
            act.wait_ge(vec_sb, 2)
            all_out(act, Count(FFN_B))

            def ffn_slots(pair, y0=0):
                def tile(f):
                    return Count(pair.base * 4 + f, pair.per * 4, pair.i)

                def tap(a, f, j):
                    c = pair.at(0, 4) + (a * D_FF // P + f)
                    return cols[:, j, bass.ds(c, 1)]

                def step(s):
                    if s % 2 == 1 and s < 9:
                        f = s // 2
                        n, b = tile(f), f % 2
                        act.wait_ge(u_conv, n.at(1))
                        a_(th[:, b, :], cg3[:, b, 0, :], ACT.Tanh, scale=0.5).then_inc(u_tanh, 1)
                    if s % 2 == 0 and 0 < s < 10:
                        f = s // 2 - 1
                        n, b = tile(f), f % 2
                        act.wait_ge(u_act, n.at(1))
                        a_(y_hi[:, y0 + f, :], act_t[:, b, :], ACT.Copy).then_inc(u_hi, 1)
                    if s % 2 == 0 and s < 8:
                        f = s // 2
                        n, b = tile(f), f % 2
                        act.wait_ge(u_mm, n.at(1))
                        if n.plus(-1).some():
                            act.wait_ge(u_act, n.at(-1 if f else 0))
                        p2 = M[f][:].rearrange("p (a s) -> p a s", a=2)
                        a_(up[:, b, :, 2:S + 2], p2, ACT.Copy)
                        for a in range(2):
                            done = a_(cg[:, b, a, :], M[f][:, a * S:(a + 1) * S], ACT.Identity,
                                      scale=tap(a, f, 2), bias=tap(a, f, 3))
                        done.then_inc(u_aff, 1)
                return step

            g = Count(FFN_0)
            first_block(1, g)
            act.wait_ge(got, 4)
            drain(g.plus(8), Count(FFN_B), 0, rms=True)
            slots(g.plus(8), 8, none)
            drain(g.plus(16), Count(FFN_B + 1), 1, rms=True)
            per = FFN_IN + FFN_OUT

            def ffn_pair(i, tail=none):
                g = Count(FFN_0 + FFN_IN - per, per, i)
                blk = Count(FFN_B + 2 - 6, 6, i)
                step = ffn_slots(Count(-1, 1, i))
                slots(g, 8, step)
                drain(g.plus(8), blk, 0, [(u_mm, i * 4)], rms=True)
                slots(g.plus(8), 8, step, 8)
                drain(g.plus(16), blk.plus(1), 1, rms=True)
                slots(g.plus(16), 8, tail)

            with act.Fori(1, PAIRS - 1) as i:
                ffn_pair(i)
            step = ffn_slots(Count(PAIRS - 1), 4)
            ffn_pair(PAIRS - 1, step)
            step(8)
            slots(Count(FOX_0 - FFN_OUT), 8, none)

            g = Count(FOX_0)
            first_block(2, g)
            drain(g.plus(8), Count(FOX_B), 0)

            def forget(s):
                if s == 9:
                    block_out(act, Count(FOX_B + 1))
                    a_(fT[:, 1, :], fT[:, 0, :], ACT.Abs).then_inc(f_abs, 1)
                    act.wait_ge(f_abs, 1)
                    a_(fT[:, 1, :], fT[:, 1, :], ACT.Exp, scale=-1.0).then_inc(f_exp, 1)
                    act.wait_ge(f_exp, 1)
                    a_(fT[:, 2, :], fT[:, 1, :], ACT.Ln, bias=1.0).then_inc(f_log, 1)

            def tanh_gate(gated, zb, t_sem, n, blk):
                block_out(act, blk)
                if n.some():
                    act.wait_ge(gated, n.at())
                a_(tmp[:, 0:TOK * COL], z[:, zb, :, :].rearrange("p t c -> p (t c)"), ACT.Tanh, scale=0.5)\
                    .then_inc(t_sem, 1)

            slots(g.plus(8), 1, none)
            for b in range(1, 4):
                slots(g.plus(1 + 8 * b), 8, forget, 8 * b)
                drain(g.plus(9 + 8 * b), Count(FOX_B + 1 + b), b)
            tanh_gate(fox.gated, 3, fox.tanh, Count(0), Count(FOX_B + 4))
            per = FOX_IN + FOX_OUT

            def fox_group(i):
                g = Count(FOX_0 + 1 + FOX_IN - per, per, i)
                blk = Count(FOX_B + 5 - 8, 8, i)
                step = att_slots(fox, Count(-4, 4, i), G_FQ, G_FK, 0, 0.5)
                slots(g, 8, step)
                drain(g.plus(8), blk, 0, [(fox.normed, i)])
                slots(g.plus(8), 8, step, 8)
                drain(g.plus(16), blk.plus(1), 1)
                slots(g.plus(16), 8, step, 16)
                drain(g.plus(24), blk.plus(2), 2, [(fox.o_mm, i * 4)])
                slots(g.plus(24), 8, none)
                drain(g.plus(32), blk.plus(3), 3, [(fox.y_sb, i * 4)])
                tanh_gate(fox.gated, 3, fox.tanh, Count(0, 1, i), blk.plus(3))

            with act.Fori(1, FOX_GROUPS - 1) as i:
                fox_group(i)
                slots(Count(FOX_0 + 1 + FOX_IN - per + 32, per, i), 8, none)
            fox_group(FOX_GROUPS - 1)
            att_tail(Count(RET_0 - 2 * FOX_OUT), att_slots(fox, Count(12), G_FQ, G_FK, 4, 0.5, TAIL_STRIDE))

            def ret_slots(n, y=y_hi, stride=RET_STRIDE):
                def step(s):
                    h, r = s // stride, s % stride
                    if h >= RET_PAIR:
                        return
                    m = n.plus(h)
                    if r == 0:
                        act.wait_ge(r_qk_mm, m.at(1))
                        if m.some():
                            act.wait_ge(r_s_mm, m.at())
                        a_(qT[:].rearrange("p k s -> p (k s)"), M[0][:], ACT.Copy)
                        a_(kT[:].rearrange("p k s -> p (k s)"), M[1][:], ACT.Copy).then_inc(r_qk_sb, 1)
                    elif r == 6:
                        act.wait_ge(r_t, m.at(1))
                        if m.some():
                            act.wait_ge(r_y_mm, m.at())
                        for t in range(TOK):
                            done = a_(y_sb[:, t, :], tmp[:, (2 + t) * COL:(3 + t) * COL], ACT.Copy, scale=rstd[:, t:t + 1])
                        done.then_inc(r_y, 1)
                    elif r == 7:
                        act.wait_ge(r_y_mm, m.at(1))
                        for k in range(2):
                            done = a_(y[:, 4 * h + 2 * k:4 * h + 2 * k + 2, :].rearrange("p k s -> p (k s)"),
                                      M[2 + k][:], ACT.Copy, scale=0.5)
                        done.then_inc(r_hi, 1)
                return step

            g = Count(RET_0)
            first_block(3, g)
            drain(g.plus(8), Count(RET_B), 0)
            for b in range(1, 6):
                slots(g.plus(8 * b), 8, none, 8 * b)
                drain(g.plus(8 * b + 8), Count(RET_B + b), b)
                if b >= 4:
                    tanh_gate(r_gated, b, r_tanh, Count(b - 4), Count(RET_B + b))
            per = RET_IN + RET_OUT

            def ret_group(i, tail):
                g = Count(RET_0 + RET_IN - per, per, i)
                blk = Count(RET_B + 6 - 10, 10, i)
                step = ret_slots(Count(-2, 2, i))
                free = {0: [(r_rot, i)], 2: [(r_o_mm, i * 2 - 1)], 3: [(r_o_mm, i * 2)], 4: [(r_t, i * 2)]}
                for b in range(6):
                    slots(g.plus(8 * b), 8, step, 8 * b)
                    drain(g.plus(8 * b + 8), blk.plus(b), b, free.get(b, ()))
                    if b >= 4:
                        tanh_gate(r_gated, b, r_tanh, Count(b - 4, 2, i), blk.plus(b))
                slots(g.plus(48), 16, tail)

            with act.Fori(1, RET_GROUPS - 1) as i:
                ret_group(i, none)
            ret_group(RET_GROUPS - 1, ret_slots(Count(RET_HEADS - 2), x_hi, RET_TAIL_STRIDE))
            slots(Count(TOTAL - RET_OUT), 16, none)

        @block.vector
        def _(v):
            V = nc.vector

            def link(ins):
                dve_n[0] += 1
                ins.then_inc(dve, 1)
                v.wait_ge(dve, dve_n[0])

            class Chain:

                def __init__(self, s, n, per):
                    self.s, self.n, self.per, self.k = s, n, per, 0

                def link(self, ins):
                    self.k += 1
                    ins.then_inc(self.s, 1)
                    v.wait_ge(self.s, self.n.at(0, self.per) + self.k)

            def split(g, k):
                g = g.plus(k)
                if g.i is None and g.base >= TOTAL:
                    return
                v.wait_ge(hi_done, g.at(1))
                a = g.base % SPLIT
                V.tensor_tensor(w_lo[:, a, :], raw[:, g.base % RAW, :], w_hi[:, a, :], ALU.subtract)\
                    .then_inc(lo_done, 1)

            def add_out(g, blk, nb):
                par = blk.base % 2
                v.wait_ge(used, g.at())
                v.wait_ge(drained[par], blk.over(2).at())
                v.wait_ge(drained[1 - par], blk.plus(1).over(2).at())
                for t in range(TOK):
                    c = slice(nb * COL, (nb + 1) * COL)
                    done = V.tensor_tensor(res[:, t, c], acc[par][t][:], res[:, t, c], ALU.add)
                done.then_inc(drained[par], 1)

            def out_slots(g, blk, kt, step=lambda s: None, s0=0, after=lambda nb: None):
                for nb in range(NOUT):
                    for c in range(kt // KC):
                        s = nb * (kt // KC) + c
                        split(g, s + LEAD)
                        step(s0 + s)
                    add_out(g.plus((nb + 1) * (kt // KC)), blk.plus(nb), nb)
                    after(nb)

            def affine(j):
                v.wait_ge(xt_mm, 24 + j + 1)
                if j >= 2:
                    v.wait_ge(xt_lo, 24 + j - 1)
                for k in range(2):
                    c = 2 * j + k
                    done = V.tensor_scalar(tq[:, j % 2, k * S:(k + 1) * S], M[j % 4][:, k * S:(k + 1) * S],
                                           gains[:, G_LG + c:G_LG + c + 1], gains[:, G_LB + c:G_LB + c + 1],
                                           ALU.mult, ALU.add)
                done.then_inc(xt_aff, 1)

            def xt_out(phase, j):
                if phase == 3:
                    if j == 0 or j >= 4:
                        affine(j)
                    if j < 3:
                        affine(j + 1)
                v.wait_ge(xt_hi, 8 * phase + j + 1)
                xl = x_lo[:, 2 * j:2 * j + 2, :]
                xh = x_hi[:, 2 * j:2 * j + 2, :]
                if phase >= 2:
                    V.tensor_tensor(xl.rearrange("p k s -> p (k s)"), M[j % 4][:] if phase == 2 else tq[:, j % 2, :],
                                    xh.rearrange("p k s -> p (k s)"), ALU.subtract).then_inc(xt_lo, 1)
                    return
                c = (G_ATT, G_FFN)[phase] + 2 * j
                for k in range(2):
                    done = V.scalar_tensor_tensor(xl[:, k, :], M[j % 4][:, k * S:(k + 1) * S],
                                                  gains[:, c + k:c + k + 1], xh[:, k, :], ALU.mult, ALU.subtract)
                done.then_inc(xt_lo, 1)

            def first_block(phase, g):
                for j in range(4):
                    xt_out(phase, j)
                for s in range(CH):
                    split(g, s + LEAD)
                    if s + 4 < 8:
                        xt_out(phase, s + 4)
                if phase < 2:
                    v.wait_ge(ssq_done, phase + 1)
                    V.tensor_scalar(ssq[:, 0:TOK], ssq[:, 0:TOK], 1.0 / D, None, ALU.mult).then_inc(want, 1)

            def slots(g, n, step=lambda s: None, s0=0):
                for s in range(s0, s0 + n):
                    split(g, s - s0 + LEAD)
                    step(s)

            def power(k, ins):
                ins.then_inc(want, 1)
                v.wait_ge(got, k.at(1))

            def row_stats(nb):
                for t in range(TOK):
                    done = V.bn_stats(stats[:, t, nb, :], res[:, t, nb * COL:(nb + 1) * COL])
                return done

            def row_norms(k, done):
                link(done)
                for t in range(TOK):
                    done = V.bn_aggr(mv[:, t, :], stats[:, t, :, :].rearrange("p a b -> p (a b)"))
                done.then_inc(want, 1)
                v.wait_ge(want, k + 1)

            def norm_qk(A, link, part, zr, k):
                t = part % 2
                q = z[:, 0:2, t, :]
                if part < 2:
                    if part == 0:
                        block_out(v, zr)
                    sq = tmp[:, 2 * COL:4 * COL]
                    link(V.tensor_tensor(sq.rearrange("p (b c) -> p b c", b=2), q, q, ALU.mult))
                    done = V.tensor_reduce(ssq[:, 8 * t:8 * t + 8], sq.rearrange("p (h c) -> p h c", c=HD), AX, ALU.add)
                    link(done)
                    if part == 1:
                        V.tensor_scalar(ssq[:], ssq[:], 1.0 / HD, None, ALU.mult).then_inc(want, 1)
                else:
                    if part == 2:
                        v.wait_ge(got, k.at(1))
                    done = V.tensor_tensor(qk[:, t, :, :].rearrange("p (b h) c -> p b h c", b=2),
                                           q.rearrange("p b (h c) -> p b h c", c=HD),
                                           rstd[:, 8 * t:8 * t + 8].rearrange("p (b h c) -> p b h c", b=2, c=1)
                                           .to_broadcast([P, 2, GROUP, HD]), ALU.mult)
                    if part == 3:
                        done.then_inc(A.normed, 1)

            NORM_LINKS = 4

            def att_slots(A, n, y0, forget, head0, mask, stride=STRIDE):
                def one(h, r):
                    m = n.plus(h)
                    if r == 0 and forget:
                        if m.some():
                            v.wait_ge(A.s_mm, m.at())
                        V.tensor_scalar(ckT, cT, ident[0:FOX_HEADS, bass.ds(head0 + h, 1)], None, ALU.mult)\
                            .then_inc(A.ck, 1)
                    elif r == 1:
                        v.wait_ge(A.s_mm, m.at(1))
                        if m.some():
                            v.wait_ge(A.exped, m.at())
                        for t in range(TOK):
                            c = slice(t * P, (1 + 2 * t) * P)
                            if forget:
                                sc = c_nat[:, bass.ds(head0 + (t * FOX_HEADS + h), 1)]
                                done = V.scalar_tensor_tensor(s_sb[:, c], M[1][:, c], sc, mask[:, c], ALU.add, ALU.add)
                            else:
                                done = V.scalar_tensor_tensor(s_sb[:, c], M[1][:, c], HD ** -0.5, mask[:, c], ALU.mult, ALU.add)
                        ch = Chain(A.chain, m, 2)
                        ch.link(done)
                        for t in range(TOK):
                            done = V.reduce_max(nmax[:, t:t + 1], s_sb[:, t * P:(1 + 2 * t) * P], AX, negate=True)
                        done.then_inc(A.maxed, 1)
                    elif r == 4:
                        v.wait_ge(A.o_mm, m.at(1))
                        if m.some():
                            v.wait_ge(A.y_mm, m.at())
                        ch = Chain(A.chain, m, 2)
                        ch.k = 1
                        ch.link(V.reciprocal(rinv[:], sums[:]))
                        for t in range(TOK):
                            o = M[3][:, t * P:(t + 1) * P]
                            if forget:
                                done = V.scalar_tensor_tensor(y_att[:, t, :], o, rinv[:, t:t + 1],
                                                              z[:, 3, t, h * HD:(h + 1) * HD], ALU.mult, ALU.mult)
                            else:
                                done = V.tensor_scalar(y_att[:, t, :], o, rinv[:, t:t + 1], None, ALU.mult)
                        done.then_inc(A.y_sb, 1)
                    elif r == 5:
                        v.wait_ge(A.y_hi, m.at(1))
                        V.scalar_tensor_tensor(y_lo[:, y0 + h, :], M[3][:, 0:S], 0.5 if forget else 1.0,
                                               y_hi[:, y0 + h, :], ALU.mult, ALU.subtract).then_inc(A.y_lo, 1)

                def step(s):
                    for h in range(GROUP):
                        one(h, s - stride * h)
                return step

            def att_tail(g, blk, step, after=lambda nb: None):
                for s in range(TAIL):
                    if s < 8:
                        split(g, s + LEAD)
                    elif HALF_AT <= s < HALF_AT + 4:
                        split(g, s - HALF_AT + 8 + LEAD)
                    step(s)
                    if s < 8 and s % 2 == 1:
                        add_out(g.plus(s + 1), blk.plus(s // 2), s // 2)
                    elif HALF_AT <= s < HALF_AT + 4:
                        nb = s - HALF_AT
                        add_out(g.plus(9 + nb), blk.plus(4 + nb), nb)
                for nb in range(NOUT):
                    split(g, 12 + nb + LEAD)
                    add_out(g.plus(13 + nb), blk.plus(8 + nb), nb)
                    after(nb)

            V.memset(minus[:], -1.0)
            V.memset(isc, 0.0)
            V.memset(ones[:], 1.0)
            link(V.memset(small[:], 0.0))
            for k in range(LEAD):
                split(Count(0), k)
            v.wait_ge(vec_sb, 1)
            link(V.tensor_scalar(gains[:, G_FQ:G_FQ + 1], gains[:, G_FQ:G_FQ + 1], HD ** -0.5, None, ALU.mult))

            def spread(s):
                if s == 9:
                    v.wait_ge(got, 1)
                    for t in range(TOK):
                        done = V.tensor_scalar(diag[:, t * P:(t + 1) * P], ident[:], rs[:, t:t + 1], None, ALU.mult)
                    done.then_inc(d_full, 1)

            first_block(0, Count(0))
            slots(Count(8), 10, spread, 8)

            def indexer(s):
                if s == 1:
                    block_out(v, Count(2))
                    v.wait_ge(rbc_sb, 1)
                    V.tensor_tensor(kiT[0:IDX_DIM, :], kwT[0:IDX_DIM, :], rbc[0:IDX_DIM, :], ALU.mult).then_inc(ki_part, 1)
                elif s == 4:
                    v.wait_ge(idx_mm, 5)
                    for t in range(TOK):
                        done = V.tensor_scalar(w_idx[:, t, :], M[2][:, t * IDX_HEADS:(t + 1) * IDX_HEADS], rs[:, t:t + 1],
                                               float(IDX_HEADS * IDX_DIM) ** -0.5, ALU.mult, ALU.mult)
                    link(done)
                if s < 5:
                    return
                for h in range(min(16, 2 * (s - 5)), min(16, 2 * (s - 5) + 2)):
                    v.wait_ge(rel_sb, h + 1)
                    if h > 0:
                        v.wait_ge(rel_add, h)
                    for t in range(TOK):
                        c = slice(t * P, (1 + 2 * t) * P)
                        done = V.scalar_tensor_tensor(isc[:, c], rel[:, h % 2, c], w_idx[:, t, h:h + 1], isc[:, c],
                                                      ALU.mult, ALU.add)
                    done.then_inc(rel_add, 1)

            slots(Count(18), 16, indexer)

            def topk(s):
                if s == 0:
                    v.wait_ge(rel_add, 16)
                    v.wait_ge(c_full, 16 * 5)
                    link(V.tensor_tensor(isc, isc, causal[:], ALU.add))
                if s < 8:
                    for t in range(TOK):
                        c = slice(t * P, (1 + 2 * t) * P)
                        done = V.max(top8[:, t, :], isc[:, c])
                    link(done)
                    for t in range(TOK):
                        c = slice(t * P, (1 + 2 * t) * P)
                        done = V.match_replace(isc[:, c], top8[:, t, :], isc[:, c], TAKEN)
                    link(done)
                if s == 8:
                    link(V.tensor_scalar(pen[:], isc, TAKEN * 0.9, NEG, ALU.is_gt, ALU.mult))
                    link(V.tensor_tensor(pen[:], pen[:], causal[:], ALU.min))

            def pool_step(s):
                topk(s)
                if 8 <= s < 16:
                    t = s - 8
                    v.wait_ge(py_hi, t + 1)
                    V.scalar_tensor_tensor(y_lo[:, t, :], M[t % 2][:, 0:S], gains[:, G_POOL + t:G_POOL + t + 1],
                                           y_hi[:, t, :], ALU.mult, ALU.subtract).then_inc(py_lo, 1)

            slots(Count(34), 24, pool_step)

            def norm_step(A, link, zr, s0, k):
                def step(s):
                    if s0 <= s < s0 + 4:
                        norm_qk(A, link, s - s0, zr, k)
                return step

            def both(one, two):
                def step(s):
                    one(s)
                    two(s)
                return step

            out_slots(Count(58), Count(8), 4, norm_step(att, link, Count(6), 0, Count(1)))
            out_slots(Count(66), Count(12), 4)
            slots(Count(74), 24, both(att_slots(att, Count(0), 0, False, 0, pen),
                                      norm_step(att, link, Count(17), 18, Count(2))))
            att_tail(Count(98), Count(19), att_slots(att, Count(4), 4, False, 0, pen, TAIL_STRIDE))

            v.wait_ge(used, FFN_0)
            link(V.memset(up[:, :, :, 0:2], 0.0))
            g = Count(FFN_0)
            first_block(1, g)
            slots(g.plus(8), 8)

            def ffn_slots(pair, y0=0):
                def tile(f):
                    return Count(pair.base * 4 + f, pair.per * 4, pair.i)

                def tap(a, f, j):
                    c = pair.at(0, 4) + (a * D_FF // P + f)
                    return cols[:, j, bass.ds(c, 1)]

                def step(s):
                    if s % 2 == 0 and 0 < s < 10:
                        f = s // 2 - 1
                        n, b = tile(f), f % 2
                        v.wait_ge(u_hi, n.at(1))
                        V.tensor_tensor(y_lo[:, y0 + f, :], act_t[:, b, :], y_hi[:, y0 + f, :], ALU.subtract).then_inc(u_lo, 1)
                    if s % 2 == 0 and s < 8:
                        f = s // 2
                        n, b = tile(f), f % 2
                        v.wait_ge(u_aff, n.at(1))
                        for a in range(2):
                            done = V.scalar_tensor_tensor(cg2[:, b, a, :], up[:, b, a, 1:S + 1], tap(a, f, 1),
                                                          cg[:, b, a, :], ALU.mult, ALU.add)
                        done.then_inc(u_c1, 1)
                        v.wait_ge(u_c1, n.at(1))
                        for a in range(2):
                            done = V.scalar_tensor_tensor(cg3[:, b, a, :], up[:, b, a, 0:S], tap(a, f, 0),
                                                          cg2[:, b, a, :], ALU.mult, ALU.add)
                        done.then_inc(u_conv, 1)
                    if s % 2 == 1 and s < 9:
                        f = s // 2
                        n, b = tile(f), f % 2
                        v.wait_ge(u_tanh, n.at(1))
                        if n.plus(-1).some():
                            v.wait_ge(u_hi, n.at(-1 if f else 0))
                        V.scalar_tensor_tensor(act_r[:, b, :], th[:, b, :], 1.0, cg3[:, b, 0, :], ALU.add, ALU.mult)\
                            .then_inc(u_r, 1)
                        v.wait_ge(u_r, n.at(1))
                        V.scalar_tensor_tensor(act_t[:, b, :], act_r[:, b, :], 0.5, cg3[:, b, 1, :], ALU.mult, ALU.mult)\
                            .then_inc(u_act, 1)
                return step

            per = FFN_IN + FFN_OUT

            def ffn_pair(i, tail=lambda s: None):
                g = Count(FFN_0 + FFN_IN - per, per, i)
                slots(g, 16, ffn_slots(Count(-1, 1, i)))
                out_slots(g.plus(16), Count(FFN_B + 4 - 6, 6, i), 4, tail)

            with v.Fori(1, PAIRS - 1) as i:
                ffn_pair(i)
            step = ffn_slots(Count(PAIRS - 1), 4)
            ffn_pair(PAIRS - 1, step)
            step(8)
            out_slots(Count(FOX_0 - FFN_OUT), Count(FOX_B - 4), 4)

            g = Count(FOX_0)
            first_block(2, g)
            v.wait_ge(xt_mm, 24)
            for t in range(TOK):
                done = V.tensor_scalar(res[:, t, :], res[:, t, :], ALPHA, None, ALU.mult)
            link(done)
            slots(g.plus(8), 1)
            v.wait_ge(used, FOX_0 + 9)
            V.memset(fT[:, 4, :], 0.0)
            par = (FOX_B + 1) % 2
            V.tensor_scalar(fT[:, 0, :], acc[par][0][0:FOX_HEADS, 0:S], bfc[:, 0:1], None, ALU.add)\
                .then_inc(drained[par], 1)
            block_out(v, Count(FOX_B + 1))

            def forget(s):
                if s == 10:
                    v.wait_ge(f_log, 1)
                    link(V.scalar_tensor_tensor(fT[:, 3, :], fT[:, 0, :], 0.0, fT[:, 2, :], ALU.min, ALU.subtract))
                    V.tensor_tensor_scan(cT, fT[:, 3, :], fT[:, 4, :], 0.0, ALU.add, ALU.add).then_inc(c_ready, 1)
                    v.wait_ge(c_ready, 1)
                if s == 12:
                    v.wait_ge(f_mm, 1)
                    link(V.tensor_copy(c_nat[:], M[0][:, 0:TOK * FOX_HEADS]))

            def group_norm(group, zr):
                return norm_step(fox, Chain(fox_norm, group, NORM_LINKS).link, zr, 18, group.plus(4))

            slots(g.plus(9), 24, both(forget, group_norm(Count(0), Count(FOX_B + 2))), 8)

            def gate(t_sem, g_sem, zb, n):
                v.wait_ge(t_sem, n)
                t = z[:, zb, :, :].rearrange("p t c -> p (t c)")
                V.scalar_tensor_tensor(t, tmp[:, 0:TOK * COL], 1.0, t, ALU.add, ALU.mult).then_inc(g_sem, 1)
                v.wait_ge(g_sem, n)

            gate(fox.tanh, fox.gated, 3, 1)
            per = FOX_IN + FOX_OUT

            def fox_group(i):
                g = Count(FOX_0 + 1 + FOX_IN - per, per, i)
                slots(g, 32, both(att_slots(fox, Count(-4, 4, i), 0, True, i * 4 - 4, causal),
                                  group_norm(Count(0, 1, i), Count(FOX_B + 6 - 8, 8, i))))
                gate(fox.tanh, fox.gated, 3, i + 1)

            with v.Fori(1, FOX_GROUPS - 1) as i:
                fox_group(i)
                out_slots(Count(FOX_0 + 1 + FOX_IN - per + 32, per, i), Count(FOX_B + 9 - 8, 8, i), 4)
            fox_group(FOX_GROUPS - 1)

            sums_in = [None] * NOUT

            def stats_after(first):
                def after(nb):
                    blk = Count(first + nb)
                    block_out(v, blk)
                    sums_in[nb] = row_stats(nb)
                return after

            att_tail(Count(RET_0 - 2 * FOX_OUT), Count(RET_B - 12),
                     att_slots(fox, Count(12), 4, True, 12, causal, TAIL_STRIDE), stats_after(RET_B - 4))
            row_norms(W_RET - 1, sums_in[-1])
            v.wait_ge(got, W_RET)
            for t in range(TOK):
                done = V.tensor_scalar(res[:, t, :], res[:, t, :], mv[:, t, 0:1], rstd[:, t:t + 1],
                                       ALU.subtract, ALU.mult)
            done.then_inc(xn_ready, 1)
            v.wait_ge(xn_ready, 1)

            def rotate(group, zr):
                ch = Chain(r_rot_chain, group, 3)

                def step(s):
                    if not 24 <= s < 26:
                        return
                    t = s - 24
                    if t == 0:
                        block_out(v, zr)
                    m = rp.rearrange("p (x a h c) -> p x a h c", x=4, a=2, h=2)
                    for a in range(2):
                        src = z[:, a, t, :].rearrange("p (h f c) -> p h f c", h=2, f=2)
                        cos = rot[:, 0, t:t + 1, :].to_broadcast([P, 2, P])
                        sin = rot[:, 1, t:t + 1, :].to_broadcast([P, 2, P])
                        V.tensor_tensor(m[:, 0, a], src[:, :, 0, :], cos, ALU.mult)
                        V.tensor_tensor(m[:, 1, a], src[:, :, 1, :], sin, ALU.mult)
                        V.tensor_tensor(m[:, 2, a], src[:, :, 0, :], sin, ALU.mult)
                        done = V.tensor_tensor(m[:, 3, a], src[:, :, 1, :], cos, ALU.mult)
                    ch.link(done)
                    for a in range(2):
                        dst = qk[:, t, 4 * a:4 * a + 4, :].rearrange("p (h f) c -> p h f c", h=2)
                        V.tensor_tensor(dst[:, :, 0, :], m[:, 0, a], m[:, 1, a], ALU.subtract)
                        done = V.tensor_tensor(dst[:, :, 1, :], m[:, 2, a], m[:, 3, a], ALU.add)
                    if t == 0:
                        ch.link(done)
                    else:
                        done.then_inc(r_rot, 1)
                        v.wait_ge(r_rot, group.at(1))
                return step

            def ret_slots(n, head0, yh=y_hi, yl=y_lo, stride=RET_STRIDE):
                def step(s):
                    h, r = s // stride, s % stride
                    if h >= RET_PAIR:
                        return
                    m = n.plus(h)
                    if r == 2:
                        v.wait_ge(r_s_mm, m.at(1))
                        if m.some():
                            v.wait_ge(r_o_mm, m.at())
                        V.tensor_tensor(s_sb[:], M[2][:, 0:3 * P], table[:, bass.ds((head0 + h) * (3 * P), 3 * P)], ALU.mult)\
                            .then_inc(r_st, 1)
                    elif r == 4:
                        v.wait_ge(r_o_mm, m.at(1))
                        if m.some():
                            v.wait_ge(r_y, m.at())
                        ch = Chain(r_chain, m, 1)
                        for t in range(TOK):
                            done = V.bn_stats(stats[:, t, 0, :], M[t][:])
                        ch.link(done)
                        V.memset(small[:, 3:4], 0.0)
                        for t in range(TOK):
                            done = V.bn_aggr(mv[:, t, :], stats[:, t, 0, :])
                        power(m.plus(W_RET), done)
                        for t in range(TOK):
                            done = V.scalar_tensor_tensor(tmp[:, (2 + t) * COL:(3 + t) * COL], M[t][:], mv[:, t, 0:1],
                                                          z[:, 4 + h, t, :], ALU.subtract, ALU.mult)
                        done.then_inc(r_t, 1)
                    elif r == 7:
                        v.wait_ge(r_hi, m.at(1))
                        for k in range(2):
                            t = 4 * h + 2 * k
                            done = V.scalar_tensor_tensor(yl[:, t:t + 2, :].rearrange("p k s -> p (k s)"), M[2 + k][:], 0.5,
                                                          yh[:, t:t + 2, :].rearrange("p k s -> p (k s)"),
                                                          ALU.mult, ALU.subtract)
                        done.then_inc(r_lo, 1)
                return step

            v.wait_ge(dec_full, 16)
            g = Count(RET_0)
            first_block(3, g)

            def residual(s):
                if s in (8, 10, 12, 14):
                    t = (s - 8) // 4
                    if s == 8:
                        v.wait_ge(xt_mm, 32)
                        v.wait_ge(ln_full, 32)
                    if s % 4 == 0:
                        link(V.scalar_tensor_tensor(res[:, t, :], res[:, t, :], ALPHA, gbc[:, 0, :], ALU.mult, ALU.mult))
                    else:
                        link(V.scalar_tensor_tensor(res[:, t, :], gbc[:, 1, :], ALPHA, res[:, t, :], ALU.mult, ALU.add))
                    if s == 14:
                        V.memset(small[:, 1:2], 0.0).then_inc(ln_used, 1)

            st = rotate(Count(0), Count(RET_B + 1))
            slots(g.plus(8), 32, both(residual, st), 8)
            gate(r_tanh, r_gated, 4, 1)
            slots(g.plus(40), 8, st, 40)
            gate(r_tanh, r_gated, 5, 2)
            per = RET_IN + RET_OUT

            def ret_group(i, tail=lambda s: None):
                g = Count(RET_0 + RET_IN - per, per, i)
                st = ret_slots(Count(-2, 2, i), i * 2 - 2)
                ro = rotate(Count(0, 1, i), Count(RET_B + 7 - 10, 10, i))
                slots(g, 40, both(st, ro))
                gate(r_tanh, r_gated, 4, i * 2 + 1)
                slots(g.plus(40), 8, st, 40)
                gate(r_tanh, r_gated, 5, i * 2 + 2)
                out_slots(g.plus(48), Count(RET_B + 12 - 10, 10, i), 8, tail)

            with v.Fori(1, RET_GROUPS - 1) as i:
                ret_group(i)
            ret_group(RET_GROUPS - 1, ret_slots(Count(RET_HEADS - 2), RET_HEADS - 2, x_hi, x_lo, RET_TAIL_STRIDE))
            last = RET_B + 10 * RET_GROUPS - 4
            out_slots(Count(TOTAL - RET_OUT), Count(last), 8, after=stats_after(last))
            row_norms(W_RET + RET_HEADS, sums_in[-1])
            v.wait_ge(ln_full, 64)
            for t in range(TOK):
                done = V.scalar_tensor_tensor(res[:, t, :], res[:, t, :], mv[:, t, 0:1], gbc[:, 0, :],
                                              ALU.subtract, ALU.mult)
            link(done)
            v.wait_ge(got, W_RET + RET_HEADS + 1)
            for t in range(TOK):
                V.scalar_tensor_tensor(res[:, t, :], res[:, t, :], rstd[:, t:t + 1], gbc[:, 1, :],
                                       ALU.mult, ALU.add).then_inc(out_ready[t], 1)


NAMES = ["x", "attn_norm_g", "w_in", "pool_w", "pool_scale", "q_norm_g", "k_norm_g", "w_out",
         "ffn_norm_g", "w_up", "conv_w", "conv_b", "w_down", "fox_w_in_2", "fox_b_f_2", "fox_q_gain_2",
         "fox_k_gain_2", "fox_w_out_2", "ret_w_in_2", "ret_w_out_2", "ln_gain_2", "ln_bias_2"]


def kernel(**inputs):
    import concourse.bacc as bacc
    from concourse.bass_utils import run_bass_kernel_spmd

    nc = bacc.Bacc("TRN2", target_bir_lowering=False, num_devices=1)
    arrays, args = {}, []
    for name in NAMES:
        arrays[f"in_{name}"] = np.ascontiguousarray(inputs[name])
    arrays.update({f"const_{k}": a for k, a in constants().items()})
    for name, a in arrays.items():
        args.append(nc.dram_tensor(name, a.shape, mybir.dt.from_np(a.dtype), kind="ExternalInput").ap())
    args.append(nc.dram_tensor("y", (1, S, D), F32, kind="ExternalOutput").ap())
    mixers_kernel(nc, *args)
    r = run_bass_kernel_spmd(nc, [arrays], core_ids=[0])
    return r.results[0]["y"]
```

```python
import numpy as np
import concourse.bass as bass
from concourse import mybir
from contextlib import ExitStack

F32 = mybir.dt.float32
F32R = mybir.dt.float32r
ALU = mybir.AluOpType
ACT = mybir.ActivationFunctionType
AX = mybir.AxisListType.X


P = 128
S = 256
TOK = S // P
D = 2048
KT = D // P
COL = 512
KC = 2
CH = KT // KC
NOUT = D // COL
HD = 128
EPS = 1e-6
LN_EPS = 1e-5
GN_EPS = 1e-6
NEG = -1e30
TAKEN = -3e38

D_POOL = 1024
POOL_W = (2, 4, 8, 16)
IDX_HEADS, IDX_DIM = 16, 64
TOPK = 64
ATT_HEADS = 8
D_IN = 5200
C_Q, C_K, C_V, C_QI, C_KI = 1024, 2048, 3072, 4096, 5120
NARROW = IDX_DIM + IDX_HEADS
NARROW_K = 8
D_FF = 5632
PAIRS = D_FF // COL
FOX_HEADS = 16
GROUP = 4
FOX_GROUPS = FOX_HEADS // GROUP
RET_HEADS, RET_QK, RET_V = 8, 256, 512
RET_PAIR = 2
RET_GROUPS = RET_HEADS // RET_PAIR
ALPHA = (2.0 * 2) ** 0.25

RAW = 4
SPLIT = 4
LEAD = SPLIT - 1
STRIDE, TAIL_STRIDE = 5, 2
FFN_AT, FFN_TAIL_AT = (0, 2, 4, 6), (0, 2, 4, 7)
TAIL = 3 * TAIL_STRIDE + 6
HALF_AT = 8
RET_STRIDE, RET_TAIL_STRIDE = 10, 8
OUT_PARTS = ((1, 0), (1, D // 2), (0, 0), (0, D // 2))

L1_CHUNKS = 16 + 2 + 16 + 24 + 16 + 24 + 8 + 8
L1_BLOCKS = 2 + 1 + 2 + 3 + 8 + 3 + 4 + 8
FFN_IN, FFN_OUT = 2 * CH, NOUT * 2
FOX_IN, FOX_OUT = 4 * CH, NOUT * 2
RET_IN, RET_OUT = 6 * CH, NOUT * 4
FFN_0 = L1_CHUNKS
FOX_0 = FFN_0 + PAIRS * (FFN_IN + FFN_OUT)
RET_0 = FOX_0 + 1 + FOX_GROUPS * (FOX_IN + FOX_OUT)
TOTAL = RET_0 + RET_GROUPS * (RET_IN + RET_OUT)
FFN_B = L1_BLOCKS
FOX_B = FFN_B + PAIRS * 6 + 4
RET_B = FOX_B + 1 + FOX_GROUPS * 8 + 4


class Count:

    def __init__(self, base, per=0, i=None):
        self.base, self.per, self.i = base, per, i

    def at(self, k=0, times=1):
        v = (self.base + k) * times
        return v if self.i is None else self.i * (self.per * times) + v

    def plus(self, k):
        return Count(self.base + k, self.per, self.i)

    def over(self, n):
        return Count(self.base // n, self.per // n, self.i)

    def some(self):
        return self.i is not None or self.base > 0


def constants():
    pen = np.zeros((P, 3 * P), np.float32)
    upper = np.where(np.arange(P)[None, :] <= np.arange(P)[:, None], 0.0, NEG).astype(np.float32)
    pen[:, 0:P] = upper
    pen[:, 2 * P:3 * P] = upper
    pool = np.zeros((len(POOL_W), S, S), np.float32)
    for g, w in enumerate(POOL_W):
        for q in range(S):
            lo = max(q + 1 - w, 0)
            pool[g, lo:q + 1, q] = 1.0 / (q + 1 - lo)
            pool[g, q, q] -= 1.0
    packed = np.concatenate([pool[:, 0:P, :], pool[:, P:S, P:S]], axis=2).transpose(1, 0, 2)
    inv = 10000.0 ** (-np.arange(0, RET_QK, 2, dtype=np.float32) / RET_QK)
    ang = (np.arange(S, dtype=np.float32)[:, None] * inv.astype(np.float32)[None, :]).astype(np.float32)
    rot = np.stack([np.cos(ang), np.sin(ang)]).astype(np.float32)
    rot = rot.reshape(2, TOK, P, P).transpose(2, 0, 1, 3)
    lg = np.log1p(-np.exp2(-5.0 - np.arange(RET_HEADS, dtype=np.float64)))
    diff = (np.arange(S)[None, :] - np.arange(S)[:, None]).astype(np.float64)
    dec = np.where(diff >= 0, np.exp(np.maximum(diff, 0)[None] * lg[:, None, None]), 0.0) * RET_QK ** -0.5
    dec = np.concatenate([dec[:, 0:P, :], dec[:, P:S, P:S]], axis=2).transpose(1, 0, 2)
    return {
        "ident": np.eye(P, dtype=np.float32),
        "causal": pen,
        "poolband": np.ascontiguousarray(packed.reshape(P, -1), dtype=np.float32),
        "rotary": np.ascontiguousarray(rot.reshape(P, -1), dtype=np.float32),
        "decay": np.ascontiguousarray(dec.reshape(P, -1), dtype=np.float32),
    }


def mixers_kernel(nc, x, w_in, pool_w, w_out, w_up, w_down, fox_w_in, fox_b_f, fox_w_out,
                  ret_w_in, ret_w_out, ln_gain, ln_bias, vectors, taps,
                  ident_d, causal_d, poolband_d, rotary_d, decay_d, out):
    ctx = ExitStack()
    with ctx:
        def sb(name, shape, dt=F32):
            return ctx.enter_context(nc.sbuf_tensor(name, shape, dt))

        def sem(name):
            return ctx.enter_context(nc.semaphore(name))

        raw = sb("raw", [P, RAW, KC * COL])
        w_hi = sb("w_hi", [P, SPLIT, KC * COL], F32R)
        w_lo = sb("w_lo", [P, SPLIT, KC * COL], F32R)
        x_hi = sb("x_hi", [P, KT, S], F32R)
        x_lo = sb("x_lo", [P, KT, S], F32R)
        y_hi = sb("y_hi", [P, 8, S], F32R)
        y_lo = sb("y_lo", [P, 8, S], F32R)
        res = sb("res", [P, TOK, D])
        z = sb("z", [P, 6, TOK, COL])
        squares_out = z[:, 0:4, :, :].rearrange("p b t c -> p (b t c)").rearrange("p (t d) -> p t d", t=TOK)
        qk = sb("qk", [P, TOK, 8, HD])
        tmp = sb("tmp", [P, 4 * COL])
        qT = sb("qT", [P, 2, S])
        kT = sb("kT", [P, 2, S])
        s_sb = sb("s_sb", [P, 3 * P])
        heads = sb("heads", [P, 2 * COL])
        y_sb = heads[:].rearrange("p (t c) -> p t c", t=TOK)
        y_att = heads[:, 0:S].rearrange("p (t c) -> p t c", t=TOK)
        p_sb = heads[:, S:S + 3 * P]
        pT = heads[:, S + 3 * P:S + 6 * P]
        pen = sb("pen", [P, 3 * P])
        top8 = sb("top8", [P, 2, 8])
        w_idx = sb("w_idx", [P, TOK, IDX_HEADS])
        ident = sb("ident_sb", [P, P])
        causal = sb("causal_sb", [P, 3 * P])
        ones = sb("ones", [P, P])
        rot = sb("rot", [P, 2, TOK, P])
        cols = sb("cols", [P, 4, P])
        gains = sb("gains", [P, 80])
        small = sb("small", [P, 4])
        pconst = sb("pconst", [P, 4])
        ssq = sb("ssq", [P, 16])
        rstd = sb("rstd", [P, 16])
        nmax = sb("nmax", [P, TOK])
        sums = sb("sums", [P, TOK])
        rinv = sb("rinv", [P, TOK])
        rs = sb("rs", [P, TOK])
        bfc = sb("bfc", [FOX_HEADS, 1])
        tq = heads[:].rearrange("p (b c) -> p b c", b=2)
        c_nat = sb("c_nat", [P, TOK * FOX_HEADS])
        cT = qT[0:FOX_HEADS, 1, :]
        ckT = kT[0:FOX_HEADS, 1, :]
        minus = sb("minus", [FOX_HEADS, P])
        stats = sb("stats", [P, TOK, 4, 6])
        mv = sb("mv", [P, TOK, 2])
        spare = z[:, 4:6, :, :].rearrange("p b t c -> p (b t c)")
        rows = spare[:, 0:4 * P].rearrange("p (r c) -> p r c", r=4)
        kwT, wT, diag, rbc = (spare[:, (2 + k) * S:(3 + k) * S] for k in range(4))
        fT = spare[0:FOX_HEADS, 0:5 * S].rearrange("p (a s) -> p a s", a=5)
        table = sb("table", [P, RET_HEADS * 3 * P])
        band = table[:, 0:4 * 3 * P]
        rel = table[:, 12 * P:18 * P].rearrange("p (b c) -> p b c", b=2)
        isc = table[:, 18 * P:21 * P]
        kiT = table[:, 21 * P:23 * P]
        arena = sb("arena", [P, 6144])

        def part(at, *shape):
            n = int(np.prod(shape))
            names = "abc"[:len(shape)]
            kw = dict(zip(names, shape))
            return arena[:, at:at + n].rearrange(f"p ({' '.join(names)}) -> p {' '.join(names)}", **kw)

        qiT, poolT, pw = part(0, 8, S), part(2048, 8, S), part(4096, 8, 256)
        up = part(0, 2, 2, S + 2)
        cg, cg2, cg3 = part(1032, 2, 2, S), part(2056, 2, 2, S), part(3080, 2, 2, S)
        th, act_t, act_r = part(4104, 2, S), part(4616, 2, S), part(5128, 2, S)
        gbc = part(0, 2, D)
        rp = arena[:, 4096:6144]

        acc = [[ctx.enter_context(nc.psum_tensor(f"acc{b}{t}", [P, COL], F32)) for t in range(TOK)]
               for b in range(2)]
        M = [ctx.enter_context(nc.psum_tensor(f"mix{b}", [P, COL], F32)) for b in range(4)]

        G_ATT, G_FFN, G_POOL, G_Q, G_K, G_FQ, G_FK, G_LG, G_LB = 0, 16, 32, 40, 41, 42, 43, 44, 60
        VECTORS = 76

        raw_full = [sem(f"raw_full{k}") for k in range(RAW)]
        hi_done, lo_done = sem("hi_done"), sem("lo_done")
        used = sem("used")
        drained = [sem("drained0"), sem("drained1")]
        x_full, c_full = [sem(f"x_full{k}") for k in range(4)], sem("c_full")
        v_full, b_full = sem("v_full"), sem("b_full")
        xn_ready = sem("xn_ready")
        ssq_done = sem("ssq_done")
        xt_mm, xt_hi, xt_lo = sem("xt_mm"), sem("xt_hi"), sem("xt_lo")
        vec_mm, vec_sb = sem("vec_mm"), sem("vec_sb")
        dve = sem("dve_chain")
        dve_n = [0]
        idx_mm, idx_sb = sem("idx_mm"), sem("idx_sb")
        rel_mm, rel_sb, rel_add = sem("rel_mm"), sem("rel_sb"), sem("rel_add")
        d_full, rbc_mm, rbc_sb, ki_part, ki_full, w_full = (sem(n) for n in (
            "diag_full", "rbc_mm", "rbc_sb", "ki_part", "ki_full", "w_full"))
        xt_aff, ln_used, ln_centred, ln_scaled = (sem(n) for n in ("xt_aff", "ln_used", "ln_centred", "ln_scaled"))
        c_ready, out_ready = sem("c_ready"), [sem(f"out_ready{k}") for k in range(len(OUT_PARTS))]
        pd_mm, pd_sb, py_mm, py_hi, py_lo = (sem(n) for n in ("pd_mm", "pd_sb", "py_mm", "py_hi", "py_lo"))
        out_sem = sem("out_sem")
        f_abs, f_exp, f_log, f_mm = (sem(n) for n in ("f_abs", "f_exp", "f_log", "f_mm"))
        want, got, added, pc = sem("power_want"), sem("power_got"), sem("power_added"), sem("power_const")
        W_RET = 4 + FOX_GROUPS + 1

        class Att:

            def __init__(self, p):
                self.normed = sem(p + "normed")
                self.gated = sem(p + "gated")
                self.tanh = sem(p + "tanh")
                self.masked, self.inverse = sem(p + "masked"), sem(p + "inverse")
                self.qk_mm, self.qk_sb = sem(p + "qk_mm"), sem(p + "qk_sb")
                self.ck = sem(p + "ck")
                self.s_mm, self.maxed, self.exped = sem(p + "s_mm"), sem(p + "maxed"), sem(p + "exped")
                self.p_mm, self.p_sb = sem(p + "p_mm"), sem(p + "p_sb")
                self.o_mm, self.y_sb = sem(p + "o_mm"), sem(p + "y_sb")
                self.y_mm, self.y_hi, self.y_lo = sem(p + "y_mm"), sem(p + "y_hi"), sem(p + "y_lo")

        att, fox = Att("att_"), Att("fox_")
        r_rot, r_gated, r_tanh = sem("r_rot"), sem("r_gated"), sem("r_tanh")
        r_chain, r_rot_chain, fox_norm = sem("r_chain"), sem("r_rot_chain"), sem("fox_norm")
        dec_full, ln_full = sem("dec_full"), sem("ln_full")
        r_qk_mm, r_qk_sb, r_s_mm, r_st, r_o_mm = (sem("r_" + n) for n in ("qk_mm", "qk_sb", "s_mm", "st", "o_mm"))
        r_t, r_y, r_y_mm, r_hi, r_lo = (sem("r_" + n) for n in ("t", "y", "y_mm", "hi", "lo"))
        u_mm, u_aff, u_c1, u_conv, u_tanh, u_r, u_act, u_hi, u_lo = (sem("u_" + n) for n in (
            "mm", "aff", "c1", "conv", "tanh", "r", "act", "hi", "lo"))

        def tiles(w):
            return w.rearrange("(k p) c -> p k c", p=P)

        w_in_v, w_out_v, w_up_v, w_down_v = tiles(w_in), tiles(w_out), tiles(w_up), tiles(w_down)
        fox_in_v, fox_out_v = tiles(fox_w_in[0]), tiles(fox_w_out[0])
        ret_in_v, ret_out_v = tiles(ret_w_in[0]), tiles(ret_w_out[0])

        def block_out(eng, blk):
            eng.wait_ge(drained[blk.base % 2], blk.plus(2).over(2).at())

        def all_out(eng, blk):
            eng.wait_ge(drained[0], blk.plus(1).over(2).at())
            eng.wait_ge(drained[1], blk.over(2).at())

        block = ctx.enter_context(nc.Block())

        @block.sync
        def _(sp):
            def chunk(g, src, kk=KC, n=COL):
                if g.base >= RAW or g.i is not None:
                    sp.wait_ge(lo_done, g.at(1 - RAW))
                slot = g.base % RAW
                sp.dma_start(raw[:, slot, 0:kk * n].rearrange("p (k c) -> p k c", k=kk), src)\
                    .then_inc(raw_full[slot], 16)

            def in_block(g, w_v, c0, n=COL, kk=KC, first=0):
                for c in range(first, KT // kk):
                    chunk(g.plus(c), w_v[:, c * kk:(c + 1) * kk, bass.ds(c0, n)], kk, n)
                return g.plus(KT // kk)

            def out_blocks(g, w_v, k0, kt):
                for n in range(NOUT):
                    for c in range(kt // KC):
                        chunk(g.plus(n * (kt // KC) + c),
                              w_v[:, bass.ds(k0 + c * KC, KC), n * COL:(n + 1) * COL])
                return g.plus(NOUT * kt // KC)

            x_v = x[0].rearrange("(t p) d -> p t d", p=P)
            g = Count(0)
            for k in range(4):
                c = slice(k * COL, (k + 1) * COL)
                sp.dma_start(res[:, :, c], x_v[:, :, c]).then_inc(x_full[k], 16)
                chunk(g.plus(k), w_in_v[:, k * KC:(k + 1) * KC, C_QI:C_QI + COL])
            g = in_block(g, w_in_v, C_QI, first=4)
            g = in_block(g, w_in_v, C_QI + COL)
            g = in_block(g, w_in_v, C_KI, NARROW, NARROW_K)
            g = in_block(g, w_in_v, 0)
            g = in_block(g, w_in_v, COL)
            for c in (C_Q, C_K, C_V):
                g = in_block(g, w_in_v, c)
            g = out_blocks(g, w_out_v, 0, 4)
            g = out_blocks(g, w_out_v, 4, 4)
            for c in (C_Q, C_K, C_V):
                g = in_block(g, w_in_v, c + COL)
            g = out_blocks(g, w_out_v, 8, 4)
            g = out_blocks(g, w_out_v, 12, 2)
            g = out_blocks(g, w_out_v, 14, 2)
            assert g.base == FFN_0

            def ffn_in(g, i):
                g = in_block(g, w_up_v, i * COL)
                return in_block(g, w_up_v, i * COL + D_FF)

            per = FFN_IN + FFN_OUT
            ffn_in(g, 0)
            with sp.Fori(1, PAIRS) as i:
                g = ffn_in(Count(FFN_0 + FFN_IN - per, per, i), i)
                out_blocks(g, w_down_v, i * 4 - 4, 4)
            for half in range(2):
                out_blocks(Count(FOX_0 - FFN_OUT + 4 * half), w_down_v, 4 * PAIRS - 4 + 2 * half, 2)

            g = in_block(Count(FOX_0), fox_in_v, 0)
            g = in_block(g, fox_in_v, 4 * D, FOX_HEADS, KT)
            for b in range(1, 4):
                g = in_block(g, fox_in_v, b * D)
            per = FOX_IN + FOX_OUT
            with sp.Fori(1, FOX_GROUPS) as i:
                g = Count(FOX_0 + 1 + FOX_IN - per, per, i)
                for b in range(4):
                    g = in_block(g, fox_in_v, i * COL + b * D)
                out_blocks(g, fox_out_v, i * 4 - 4, 4)
            for half in range(2):
                out_blocks(Count(RET_0 - FOX_OUT + 4 * half), fox_out_v, 4 * FOX_GROUPS - 4 + 2 * half, 2)

            def ret_in(g, i):
                g = in_block(g, ret_in_v, i * COL)
                g = in_block(g, ret_in_v, i * COL + D)
                for b in range(4):
                    g = in_block(g, ret_in_v, i * (2 * COL) + 2 * D + (b // 2) * 2 * D + (b % 2) * COL)
                return g

            per = RET_IN + RET_OUT
            ret_in(Count(RET_0), 0)
            with sp.Fori(1, RET_GROUPS) as i:
                g = ret_in(Count(RET_0 + RET_IN - per, per, i), i)
                out_blocks(g, ret_out_v, i * 8 - 8, 8)
            out_blocks(Count(TOTAL - RET_OUT), ret_out_v, 8 * RET_GROUPS - 8, 8)

            def store(k, t, c):
                sp.wait_ge(out_ready[k], 1)
                sp.dma_start(out[0, t * P:(t + 1) * P, c:c + D // 2], res[:, t, c:c + D // 2]).then_inc(out_sem, 16)

            for k, (t, c) in enumerate(OUT_PARTS):
                store(k, t, c)
            sp.wait_ge(out_sem, 16 * len(OUT_PARTS))

        @block.gpsimd
        def _(pool):
            def load(dst, src, s):
                pool.dma_start(dst, src).then_inc(s, 16)

            def power(k, o, i_, eps):
                pool.wait_ge(want, k.at(1))
                n = i_.shape[1]
                c = 0 if eps == EPS else 1
                nc.gpsimd.tensor_tensor(o, i_, pconst[:, c:c + 1].to_broadcast([P, n]), ALU.add).then_inc(added, 1)
                pool.wait_ge(added, k.at(1))
                nc.gpsimd.tensor_tensor(o, o, pconst[:, 2:3].to_broadcast([P, n]), ALU.pow).then_inc(got, 1)

            def rows_power(k):
                power(Count(k), rs[:], ssq[:, 0:TOK], EPS)

            def heads_power(k):
                power(k, rstd[:], ssq[:], EPS)

            def var_power(k, eps):
                power(k, rstd[:, 0:TOK], mv[:, :, 1], eps)

            nc.gpsimd.memset(pconst[:, 0:1], EPS)
            nc.gpsimd.memset(pconst[:, 1:2], LN_EPS)
            nc.gpsimd.memset(pconst[:, 2:3], -0.5).then_inc(pc, 1)
            pool.wait_ge(pc, 1)
            rows_power(0)
            load(causal[:], causal_d, c_full)
            load(band, poolband_d, c_full)
            load(pw, pool_w.rearrange("g (t p) d -> p (g t) d", p=P), c_full)
            load(rot[:].rearrange("p a t c -> p (a t c)"), rotary_d, c_full)
            load(bfc[:], fox_b_f.rearrange("a h -> h a"), c_full)
            pool.wait_ge(vec_sb, 1)
            load(rows[0:2 * D_FF // P, :, :], taps.rearrange("a (j p) -> j a p", p=P), b_full)
            pool.wait_ge(drained[0], 2)
            load(wT[0:IDX_HEADS, :], kwT[64:64 + IDX_HEADS, :], w_full)
            pool.wait_ge(ki_part, 1)
            load(kiT[64:128, :], kiT[0:64, :], ki_full)
            pool.wait_ge(py_lo, 8)
            load(table[:], decay_d, dec_full)
            heads_power(Count(1))
            heads_power(Count(2))
            rows_power(3)
            all_out(pool, Count(FOX_B))
            load(gbc[:, 0, :], ln_gain[0:1, :].to_broadcast([P, D]), ln_full)
            load(gbc[:, 1, :], ln_bias[0:1, :].to_broadcast([P, D]), ln_full)
            heads_power(Count(4))
            with pool.Fori(1, FOX_GROUPS) as i:
                heads_power(Count(4, 1, i))
            var_power(Count(W_RET - 1), LN_EPS)
            pool.wait_ge(ln_used, 1)
            load(gbc[:, 0, :], ln_gain[1:2, :].to_broadcast([P, D]), ln_full)
            load(gbc[:, 1, :], ln_bias[1:2, :].to_broadcast([P, D]), ln_full)
            with pool.Fori(1, RET_GROUPS) as i:
                for h in range(RET_PAIR):
                    var_power(Count(W_RET - 2 + h, 2, i), GN_EPS)
            for h in range(RET_PAIR):
                var_power(Count(W_RET + RET_HEADS - 2 + h), GN_EPS)
            var_power(Count(W_RET + RET_HEADS), LN_EPS)
            for h in range(2):
                pool.wait_ge(ln_scaled, h + 1)
                c = slice(h * D // 2, (h + 1) * D // 2)
                nc.gpsimd.tensor_tensor(res[:, 0, c], res[:, 0, c], gbc[:, 1, c], ALU.add).then_inc(out_ready[2 + h], 1)

        @block.tensor
        def _(pe):
            def mm(o, l, r, start, stop):
                return nc.tensor.matmul(o, l, r, start=start, stop=stop)

            def chunk(g, b, lhs_hi, lhs_lo, k0, first, last, kk=KC, n=COL):
                pe.wait_ge(lo_done, g.at(1))
                slot = g.base % SPLIT
                for k in range(kk):
                    wh = w_hi[:, slot, k * n:(k + 1) * n]
                    wl = w_lo[:, slot, k * n:(k + 1) * n]
                    for t in range(TOK):
                        xh = lhs_hi[:, k0 + k, t * P:(t + 1) * P]
                        xl = lhs_lo[:, k0 + k, t * P:(t + 1) * P]
                        o = acc[b][t][:, 0:n]
                        mm(o, xh, wh, first and k == 0, False)
                        mm(o, xh, wl, False, False)
                        done = mm(o, xl, wh, False, last and k == kk - 1)
                done.then_inc(used, 1)

            def in_block(g, blk, step, slot, n=COL, kk=KC, build=None, hook=True):
                par = blk.base % 2
                if blk.plus(-1).some():
                    pe.wait_ge(drained[par], blk.over(2).at())
                for c in range(KT // kk):
                    if build is not None:
                        pe.wait_ge(xt_lo, 8 * build + c + 1)
                    chunk(g.plus(c), par, x_hi, x_lo, c * kk, c == 0, c == KT // kk - 1, kk, n)
                    if build is not None and c + 4 < 8:
                        xt(build, c + 4)
                    step(slot + c)

            def out_slot(g, blk, y0, kt, s, y=(y_hi, y_lo)):
                per = kt // KC
                nb, c = s // per, s % per
                par = (blk.base + nb) % 2
                if c == 0:
                    pe.wait_ge(drained[par], blk.plus(nb).over(2).at())
                chunk(g.plus(s), par, *y, y0 + c * KC, c == 0, c == per - 1)

            def out_blocks(g, blk, y0, kt, step, slot, y=(y_hi, y_lo)):
                for s in range(NOUT * kt // KC):
                    out_slot(g, blk, y0, kt, s, y)
                    step(slot + s)

            def xt(phase, j):
                if j >= 4:
                    pe.wait_ge(xt_lo, 8 * phase + j - 3)
                if phase == 0:
                    pe.wait_ge(x_full[j // 2], 16)
                elif phase == 3:
                    pe.wait_ge(xn_ready, 1 + j // 2)
                else:
                    block_out(pe, Count((FFN_B, FOX_B)[phase - 1] - 4 + j // 2))
                for k in range(2):
                    for t in range(TOK):
                        c = k * S + t * P
                        done = nc.tensor.transpose(M[j % 4][:, c:c + P],
                                                   res[:, t, (2 * j + k) * P:(2 * j + k + 1) * P], ident[:])
                done.then_inc(xt_mm, 1)

            def xt_start(phase):
                for j in range(4):
                    xt(phase, j)

            def last_out(g, blk, y0, phase):
                for s in range(NOUT):
                    out_slot(g, blk, y0, 2, s)
                    if phase < 3 and s >= 2:
                        xt(phase, 2 * s - 4)
                        xt(phase, 2 * s - 3)

            def narrow_block(g, blk, n, kk):
                par = blk.base % 2
                all_out(pe, blk)
                o = acc[par][0][:, 0:S]
                for c in range(KT // kk):
                    pe.wait_ge(lo_done, g.at(c + 1))
                    slot = (g.base + c) % SPLIT
                    for k in range(kk):
                        wh, wl = w_hi[:, slot, k * n:k * n + P], w_lo[:, slot, k * n:k * n + P]
                        t = c * kk + k
                        mm(o, wh, x_hi[:, t, :], t == 0, False)
                        mm(o, wl, x_hi[:, t, :], False, False)
                        done = mm(o, wh, x_lo[:, t, :], False, t == KT - 1)
                    done.then_inc(used, 1)

            none = lambda s: None

            def att_step(A, what, n, h, group, forget, blk0):
                if what == "T":
                    pe.wait_ge(A.normed, group.at(1))
                    if h > 0:
                        pe.wait_ge(A.qk_sb, n.at())
                    for a in range(2):
                        for t in range(TOK):
                            c = a * S + t * P
                            done = nc.tensor.transpose(M[0][:, c:c + P], qk[:, t, a * GROUP + h, :], ident[:])
                    done.then_inc(A.qk_mm, 1)
                elif what == "S":
                    pe.wait_ge(A.qk_sb, n.at(1))
                    if h > 0:
                        pe.wait_ge(A.maxed, n.at())
                    if forget:
                        pe.wait_ge(A.ck, n.at(1))
                    for t in range(TOK):
                        o = M[1][:, t * P:(1 + 2 * t) * P]
                        keys = (t + 1) * P
                        done = mm(o, qT[:, 0, t * P:(t + 1) * P], kT[:, 0, 0:keys], True, not forget)
                        if forget:
                            done = mm(o, minus[:], ckT[:, 0:keys], False, True)
                    done.then_inc(A.s_mm, 1)
                elif what == "PT":
                    pe.wait_ge(A.exped, n.at(1))
                    if h > 0:
                        pe.wait_ge(A.p_sb, n.at())
                    for c in range(3):
                        done = nc.tensor.transpose(M[2][:, c * P:(c + 1) * P], p_sb[:, c * P:(c + 1) * P], ident[:])
                    done.then_inc(A.p_mm, 1)
                elif what == "V":
                    if h == 0:
                        all_out(pe, blk0)
                    pe.wait_ge(A.p_sb, n.at(1))
                    if h > 0:
                        pe.wait_ge(A.y_lo, n.at())
                    v = z[:, 2, :, h * HD:(h + 1) * HD]
                    mm(M[3][:, 0:P], pT[:, 0:P], v[:, 0, :], True, True)
                    mm(M[3][:, P:2 * P], pT[:, P:2 * P], v[:, 0, :], True, False)
                    mm(M[3][:, P:2 * P], pT[:, 2 * P:3 * P], v[:, 1, :], False, True).then_inc(A.o_mm, 1)
                elif what == "Y":
                    pe.wait_ge(A.y_sb, n.at(1))
                    for t in range(TOK):
                        done = nc.tensor.transpose(M[3][:, t * P:(t + 1) * P], y_att[:, t, :], ident[:])
                    done.then_inc(A.y_mm, 1)

            ATT_AT = {0: "T", 1: "S", 3: "PT", 4: "V", 5: "Y"}

            def att_slots(A, n, group, forget, blk0, stride=STRIDE):
                def step(s):
                    for h in range(GROUP):
                        if s - stride * h in ATT_AT:
                            att_step(A, ATT_AT[s - stride * h], n.plus(h), h, group, forget, blk0)
                return step

            def att_tail(g, blk, y0, step, y0_last, lo, phase):
                for s in range(TAIL):
                    if s < 8:
                        out_slot(g, blk, y0, 4, s)
                    elif HALF_AT <= s < HALF_AT + 4:
                        if s == HALF_AT:
                            pe.wait_ge(lo[0], lo[1] - 2)
                        out_slot(g.plus(8), blk.plus(4), y0_last, 2, s - HALF_AT)
                    step(s)
                pe.wait_ge(*lo)
                last_out(g.plus(12), blk.plus(8), y0_last + 2, phase)

            pe.wait_ge(v_full, 16 * 2)
            nc.tensor.transpose(M[0][:, 0:76], rows[0:VECTORS, 3, :], ident[0:VECTORS, 0:VECTORS]).then_inc(vec_mm, 1)
            pe.wait_ge(vec_sb, 1)

            def spread(s):
                if s == 10:
                    pe.wait_ge(d_full, 1)
                    pe.wait_ge(xt_lo, 8)
                    mm(M[0][:, 0:S], ones[:], diag, True, True).then_inc(rbc_mm, 1)

            xt_start(0)
            in_block(Count(0), Count(0), none, 0, build=0)
            in_block(Count(8), Count(1), spread, 8)
            narrow_block(Count(16), Count(2), NARROW, NARROW_K)

            def indexer(s):
                if s < 4:
                    if s == 0:
                        all_out(pe, Count(2))
                        pe.wait_ge(rbc_sb, 1)
                    for k in range(2):
                        for t in range(TOK):
                            f = (2 * s + k) * P
                            c = k * S + t * P
                            done = nc.tensor.transpose(
                                M[s][:, c:c + P], z[:, f // COL, t, f % COL:f % COL + P], ident[:])
                    done.then_inc(idx_mm, 1)
                elif s == 4:
                    pe.wait_ge(w_full, 16)
                    pe.wait_ge(idx_sb, 4)
                    for t in range(TOK):
                        done = nc.tensor.transpose(M[2][:, t * 16:(t + 1) * 16], wT[0:IDX_HEADS, t * P:(t + 1) * P],
                                                   ident[0:IDX_HEADS, 0:IDX_HEADS])
                    done.then_inc(idx_mm, 1)
                elif s < 16:
                    for h in range(min(16, 2 * (s - 5)), min(16, 2 * (s - 5) + 2)):
                        if h == 0:
                            pe.wait_ge(ki_full, 16)
                        else:
                            if h >= 2:
                                pe.wait_ge(rel_sb, h - 1)
                        half = slice(64 * (h % 2), 64 * (h % 2) + 64)
                        for t in range(TOK):
                            done = mm(M[h % 2][:, t * P:(1 + 2 * t) * P], qiT[half, h // 2, t * P:(t + 1) * P],
                                      kiT[half, 0:(t + 1) * P], True, True)
                        done.then_inc(rel_mm, 1)

            in_block(Count(18), Count(3), indexer, 0)
            in_block(Count(26), Count(4), indexer, 8)

            def pool_step(s):
                if s < 8:
                    b = s % 2
                    if s == 0:
                        all_out(pe, Count(5))
                        pe.wait_ge(c_full, 16 * 5)
                    if s >= 2:
                        pe.wait_ge(pd_sb, s - 1)
                    else:
                        pe.wait_ge(rel_sb, 16)
                    grp = s // 2
                    u = z[:, 2 + s // 4, :, (s % 4) * P:(s % 4 + 1) * P]
                    c = grp * 3 * P
                    o = M[2 + b]
                    mm(o[:, 0:S], u[:, 0, :], band[:, c:c + S], True, False)
                    mm(o[:, P:S], u[:, 1, :], band[:, c + S:c + 3 * P], False, True).then_inc(pd_mm, 1)
                elif s < 16:
                    t = s - 8
                    grp = t // 2
                    pe.wait_ge(pd_sb, 8)
                    if t >= 2:
                        pe.wait_ge(py_lo, t - 1)
                    for k in range(2):
                        done = mm(M[t % 2][:, 0:S], pw[:, 2 * grp + k, (t % 2) * P:(t % 2 + 1) * P],
                                  poolT[:, 2 * grp + k, :], k == 0, k == 1)
                    done.then_inc(py_mm, 1)

            for b in range(3):
                in_block(Count(34 + 8 * b), Count(5 + b), pool_step, 8 * b)
            pe.wait_ge(py_lo, 8)
            out_blocks(Count(58), Count(8), 0, 4, none, 0)
            pe.wait_ge(b_full, 16)
            n = 2 * D_FF // P
            for j in range(4):
                done = nc.tensor.transpose(M[0][:, j * P:j * P + n], rows[0:n, j, :], ident[0:n, 0:n])
            done.then_inc(vec_mm, 1)
            out_blocks(Count(66), Count(12), 4, 4, none, 0)
            pe.wait_ge(vec_sb, 2)
            step = att_slots(att, Count(0), Count(0), False, Count(8))
            for b in range(3):
                in_block(Count(74 + 8 * b), Count(16 + b), step, 8 * b)
            pe.wait_ge(att.y_lo, 4)
            step = att_slots(att, Count(4), Count(1), False, Count(19), TAIL_STRIDE)
            att_tail(Count(98), Count(19), 0, step, 4, (att.y_lo, 8), 1)

            def ffn_slots(pair, blk0, starts=FFN_AT):
                def step(s):
                    if s in starts:
                        f = starts.index(s)
                        if f == 0:
                            all_out(pe, blk0)
                        for a in range(2):
                            for t in range(TOK):
                                c = a * S + t * P
                                done = nc.tensor.transpose(M[f][:, c:c + P], z[:, a, t, f * P:(f + 1) * P], ident[:])
                        done.then_inc(u_mm, 1)
                return step

            in_block(Count(FFN_0), Count(FFN_B), none, 0, build=1)
            in_block(Count(FFN_0 + 8), Count(FFN_B + 1), none, 8)
            per = FFN_IN + FFN_OUT
            def ffn_pair(i, last):
                g = Count(FFN_0 + FFN_IN - per, per, i) if not last else Count(FOX_0 - 2 * FFN_OUT - FFN_IN)
                blk = Count(FFN_B + 2 - 6, 6, i) if not last else Count(FOX_B - 14)
                pair = Count(-1, 1, i) if not last else Count(PAIRS - 2)
                step = ffn_slots(pair, blk)
                in_block(g, blk, step, 0)
                in_block(g.plus(8), blk.plus(1), step, 8)
                pe.wait_ge(u_lo, pair.at(1, 4))
                step = none
                if last:
                    step = ffn_slots(Count(PAIRS - 1), blk.plus(2), FFN_TAIL_AT)
                out_blocks(g.plus(16), blk.plus(2), 0, 4, step, 0)
                return step

            with pe.Fori(1, PAIRS - 1) as i:
                ffn_pair(i, False)
            step = ffn_pair(None, True)
            pe.wait_ge(u_lo, 4 * PAIRS - 2)
            out_blocks(Count(FOX_0 - FFN_OUT), Count(FOX_B - 8), 4, 2, step, 8)
            pe.wait_ge(u_lo, 4 * PAIRS)
            last_out(Count(FOX_0 - 4), Count(FOX_B - 4), 6, 2)

            def forget(s):
                if s == 11:
                    pe.wait_ge(c_ready, 1)
                    pe.wait_ge(xt_lo, 24)
                    for t in range(TOK):
                        done = nc.tensor.transpose(M[0][:, t * 16:(t + 1) * 16], cT[:, t * P:(t + 1) * P],
                                                   ident[0:FOX_HEADS, 0:FOX_HEADS])
                    done.then_inc(f_mm, 1)

            in_block(Count(FOX_0), Count(FOX_B), none, 0, build=2)
            narrow_block(Count(FOX_0 + 8), Count(FOX_B + 1), FOX_HEADS, KT)
            for b in range(1, 4):
                in_block(Count(FOX_0 + 1 + 8 * b), Count(FOX_B + 1 + b), forget, 8 * b)
            per = FOX_IN + FOX_OUT
            def fox_group(i):
                last = i is None
                g = Count(FOX_0 + 1 + FOX_IN - per, per, i) if not last else Count(RET_0 - 2 * FOX_OUT - FOX_IN)
                blk = Count(FOX_B + 5 - 8, 8, i) if not last else Count(RET_B - 16)
                group = Count(-1, 1, i) if not last else Count(FOX_GROUPS - 2)
                n = Count(-4, 4, i) if not last else Count(FOX_HEADS - 8)
                step = att_slots(fox, n, group, True, blk)
                for b in range(4):
                    in_block(g.plus(8 * b), blk.plus(b), step, 8 * b)
                pe.wait_ge(fox.y_lo, n.at(4))
                if not last:
                    out_blocks(g.plus(32), blk.plus(4), 0, 4, none, 0)
                    return
                step = att_slots(fox, Count(FOX_HEADS - 4), Count(FOX_GROUPS - 1), True, blk.plus(4), TAIL_STRIDE)
                att_tail(g.plus(32), blk.plus(4), 0, step, 4, (fox.y_lo, FOX_HEADS), 3)

            with pe.Fori(1, FOX_GROUPS - 1) as i:
                fox_group(i)
            fox_group(None)

            def ret_step(what, n, h, group, blk0):
                if what == "T":
                    if h == 0:
                        all_out(pe, blk0)
                    pe.wait_ge(r_rot, group.at(1))
                    if h > 0:
                        pe.wait_ge(r_y, n.at())
                    for a in range(2):
                        for dt in range(2):
                            for t in range(TOK):
                                c = dt * S + t * P
                                src = qk[:, t, 4 * a + 2 * h + dt, :]
                                done = nc.tensor.transpose(M[a][:, c:c + P], src, ident[:])
                    done.then_inc(r_qk_mm, 1)
                elif what == "S":
                    pe.wait_ge(r_qk_sb, n.at(1))
                    if h > 0:
                        pe.wait_ge(r_lo, n.at())
                    for dt in range(2):
                        mm(M[2][:, 0:S], kT[:, dt, 0:P], qT[:, dt, :], dt == 0, dt == 1)
                    for dt in range(2):
                        done = mm(M[2][:, S:S + P], kT[:, dt, P:S], qT[:, dt, P:S], dt == 0, dt == 1)
                    done.then_inc(r_s_mm, 1)
                elif what == "O":
                    pe.wait_ge(r_st, n.at(1))
                    v = z[:, 2 + h, :, :]
                    mm(M[0][:], s_sb[:, 0:P], v[:, 0, :], True, True)
                    mm(M[1][:], s_sb[:, P:2 * P], v[:, 0, :], True, False)
                    mm(M[1][:], s_sb[:, 2 * P:3 * P], v[:, 1, :], False, True).then_inc(r_o_mm, 1)
                elif what == "Y":
                    pe.wait_ge(r_y, n.at(1))
                    for k in range(4):
                        for t in range(TOK):
                            c = (k % 2) * S + t * P
                            done = nc.tensor.transpose(M[2 + k // 2][:, c:c + P], y_sb[:, t, k * P:(k + 1) * P], ident[:])
                    done.then_inc(r_y_mm, 1)

            RET_AT = {0: "T", 2: "S", 4: "O", 7: "Y"}

            def ret_slots(n, group, blk0, stride=RET_STRIDE):
                def step(s):
                    for h in range(RET_PAIR):
                        if s - stride * h in RET_AT:
                            ret_step(RET_AT[s - stride * h], n.plus(h), h, group, blk0)
                return step

            xt_start(3)
            in_block(Count(RET_0), Count(RET_B), none, 0, build=3)
            for b in range(1, 6):
                in_block(Count(RET_0 + 8 * b), Count(RET_B + b), none, 8 * b)
            per = RET_IN + RET_OUT
            def ret_group(i):
                last = i is None
                g = Count(RET_0 + RET_IN - per, per, i) if not last else Count(TOTAL - 2 * RET_OUT - RET_IN)
                blk = Count(RET_B + 6 - 10, 10, i) if not last else Count(RET_B + 10 * RET_GROUPS - 14)
                group = Count(-1, 1, i) if not last else Count(RET_GROUPS - 2)
                n = Count(-2, 2, i) if not last else Count(RET_HEADS - 4)
                step = ret_slots(n, group, blk)
                for b in range(6):
                    in_block(g.plus(8 * b), blk.plus(b), step, 8 * b)
                pe.wait_ge(r_lo, n.at(2))
                step = none
                if last:
                    step = ret_slots(Count(RET_HEADS - 2), Count(RET_GROUPS - 1), blk.plus(6), RET_TAIL_STRIDE)
                out_blocks(g.plus(48), blk.plus(6), 0, 8, step, 0)

            with pe.Fori(1, RET_GROUPS - 1) as i:
                ret_group(i)
            ret_group(None)

            def last_head(s):
                if s == 1:
                    pe.wait_ge(r_lo, RET_HEADS)

            pe.wait_ge(r_lo, RET_HEADS - 1)
            out_blocks(Count(TOTAL - RET_OUT), Count(RET_B + 10 * RET_GROUPS - 4), 0, 8, last_head, 0,
                       (x_hi, x_lo))

        @block.scalar
        def _(act):
            def a_(o, i_, f, **kw):
                return nc.scalar.activation(o, i_, f, **kw)

            def split(g, k):
                g = g.plus(k)
                if g.i is None and g.base >= TOTAL:
                    return
                act.wait_ge(raw_full[g.base % RAW], g.over(RAW).at(1, 16))
                if g.plus(1 - SPLIT).some():
                    act.wait_ge(used, g.at(1 - SPLIT))
                a_(w_hi[:, g.base % SPLIT, :], raw[:, g.base % RAW, :], ACT.Copy).then_inc(hi_done, 1)

            def drain(g, blk, zb, free=(), rms=False):
                act.wait_ge(used, g.at())
                for s, v in free:
                    act.wait_ge(s, v)
                par = blk.base % 2
                for t in range(TOK):
                    done = a_(z[:, zb, t, :], acc[par][t][:], ACT.Copy, **({"scale": rs[:, t:t + 1]} if rms else {}))
                done.then_inc(drained[par], 1)

            def xt_out(phase, j):
                if phase == 3:
                    act.wait_ge(xt_mm, 24 + j + 1)
                    if j >= 2:
                        act.wait_ge(xt_lo, 24 + j - 1)
                    for k in range(2):
                        c = 2 * j + k
                        done = a_(tq[:, j % 2, k * S:(k + 1) * S], M[j % 4][:, k * S:(k + 1) * S], ACT.Identity,
                                  scale=gains[:, G_LG + c:G_LG + c + 1], bias=gains[:, G_LB + c:G_LB + c + 1])
                    done.then_inc(xt_aff, 1)
                    act.wait_ge(xt_aff, j + 1)
                    a_(x_hi[:, 2 * j:2 * j + 2, :].rearrange("p k s -> p (k s)"), tq[:, j % 2, :], ACT.Copy)\
                        .then_inc(xt_hi, 1)
                    return
                act.wait_ge(xt_mm, 8 * phase + j + 1)
                if phase == 2:
                    a_(x_hi[:, 2 * j:2 * j + 2, :].rearrange("p k s -> p (k s)"), M[j % 4][:], ACT.Copy)\
                        .then_inc(xt_hi, 1)
                    return
                c = (G_ATT, G_FFN)[phase] + 2 * j
                for k in range(2):
                    done = a_(x_hi[:, 2 * j + k, :], M[j % 4][:, k * S:(k + 1) * S], ACT.Copy,
                              scale=gains[:, c + k:c + k + 1])
                done.then_inc(xt_hi, 1)

            def first_block(phase, g):
                for j in range(4):
                    if phase == 0 and j < LEAD:
                        split(g, j)
                    xt_out(phase, j)
                for s in range(CH):
                    split(g, s + LEAD)
                    if s + 4 < 8:
                        xt_out(phase, s + 4)
                    elif phase < 2 and s < 6:
                        t = s - 4
                        if t == 0 and phase == 0:
                            for k in range(4):
                                act.wait_ge(x_full[k], 16)
                        elif t == 0:
                            all_out(act, Count(FFN_B))
                        done = a_(squares_out[:, t, :], res[:, t, :], ACT.Square, accum_out=ssq[:, t:t + 1])
                        if t == TOK - 1:
                            done.then_inc(ssq_done, 1)

            def slots(g, n, step, s0=0):
                for s in range(s0, s0 + n):
                    split(g, s - s0 + LEAD)
                    step(s)

            none = lambda s: None

            def att_step(A, what, n, h, gq, gk):
                if what == "E":
                    act.wait_ge(A.qk_mm, n.at(1))
                    if h > 0:
                        act.wait_ge(A.s_mm, n.at())
                    a_(qT[:, 0, :], M[0][:, 0:S], ACT.Copy, scale=gains[:, gq:gq + 1])
                    a_(kT[:, 0, :], M[0][:, S:2 * S], ACT.Copy, scale=gains[:, gk:gk + 1]).then_inc(A.qk_sb, 1)
                elif what == "P":
                    act.wait_ge(A.maxed, n.at(1))
                    if h > 0:
                        act.wait_ge(A.p_mm, n.at())
                        act.wait_ge(A.y_sb, n.at())
                    for t in range(TOK):
                        c = slice(t * P, (1 + 2 * t) * P)
                        done = a_(p_sb[:, c], s_sb[:, c], ACT.Exp, bias=nmax[:, t:t + 1], accum_out=sums[:, t:t + 1])
                    done.then_inc(A.exped, 1)
                elif what == "C":
                    act.wait_ge(A.p_mm, n.at(1))
                    if h > 0:
                        act.wait_ge(A.o_mm, n.at())
                    a_(pT, M[2][:, 0:3 * P], ACT.Copy).then_inc(A.p_sb, 1)

            def att_slots(A, n, gq, gk, y0, half, stride=STRIDE):
                def step(s):
                    for h in range(GROUP):
                        m, r = n.plus(h), s - stride * h
                        if r in (0, 2, 3):
                            att_step(A, {0: "E", 2: "P", 3: "C"}[r], m, h, gq, gk)
                        elif r == 5:
                            act.wait_ge(A.y_mm, m.at(1))
                            a_(y_hi[:, y0 + h, :], M[3][:, 0:S], ACT.Copy, scale=half).then_inc(A.y_hi, 1)
                return step

            def att_tail(g, step):
                for s in range(TAIL):
                    if s < 8:
                        split(g, s + LEAD)
                    elif HALF_AT <= s < HALF_AT + 4:
                        split(g, s - HALF_AT + 8 + LEAD)
                    step(s)
                slots(g.plus(12), 4, none)

            def load(dst, src):
                act.dma_start(dst, src).then_inc(v_full, 16)

            load(ident[:], ident_d)
            load(rows[0:VECTORS, 3, :], vectors)
            act.wait_ge(vec_mm, 1)
            a_(gains[:, 0:VECTORS], M[0][:, 0:VECTORS], ACT.Copy).then_inc(vec_sb, 1)
            act.wait_ge(vec_sb, 1)

            def spread(s):
                if s == 11:
                    act.wait_ge(rbc_mm, 1)
                    a_(rbc, M[0][:, 0:S], ACT.Copy).then_inc(rbc_sb, 1)

            first_block(0, Count(0))
            act.wait_ge(got, 1)
            drain(Count(8), Count(0), 0, rms=True)
            slots(Count(8), 8, spread, 8)
            drain(Count(16), Count(1), 1, rms=True)
            slots(Count(16), 2, none)
            act.wait_ge(used, 18)
            a_(kwT[0:NARROW, :], acc[0][0][0:NARROW, 0:S], ACT.Copy).then_inc(drained[0], 1)

            def indexer(s):
                if s < 4:
                    act.wait_ge(idx_mm, s + 1)
                    a_(qiT[:, 2 * s:2 * s + 2, :].rearrange("p k s -> p (k s)"), M[s][:], ACT.Copy).then_inc(idx_sb, 1)
                elif s > 4:
                    for h in range(min(16, 2 * (s - 5)), min(16, 2 * (s - 5) + 2)):
                        act.wait_ge(rel_mm, h + 1)
                        if h >= 2:
                            act.wait_ge(rel_add, h - 1)
                        a_(rel[:, h % 2, :], M[h % 2][:, 0:3 * P], ACT.Relu).then_inc(rel_sb, 1)

            slots(Count(18), 8, indexer)
            drain(Count(26), Count(3), 2, rms=True)
            slots(Count(26), 8, indexer, 8)
            drain(Count(34), Count(4), 3, rms=True)

            def pool_step(s):
                if s < 8:
                    act.wait_ge(pd_mm, s + 1)
                    a_(poolT[:, s, :], M[2 + s % 2][:, 0:S], ACT.Copy).then_inc(pd_sb, 1)
                elif s < 16:
                    t = s - 8
                    act.wait_ge(py_mm, t + 1)
                    a_(y_hi[:, t, :], M[t % 2][:, 0:S], ACT.Copy, scale=gains[:, G_POOL + t:G_POOL + t + 1])\
                        .then_inc(py_hi, 1)

            slots(Count(34), 8, pool_step)
            drain(Count(42), Count(5), 0, [(idx_mm, 4)], rms=True)
            slots(Count(42), 8, pool_step, 8)
            drain(Count(50), Count(6), 1, rms=True)
            slots(Count(50), 8, pool_step, 16)
            drain(Count(58), Count(7), 2, [(pd_mm, 8)], rms=True)
            slots(Count(58), 8, none)
            act.wait_ge(vec_mm, 2)
            a_(cols[:].rearrange("p a c -> p (a c)"), M[0][:], ACT.Copy).then_inc(vec_sb, 1)
            act.wait_ge(vec_sb, 2)
            slots(Count(66), 8, none)
            step = att_slots(att, Count(0), G_Q, G_K, 0, 1.0)
            slots(Count(74), 8, step)
            drain(Count(82), Count(16), 0, [(att.normed, 1)], rms=True)
            slots(Count(82), 8, step, 8)
            drain(Count(90), Count(17), 1, rms=True)
            slots(Count(90), 8, step, 16)
            drain(Count(98), Count(18), 2, [(att.o_mm, 4)], rms=True)
            att_tail(Count(98), att_slots(att, Count(4), G_Q, G_K, 4, 1.0, TAIL_STRIDE))

            def ffn_slots(pair, y0=0, starts=FFN_AT):
                def tile(f):
                    return Count(pair.base * 4 + f, pair.per * 4, pair.i)

                def tap(a, f, j):
                    c = pair.at(0, 4) + (a * D_FF // P + f)
                    return cols[:, j, bass.ds(c, 1)]

                def one(f, r):
                    n, b = tile(f), f % 2
                    if r == 0:
                        act.wait_ge(u_mm, n.at(1))
                        if f >= 2:
                            act.wait_ge(u_act, n.at(-1))
                        p2 = M[f][:].rearrange("p (a s) -> p a s", a=2)
                        a_(up[:, b, :, 2:S + 2], p2, ACT.Copy)
                        for a in range(2):
                            done = a_(cg[:, b, a, :], M[f][:, a * S:(a + 1) * S], ACT.Identity,
                                      scale=tap(a, f, 2), bias=tap(a, f, 3))
                        done.then_inc(u_aff, 1)
                    elif r == 1:
                        act.wait_ge(u_conv, n.at(1))
                        a_(th[:, b, :], cg3[:, b, 0, :], ACT.Tanh, scale=0.5).then_inc(u_tanh, 1)
                    elif r == 2:
                        act.wait_ge(u_act, n.at(1))
                        a_(y_hi[:, y0 + f, :], act_t[:, b, :], ACT.Copy).then_inc(u_hi, 1)

                def step(s):
                    for f in reversed(range(4)):
                        one(f, s - starts[f])
                return step

            g = Count(FFN_0)
            first_block(1, g)
            act.wait_ge(got, 4)
            drain(g.plus(8), Count(FFN_B), 0, rms=True)
            slots(g.plus(8), 8, none)
            drain(g.plus(16), Count(FFN_B + 1), 1, rms=True)
            per = FFN_IN + FFN_OUT

            def ffn_pair(i, tail=none):
                g = Count(FFN_0 + FFN_IN - per, per, i)
                blk = Count(FFN_B + 2 - 6, 6, i)
                step = ffn_slots(Count(-1, 1, i))
                slots(g, 8, step)
                drain(g.plus(8), blk, 0, [(u_mm, i * 4)], rms=True)
                slots(g.plus(8), 8, step, 8)
                drain(g.plus(16), blk.plus(1), 1, rms=True)
                slots(g.plus(16), 8, tail)

            with act.Fori(1, PAIRS - 1) as i:
                ffn_pair(i)
            step = ffn_slots(Count(PAIRS - 1), 4, FFN_TAIL_AT)
            ffn_pair(PAIRS - 1, step)
            slots(Count(FOX_0 - FFN_OUT), 8, step, 8)

            g = Count(FOX_0)
            first_block(2, g)
            drain(g.plus(8), Count(FOX_B), 0)

            def forget(s):
                if s == 9:
                    block_out(act, Count(FOX_B + 1))
                    a_(fT[:, 1, :], fT[:, 0, :], ACT.Abs).then_inc(f_abs, 1)
                    act.wait_ge(f_abs, 1)
                    a_(fT[:, 1, :], fT[:, 1, :], ACT.Exp, scale=-1.0).then_inc(f_exp, 1)
                    act.wait_ge(f_exp, 1)
                    a_(fT[:, 2, :], fT[:, 1, :], ACT.Ln, bias=1.0).then_inc(f_log, 1)

            def tanh_gate(gated, zb, t_sem, n, blk):
                block_out(act, blk)
                if n.some():
                    act.wait_ge(gated, n.at())
                a_(tmp[:, 0:TOK * COL], z[:, zb, :, :].rearrange("p t c -> p (t c)"), ACT.Tanh, scale=0.5)\
                    .then_inc(t_sem, 1)

            slots(g.plus(8), 1, none)
            for b in range(1, 4):
                slots(g.plus(1 + 8 * b), 8, forget, 8 * b)
                drain(g.plus(9 + 8 * b), Count(FOX_B + 1 + b), b)
            tanh_gate(fox.gated, 3, fox.tanh, Count(0), Count(FOX_B + 4))
            per = FOX_IN + FOX_OUT

            def fox_group(i):
                g = Count(FOX_0 + 1 + FOX_IN - per, per, i)
                blk = Count(FOX_B + 5 - 8, 8, i)
                step = att_slots(fox, Count(-4, 4, i), G_FQ, G_FK, 0, 0.5)
                slots(g, 8, step)
                drain(g.plus(8), blk, 0, [(fox.normed, i)])
                slots(g.plus(8), 8, step, 8)
                drain(g.plus(16), blk.plus(1), 1)
                slots(g.plus(16), 8, step, 16)
                drain(g.plus(24), blk.plus(2), 2, [(fox.o_mm, i * 4)])
                slots(g.plus(24), 8, none)
                drain(g.plus(32), blk.plus(3), 3, [(fox.y_sb, i * 4)])
                tanh_gate(fox.gated, 3, fox.tanh, Count(0, 1, i), blk.plus(3))

            with act.Fori(1, FOX_GROUPS - 1) as i:
                fox_group(i)
                slots(Count(FOX_0 + 1 + FOX_IN - per + 32, per, i), 8, none)
            fox_group(FOX_GROUPS - 1)
            att_tail(Count(RET_0 - 2 * FOX_OUT), att_slots(fox, Count(12), G_FQ, G_FK, 4, 0.5, TAIL_STRIDE))

            def ret_slots(n, y=y_hi, stride=RET_STRIDE):
                def step(s):
                    h, r = s // stride, s % stride
                    if h >= RET_PAIR:
                        return
                    m = n.plus(h)
                    if r == 0:
                        act.wait_ge(r_qk_mm, m.at(1))
                        if h > 0:
                            act.wait_ge(r_s_mm, m.at())
                        a_(qT[:].rearrange("p k s -> p (k s)"), M[0][:], ACT.Copy)
                        a_(kT[:].rearrange("p k s -> p (k s)"), M[1][:], ACT.Copy).then_inc(r_qk_sb, 1)
                    elif r == 6:
                        act.wait_ge(r_t, m.at(1))
                        if h > 0:
                            act.wait_ge(r_y_mm, m.at())
                        for t in range(TOK):
                            done = a_(y_sb[:, t, :], tmp[:, (2 + t) * COL:(3 + t) * COL], ACT.Copy, scale=rstd[:, t:t + 1])
                        done.then_inc(r_y, 1)
                    elif r == 7:
                        act.wait_ge(r_y_mm, m.at(1))
                        for k in range(2):
                            done = a_(y[:, 4 * h + 2 * k:4 * h + 2 * k + 2, :].rearrange("p k s -> p (k s)"),
                                      M[2 + k][:], ACT.Copy, scale=0.5)
                        done.then_inc(r_hi, 1)
                return step

            g = Count(RET_0)
            first_block(3, g)
            drain(g.plus(8), Count(RET_B), 0)
            for b in range(1, 6):
                slots(g.plus(8 * b), 8, none, 8 * b)
                drain(g.plus(8 * b + 8), Count(RET_B + b), b)
                if b >= 4:
                    tanh_gate(r_gated, b, r_tanh, Count(b - 4), Count(RET_B + b))
            per = RET_IN + RET_OUT

            def ret_group(i, tail):
                g = Count(RET_0 + RET_IN - per, per, i)
                blk = Count(RET_B + 6 - 10, 10, i)
                step = ret_slots(Count(-2, 2, i))
                free = {0: [(r_rot, i)], 2: [(r_o_mm, i * 2 - 1)], 3: [(r_o_mm, i * 2)], 4: [(r_t, i * 2)]}
                for b in range(6):
                    slots(g.plus(8 * b), 8, step, 8 * b)
                    drain(g.plus(8 * b + 8), blk.plus(b), b, free.get(b, ()))
                    if b >= 4:
                        tanh_gate(r_gated, b, r_tanh, Count(b - 4, 2, i), blk.plus(b))
                slots(g.plus(48), 16, tail)

            with act.Fori(1, RET_GROUPS - 1) as i:
                ret_group(i, none)
            ret_group(RET_GROUPS - 1, ret_slots(Count(RET_HEADS - 2), x_hi, RET_TAIL_STRIDE))
            slots(Count(TOTAL - RET_OUT), 16, none)
            act.wait_ge(got, W_RET + RET_HEADS + 1)
            act.wait_ge(ln_centred, 1)
            for h in range(2):
                c = slice(h * D // 2, (h + 1) * D // 2)
                a_(res[:, 0, c], res[:, 0, c], ACT.Copy, scale=rstd[:, 0:1]).then_inc(ln_scaled, 1)

        @block.vector
        def _(v):
            V = nc.vector

            def link(ins):
                dve_n[0] += 1
                ins.then_inc(dve, 1)
                v.wait_ge(dve, dve_n[0])

            class Chain:

                def __init__(self, s, n, per):
                    self.s, self.n, self.per, self.k = s, n, per, 0

                def link(self, ins):
                    self.k += 1
                    ins.then_inc(self.s, 1)
                    v.wait_ge(self.s, self.n.at(0, self.per) + self.k)

            def split(g, k):
                g = g.plus(k)
                if g.i is None and g.base >= TOTAL:
                    return
                v.wait_ge(hi_done, g.at(1))
                a = g.base % SPLIT
                V.tensor_tensor(w_lo[:, a, :], raw[:, g.base % RAW, :], w_hi[:, a, :], ALU.subtract)\
                    .then_inc(lo_done, 1)

            def add_out(g, blk, nb):
                par = blk.base % 2
                v.wait_ge(used, g.at())
                v.wait_ge(drained[par], blk.over(2).at())
                v.wait_ge(drained[1 - par], blk.plus(1).over(2).at())
                for t in range(TOK):
                    c = slice(nb * COL, (nb + 1) * COL)
                    done = V.tensor_tensor(res[:, t, c], acc[par][t][:], res[:, t, c], ALU.add)
                done.then_inc(drained[par], 1)

            def out_slots(g, blk, kt, step=lambda s: None, s0=0, after=lambda nb: None):
                for nb in range(NOUT):
                    for c in range(kt // KC):
                        s = nb * (kt // KC) + c
                        split(g, s + LEAD)
                        if c < kt // KC - 1:
                            step(s0 + s)
                    add_out(g.plus((nb + 1) * (kt // KC)), blk.plus(nb), nb)
                    after(nb)
                    step(s0 + s)

            def xt_out(phase, j):
                v.wait_ge(xt_hi, 8 * phase + j + 1)
                xl = x_lo[:, 2 * j:2 * j + 2, :]
                xh = x_hi[:, 2 * j:2 * j + 2, :]
                if phase >= 2:
                    V.tensor_tensor(xl.rearrange("p k s -> p (k s)"), M[j % 4][:] if phase == 2 else tq[:, j % 2, :],
                                    xh.rearrange("p k s -> p (k s)"), ALU.subtract).then_inc(xt_lo, 1)
                    return
                c = (G_ATT, G_FFN)[phase] + 2 * j
                for k in range(2):
                    done = V.scalar_tensor_tensor(xl[:, k, :], M[j % 4][:, k * S:(k + 1) * S],
                                                  gains[:, c + k:c + k + 1], xh[:, k, :], ALU.mult, ALU.subtract)
                done.then_inc(xt_lo, 1)

            def first_block(phase, g):
                for j in (range(4), range(2, 4), range(2, 4), ())[phase]:
                    if phase == 0 and j < LEAD:
                        split(g, j)
                    xt_out(phase, j)
                for s in range(CH):
                    split(g, s + LEAD)
                    if s + 4 < 8:
                        xt_out(phase, s + 4)
                if phase < 2:
                    v.wait_ge(ssq_done, phase + 1)
                    V.tensor_scalar(ssq[:, 0:TOK], ssq[:, 0:TOK], 1.0 / D, None, ALU.mult).then_inc(want, 1)

            def slots(g, n, step=lambda s: None, s0=0):
                for s in range(s0, s0 + n):
                    split(g, s - s0 + LEAD)
                    step(s)

            def power(k, ins):
                ins.then_inc(want, 1)
                v.wait_ge(got, k.at(1))

            def row_norms(k):
                for t in range(TOK):
                    done = V.bn_aggr(mv[:, t, :], stats[:, t, :, :].rearrange("p a b -> p (a b)"))
                done.then_inc(want, 1)
                v.wait_ge(want, k + 1)

            def norm_qk(A, link, part, zr, k):
                t = part % 2
                q = z[:, 0:2, t, :]
                if part < 2:
                    if part == 0:
                        block_out(v, zr)
                    sq = tmp[:, 2 * COL:4 * COL]
                    link(V.tensor_tensor(sq.rearrange("p (b c) -> p b c", b=2), q, q, ALU.mult))
                    done = V.tensor_reduce(ssq[:, 8 * t:8 * t + 8], sq.rearrange("p (h c) -> p h c", c=HD), AX, ALU.add)
                    link(done)
                    if part == 1:
                        V.tensor_scalar(ssq[:], ssq[:], 1.0 / HD, None, ALU.mult).then_inc(want, 1)
                else:
                    if part == 2:
                        v.wait_ge(got, k.at(1))
                    done = V.tensor_tensor(qk[:, t, :, :].rearrange("p (b h) c -> p b h c", b=2),
                                           q.rearrange("p b (h c) -> p b h c", c=HD),
                                           rstd[:, 8 * t:8 * t + 8].rearrange("p (b h c) -> p b h c", b=2, c=1)
                                           .to_broadcast([P, 2, GROUP, HD]), ALU.mult)
                    if part == 3:
                        done.then_inc(A.normed, 1)

            NORM_LINKS = 4

            def att_slots(A, n, y0, forget, head0, mask, stride=STRIDE):
                def one(h, r):
                    m = n.plus(h)
                    if r == 0 and forget:
                        if h > 0:
                            v.wait_ge(A.s_mm, m.at())
                        V.tensor_scalar(ckT, cT, ident[0:FOX_HEADS, bass.ds(head0 + h, 1)], None, ALU.mult)\
                            .then_inc(A.ck, 1)
                    elif r == 1:
                        v.wait_ge(A.s_mm, m.at(1))
                        if h > 0:
                            v.wait_ge(A.exped, m.at())
                        for t in range(TOK):
                            c = slice(t * P, (1 + 2 * t) * P)
                            if forget:
                                sc = c_nat[:, bass.ds(head0 + (t * FOX_HEADS + h), 1)]
                                done = V.scalar_tensor_tensor(s_sb[:, c], M[1][:, c], sc, mask[:, c], ALU.add, ALU.add)
                            else:
                                done = V.scalar_tensor_tensor(s_sb[:, c], M[1][:, c], HD ** -0.5, mask[:, c], ALU.mult, ALU.add)
                        Chain(A.masked, m, 1).link(done)
                        for t in range(TOK):
                            done = V.reduce_max(nmax[:, t:t + 1], s_sb[:, t * P:(1 + 2 * t) * P], AX, negate=True)
                        done.then_inc(A.maxed, 1)
                    elif r == 4:
                        v.wait_ge(A.o_mm, m.at(1))
                        if h > 0:
                            v.wait_ge(A.y_mm, m.at())
                        Chain(A.inverse, m, 1).link(V.reciprocal(rinv[:], sums[:]))
                        for t in range(TOK):
                            o = M[3][:, t * P:(t + 1) * P]
                            if forget:
                                done = V.scalar_tensor_tensor(y_att[:, t, :], o, rinv[:, t:t + 1],
                                                              z[:, 3, t, h * HD:(h + 1) * HD], ALU.mult, ALU.mult)
                            else:
                                done = V.tensor_scalar(y_att[:, t, :], o, rinv[:, t:t + 1], None, ALU.mult)
                        done.then_inc(A.y_sb, 1)
                    elif r == 5:
                        v.wait_ge(A.y_hi, m.at(1))
                        V.scalar_tensor_tensor(y_lo[:, y0 + h, :], M[3][:, 0:S], 0.5 if forget else 1.0,
                                               y_hi[:, y0 + h, :], ALU.mult, ALU.subtract).then_inc(A.y_lo, 1)

                def step(s):
                    for h in range(GROUP):
                        one(h, s - stride * h)
                return step

            def last_out(g, blk, phase, after=lambda nb: None):
                for nb in range(NOUT):
                    if phase < 3 or nb == 0:
                        split(g, nb + LEAD)
                    if phase < 3 and nb == NOUT - 1:
                        xt_out(phase, 0)
                        xt_out(phase, 1)
                    add_out(g.plus(1 + nb), blk.plus(nb), nb)
                    after(nb)

            def att_tail(g, blk, step, phase, after=lambda nb: None):
                for s in range(TAIL):
                    step(s)
                    if s < 8:
                        split(g, s + LEAD)
                    elif HALF_AT <= s < HALF_AT + 4:
                        split(g, s - HALF_AT + 8 + LEAD)
                    if s < 8 and s % 2 == 1:
                        add_out(g.plus(s + 1), blk.plus(s // 2), s // 2)
                    elif HALF_AT <= s < HALF_AT + 4:
                        nb = s - HALF_AT
                        add_out(g.plus(9 + nb), blk.plus(4 + nb), nb)
                last_out(g.plus(12), blk.plus(8), phase, after)

            V.memset(minus[:], -1.0)
            V.memset(isc, 0.0)
            V.memset(ones[:], 1.0)
            link(V.memset(small[:], 0.0))
            v.wait_ge(vec_sb, 1)
            link(V.tensor_scalar(gains[:, G_FQ:G_FQ + 1], gains[:, G_FQ:G_FQ + 1], HD ** -0.5, None, ALU.mult))

            def spread(s):
                if s == 9:
                    v.wait_ge(got, 1)
                    for t in range(TOK):
                        done = V.tensor_scalar(diag[:, t * P:(t + 1) * P], ident[:], rs[:, t:t + 1], None, ALU.mult)
                    done.then_inc(d_full, 1)

            first_block(0, Count(0))
            slots(Count(8), 10, spread, 8)

            def indexer(s):
                if s == 1:
                    block_out(v, Count(2))
                    v.wait_ge(rbc_sb, 1)
                    V.tensor_tensor(kiT[0:IDX_DIM, :], kwT[0:IDX_DIM, :], rbc[0:IDX_DIM, :], ALU.mult).then_inc(ki_part, 1)
                elif s == 4:
                    v.wait_ge(idx_mm, 5)
                    for t in range(TOK):
                        done = V.tensor_scalar(w_idx[:, t, :], M[2][:, t * IDX_HEADS:(t + 1) * IDX_HEADS], rs[:, t:t + 1],
                                               float(IDX_HEADS * IDX_DIM) ** -0.5, ALU.mult, ALU.mult)
                    link(done)
                if s < 5:
                    return
                for h in range(min(16, 2 * (s - 5)), min(16, 2 * (s - 5) + 2)):
                    v.wait_ge(rel_sb, h + 1)
                    if h > 0:
                        v.wait_ge(rel_add, h)
                    for t in range(TOK):
                        c = slice(t * P, (1 + 2 * t) * P)
                        done = V.scalar_tensor_tensor(isc[:, c], rel[:, h % 2, c], w_idx[:, t, h:h + 1], isc[:, c],
                                                      ALU.mult, ALU.add)
                    done.then_inc(rel_add, 1)

            slots(Count(18), 16, indexer)

            def topk(s):
                if s == 0:
                    v.wait_ge(rel_add, 16)
                    v.wait_ge(c_full, 16 * 5)
                    link(V.tensor_tensor(isc, isc, causal[:], ALU.add))
                if s < 8:
                    for t in range(TOK):
                        c = slice(t * P, (1 + 2 * t) * P)
                        done = V.max(top8[:, t, :], isc[:, c])
                    link(done)
                    for t in range(TOK):
                        c = slice(t * P, (1 + 2 * t) * P)
                        done = V.match_replace(isc[:, c], top8[:, t, :], isc[:, c], TAKEN)
                    link(done)
                if s == 8:
                    link(V.tensor_scalar(pen[:], isc, TAKEN * 0.9, NEG, ALU.is_gt, ALU.mult))
                    link(V.tensor_tensor(pen[:], pen[:], causal[:], ALU.min))

            def pool_step(s):
                topk(s)
                if 8 <= s < 16:
                    t = s - 8
                    v.wait_ge(py_hi, t + 1)
                    V.scalar_tensor_tensor(y_lo[:, t, :], M[t % 2][:, 0:S], gains[:, G_POOL + t:G_POOL + t + 1],
                                           y_hi[:, t, :], ALU.mult, ALU.subtract).then_inc(py_lo, 1)

            slots(Count(34), 24, pool_step)

            def norm_step(A, link, zr, s0, k, every=1):
                def step(s):
                    if s in range(s0, s0 + 4 * every, every):
                        norm_qk(A, link, (s - s0) // every, zr, k)
                return step

            def both(one, two):
                def step(s):
                    one(s)
                    two(s)
                return step

            out_slots(Count(58), Count(8), 4, norm_step(att, link, Count(6), 0, Count(1), 2))
            out_slots(Count(66), Count(12), 4)
            slots(Count(74), 24, both(att_slots(att, Count(0), 0, False, 0, pen),
                                      norm_step(att, link, Count(17), 18, Count(2))))
            att_tail(Count(98), Count(19), att_slots(att, Count(4), 4, False, 0, pen, TAIL_STRIDE), 1)

            g = Count(FFN_0)
            first_block(1, g)
            link(V.memset(up[:, :, :, 0:2], 0.0))
            slots(g.plus(8), 8)

            def ffn_slots(pair, y0=0, starts=FFN_AT):
                def tile(f):
                    return Count(pair.base * 4 + f, pair.per * 4, pair.i)

                def tap(a, f, j):
                    c = pair.at(0, 4) + (a * D_FF // P + f)
                    return cols[:, j, bass.ds(c, 1)]

                def one(f, r):
                    n, b = tile(f), f % 2
                    if r == 0:
                        v.wait_ge(u_aff, n.at(1))
                        for a in range(2):
                            done = V.scalar_tensor_tensor(cg2[:, b, a, :], up[:, b, a, 1:S + 1], tap(a, f, 1),
                                                          cg[:, b, a, :], ALU.mult, ALU.add)
                        done.then_inc(u_c1, 1)
                        v.wait_ge(u_c1, n.at(1))
                        for a in range(2):
                            done = V.scalar_tensor_tensor(cg3[:, b, a, :], up[:, b, a, 0:S], tap(a, f, 0),
                                                          cg2[:, b, a, :], ALU.mult, ALU.add)
                        done.then_inc(u_conv, 1)
                    elif r == 1:
                        v.wait_ge(u_tanh, n.at(1))
                        if f >= 2:
                            v.wait_ge(u_hi, n.at(-1))
                        V.scalar_tensor_tensor(act_r[:, b, :], th[:, b, :], 1.0, cg3[:, b, 0, :], ALU.add, ALU.mult)\
                            .then_inc(u_r, 1)
                        v.wait_ge(u_r, n.at(1))
                        V.scalar_tensor_tensor(act_t[:, b, :], act_r[:, b, :], 0.5, cg3[:, b, 1, :], ALU.mult, ALU.mult)\
                            .then_inc(u_act, 1)
                    elif r == 2:
                        v.wait_ge(u_hi, n.at(1))
                        V.tensor_tensor(y_lo[:, y0 + f, :], act_t[:, b, :], y_hi[:, y0 + f, :], ALU.subtract).then_inc(u_lo, 1)

                def step(s):
                    for f in reversed(range(4)):
                        one(f, s - starts[f])
                return step

            per = FFN_IN + FFN_OUT

            def ffn_pair(i, tail=lambda s: None):
                g = Count(FFN_0 + FFN_IN - per, per, i)
                slots(g, 16, ffn_slots(Count(-1, 1, i)))
                out_slots(g.plus(16), Count(FFN_B + 4 - 6, 6, i), 4, tail)

            with v.Fori(1, PAIRS - 1) as i:
                ffn_pair(i)
            step = ffn_slots(Count(PAIRS - 1), 4, FFN_TAIL_AT)
            ffn_pair(PAIRS - 1, step)
            out_slots(Count(FOX_0 - FFN_OUT), Count(FOX_B - 8), 2, step, 8)
            last_out(Count(FOX_0 - 4), Count(FOX_B - 4), 2)

            g = Count(FOX_0)
            first_block(2, g)
            v.wait_ge(xt_mm, 24)
            for t in range(TOK):
                done = V.tensor_scalar(res[:, t, :], res[:, t, :], ALPHA, None, ALU.mult)
            link(done)
            slots(g.plus(8), 1)
            v.wait_ge(used, FOX_0 + 9)
            V.memset(fT[:, 4, :], 0.0)
            par = (FOX_B + 1) % 2
            V.tensor_scalar(fT[:, 0, :], acc[par][0][0:FOX_HEADS, 0:S], bfc[:, 0:1], None, ALU.add)\
                .then_inc(drained[par], 1)
            block_out(v, Count(FOX_B + 1))

            def forget(s):
                if s == 10:
                    v.wait_ge(f_log, 1)
                    link(V.scalar_tensor_tensor(fT[:, 3, :], fT[:, 0, :], 0.0, fT[:, 2, :], ALU.min, ALU.subtract))
                    V.tensor_tensor_scan(cT, fT[:, 3, :], fT[:, 4, :], 0.0, ALU.add, ALU.add).then_inc(c_ready, 1)
                    v.wait_ge(c_ready, 1)
                if s == 12:
                    v.wait_ge(f_mm, 1)
                    link(V.tensor_copy(c_nat[:], M[0][:, 0:TOK * FOX_HEADS]))

            def group_norm(group, zr):
                return norm_step(fox, Chain(fox_norm, group, NORM_LINKS).link, zr, 18, group.plus(4))

            slots(g.plus(9), 24, both(forget, group_norm(Count(0), Count(FOX_B + 2))), 8)

            def gate(t_sem, g_sem, zb, n):
                v.wait_ge(t_sem, n)
                t = z[:, zb, :, :].rearrange("p t c -> p (t c)")
                V.scalar_tensor_tensor(t, tmp[:, 0:TOK * COL], 1.0, t, ALU.add, ALU.mult).then_inc(g_sem, 1)
                v.wait_ge(g_sem, n)

            gate(fox.tanh, fox.gated, 3, 1)
            per = FOX_IN + FOX_OUT

            def fox_group(i):
                g = Count(FOX_0 + 1 + FOX_IN - per, per, i)
                slots(g, 32, both(att_slots(fox, Count(-4, 4, i), 0, True, i * 4 - 4, causal),
                                  group_norm(Count(0, 1, i), Count(FOX_B + 6 - 8, 8, i))))
                gate(fox.tanh, fox.gated, 3, i + 1)

            with v.Fori(1, FOX_GROUPS - 1) as i:
                fox_group(i)
                out_slots(Count(FOX_0 + 1 + FOX_IN - per + 32, per, i), Count(FOX_B + 9 - 8, 8, i), 4)
            fox_group(FOX_GROUPS - 1)

            def stats_after(first):
                def after(nb):
                    block_out(v, Count(first + nb))
                    for t in range(TOK):
                        done = V.bn_stats(stats[:, t, nb, :], res[:, t, nb * COL:(nb + 1) * COL])
                    if nb == NOUT - 1:
                        link(done)
                return after

            att_tail(Count(RET_0 - 2 * FOX_OUT), Count(RET_B - 12),
                     att_slots(fox, Count(12), 4, True, 12, causal, TAIL_STRIDE), 3, stats_after(RET_B - 4))
            row_norms(W_RET - 1)
            g = Count(RET_0)
            split(g, 0)
            v.wait_ge(got, W_RET)

            def normalise(nb):
                c = slice(nb * COL, (nb + 1) * COL)
                for t in range(TOK):
                    done = V.tensor_scalar(res[:, t, c], res[:, t, c], mv[:, t, 0:1], rstd[:, t:t + 1],
                                           ALU.subtract, ALU.mult)
                done.then_inc(xn_ready, 1)

            normalise(0)
            normalise(1)
            xt_out(3, 0)
            xt_out(3, 1)
            split(g, 1)
            normalise(2)
            xt_out(3, 2)
            split(g, 2)
            normalise(3)
            xt_out(3, 3)
            v.wait_ge(xn_ready, NOUT)

            def rotate(group, zr):
                ch = Chain(r_rot_chain, group, 7)

                def step(s):
                    if s not in (18, 20, 22, 24):
                        return
                    a, t = (s - 18) // 4, (s - 18) // 2 % 2
                    if s == 18:
                        block_out(v, zr)
                    m = rp.rearrange("p (x a h c) -> p x a h c", x=4, a=2, h=2)
                    src = z[:, a, t, :].rearrange("p (h f c) -> p h f c", h=2, f=2)
                    cos = rot[:, 0, t:t + 1, :].to_broadcast([P, 2, P])
                    sin = rot[:, 1, t:t + 1, :].to_broadcast([P, 2, P])
                    V.tensor_tensor(m[:, 0, a], src[:, :, 0, :], cos, ALU.mult)
                    V.tensor_tensor(m[:, 1, a], src[:, :, 1, :], sin, ALU.mult)
                    V.tensor_tensor(m[:, 2, a], src[:, :, 0, :], sin, ALU.mult)
                    ch.link(V.tensor_tensor(m[:, 3, a], src[:, :, 1, :], cos, ALU.mult))
                    dst = qk[:, t, 4 * a:4 * a + 4, :].rearrange("p (h f) c -> p h f c", h=2)
                    V.tensor_tensor(dst[:, :, 0, :], m[:, 0, a], m[:, 1, a], ALU.subtract)
                    done = V.tensor_tensor(dst[:, :, 1, :], m[:, 2, a], m[:, 3, a], ALU.add)
                    if s < 24:
                        ch.link(done)
                    else:
                        done.then_inc(r_rot, 1)
                        v.wait_ge(r_rot, group.at(1))
                return step

            def ret_slots(n, head0, yh=y_hi, yl=y_lo, stride=RET_STRIDE):
                def step(s):
                    h, r = s // stride, s % stride
                    if h >= RET_PAIR:
                        return
                    m = n.plus(h)
                    if r == 2:
                        v.wait_ge(r_s_mm, m.at(1))
                        if h > 0:
                            v.wait_ge(r_o_mm, m.at())
                        V.tensor_tensor(s_sb[:], M[2][:, 0:3 * P], table[:, bass.ds((head0 + h) * (3 * P), 3 * P)], ALU.mult)\
                            .then_inc(r_st, 1)
                    elif r == 4:
                        v.wait_ge(r_o_mm, m.at(1))
                        if h > 0:
                            v.wait_ge(r_y, m.at())
                        ch = Chain(r_chain, m, 1)
                        for t in range(TOK):
                            done = V.bn_stats(stats[:, t, 0, :], M[t][:])
                        ch.link(done)
                        V.memset(small[:, 3:4], 0.0)
                        for t in range(TOK):
                            done = V.bn_aggr(mv[:, t, :], stats[:, t, 0, :])
                        power(m.plus(W_RET), done)
                        for t in range(TOK):
                            done = V.scalar_tensor_tensor(tmp[:, (2 + t) * COL:(3 + t) * COL], M[t][:], mv[:, t, 0:1],
                                                          z[:, 4 + h, t, :], ALU.subtract, ALU.mult)
                        done.then_inc(r_t, 1)
                    elif r == 7:
                        v.wait_ge(r_hi, m.at(1))
                        for k in range(2):
                            t = 4 * h + 2 * k
                            done = V.scalar_tensor_tensor(yl[:, t:t + 2, :].rearrange("p k s -> p (k s)"), M[2 + k][:], 0.5,
                                                          yh[:, t:t + 2, :].rearrange("p k s -> p (k s)"),
                                                          ALU.mult, ALU.subtract)
                        done.then_inc(r_lo, 1)
                return step

            v.wait_ge(dec_full, 16)
            g = Count(RET_0)
            first_block(3, g)

            def residual(s):
                if s in (8, 10, 12, 14):
                    t = (s - 8) // 4
                    if s == 8:
                        v.wait_ge(xt_mm, 32)
                        v.wait_ge(ln_full, 32)
                    if s % 4 == 0:
                        link(V.scalar_tensor_tensor(res[:, t, :], res[:, t, :], ALPHA, gbc[:, 0, :], ALU.mult, ALU.mult))
                    else:
                        link(V.scalar_tensor_tensor(res[:, t, :], gbc[:, 1, :], ALPHA, res[:, t, :], ALU.mult, ALU.add))
                    if s == 14:
                        V.memset(small[:, 1:2], 0.0).then_inc(ln_used, 1)

            st = rotate(Count(0), Count(RET_B + 1))
            slots(g.plus(8), 32, both(residual, st), 8)
            gate(r_tanh, r_gated, 4, 1)
            slots(g.plus(40), 8, st, 40)
            gate(r_tanh, r_gated, 5, 2)
            per = RET_IN + RET_OUT

            def ret_group(i, tail=lambda s: None):
                g = Count(RET_0 + RET_IN - per, per, i)
                st = ret_slots(Count(-2, 2, i), i * 2 - 2)
                ro = rotate(Count(0, 1, i), Count(RET_B + 7 - 10, 10, i))
                slots(g, 40, both(st, ro))
                gate(r_tanh, r_gated, 4, i * 2 + 1)
                slots(g.plus(40), 8, st, 40)
                gate(r_tanh, r_gated, 5, i * 2 + 2)
                out_slots(g.plus(48), Count(RET_B + 12 - 10, 10, i), 8, tail)

            with v.Fori(1, RET_GROUPS - 1) as i:
                ret_group(i)
            ret_group(RET_GROUPS - 1, ret_slots(Count(RET_HEADS - 2), RET_HEADS - 2, x_hi, x_lo, RET_TAIL_STRIDE))
            last = RET_B + 10 * RET_GROUPS - 4
            out_slots(Count(TOTAL - RET_OUT), Count(last), 8, after=stats_after(last))
            row_norms(W_RET + RET_HEADS)
            v.wait_ge(ln_full, 64)
            for t in range(TOK):
                V.scalar_tensor_tensor(res[:, t, :], res[:, t, :], mv[:, t, 0:1], gbc[:, 0, :],
                                       ALU.subtract, ALU.mult).then_inc(ln_centred, 1)
            v.wait_ge(ln_centred, 2)
            v.wait_ge(got, W_RET + RET_HEADS + 1)
            for k, (t, c) in enumerate(OUT_PARTS[:2]):
                c = slice(c, c + D // 2)
                V.scalar_tensor_tensor(res[:, t, c], res[:, t, c], rstd[:, t:t + 1], gbc[:, 1, c],
                                       ALU.mult, ALU.add).then_inc(out_ready[k], 1)


NAMES = ["x", "w_in", "pool_w", "w_out", "w_up", "w_down", "fox_w_in_2", "fox_b_f_2", "fox_w_out_2",
         "ret_w_in_2", "ret_w_out_2", "ln_gain_2", "ln_bias_2"]


def kernel(**inputs):
    import concourse.bacc as bacc
    from concourse.bass_utils import run_bass_kernel_spmd

    nc = bacc.Bacc("TRN2", target_bir_lowering=False, num_devices=1)
    arrays, args = {}, []
    for name in NAMES:
        arrays[f"in_{name}"] = np.ascontiguousarray(inputs[name])
    arrays["in_vectors"] = np.concatenate([np.asarray(v).reshape(-1, P) for v in (
        inputs["attn_norm_g"], inputs["ffn_norm_g"], inputs["pool_scale"], inputs["q_norm_g"], inputs["k_norm_g"],
        inputs["fox_q_gain_2"], inputs["fox_k_gain_2"], inputs["ln_gain_2"][0], inputs["ln_bias_2"][0])])
    arrays["in_taps"] = np.concatenate([np.asarray(inputs["conv_w"]), np.asarray(inputs["conv_b"])[None]])
    arrays.update({f"const_{k}": a for k, a in constants().items()})
    for name, a in arrays.items():
        args.append(nc.dram_tensor(name, a.shape, mybir.dt.from_np(a.dtype), kind="ExternalInput").ap())
    args.append(nc.dram_tensor("y", (1, S, D), F32, kind="ExternalOutput").ap())
    mixers_kernel(nc, *args)
    r = run_bass_kernel_spmd(nc, [arrays], core_ids=[0])
    return r.results[0]["y"]
```
